# Optimizing a Trainium2 kernel written in Bass

```python
import math
import jax, jax.numpy as jnp
from jax import lax
import numpy as np

D_MODEL = 1024
BATCH = 1
SEQ = 2048
DEPTH = 1

SSD_HEAD_DIM = 64
SSD_HEADS = D_MODEL // SSD_HEAD_DIM
D_SSD = SSD_HEADS * SSD_HEAD_DIM
SSD_GROUPS = 2
SSD_HEADS_PER_GROUP = SSD_HEADS // SSD_GROUPS
D_STATE = 128
SSD_CONV = 4
SSD_CHUNK = 128
CONV_DIM = D_SSD + 2 * SSD_GROUPS * D_STATE
GM_HEAD_DIM = 128
GM_HEADS = D_MODEL // GM_HEAD_DIM
D_GM = GM_HEADS * GM_HEAD_DIM
GM_CHUNK = 128
D_MIX = D_SSD + D_GM
N_IN = D_SSD + CONV_DIM + SSD_HEADS + 2 * D_GM
D_FF = ((8 * D_MODEL // 3 + 255) // 256) * 256
FF_CONV = 3
N_MOD = 6
EPS = 1e-6

kernel_name = "hybrid_ssd_gmlp_convffn_adaln"

def rmsnorm(x, g):
    xf = x.astype(jnp.float32)
    y = xf * lax.rsqrt(jnp.mean(xf * xf, axis=-1, keepdims=True) + EPS)
    return (y * g.astype(jnp.float32)).astype(x.dtype)

def causal_dwconv(x, w, b):
    k, ch = w.shape
    y = lax.conv_general_dilated(x, w[:, None, :].astype(x.dtype), window_strides=(1,), padding=[(k - 1, 0)], dimension_numbers=("NWC", "WIO", "NWC"), feature_group_count=ch)
    return y + b.astype(x.dtype)

def ssd_chunked(xh, dt, a, bm, cm):
    bsz, s = xh.shape[:2]
    nc = s // SSD_CHUNK
    chunk = lambda t: t.reshape((bsz, nc, SSD_CHUNK) + t.shape[2:])
    xc = chunk(xh * dt[..., None])
    bc, cc = chunk(bm), chunk(cm)
    a_cs = jnp.cumsum(jnp.moveaxis(chunk(dt * a), 2, -1), axis=-1)
    causal = jnp.tril(jnp.ones((SSD_CHUNK, SSD_CHUNK), dtype=bool))
    seg = jnp.where(causal, a_cs[..., :, None] - a_cs[..., None, :], -jnp.inf)
    cb = jnp.einsum("bclgn,bcsgn->bcgls", cc, bc)
    att = cb[:, :, :, None] * jnp.exp(seg)
    y_diag = jnp.einsum("bcgrls,bcsgrp->bclgrp", att, xc)
    decay_st = jnp.moveaxis(jnp.exp(a_cs[..., -1:] - a_cs), -1, 2)
    states = jnp.einsum("bclgn,bclgrp->bcgrpn", bc, xc * decay_st[..., None])
    chunk_decay = jnp.exp(a_cs[..., -1])

    def step(h, inp):
        st, dec = inp
        return h * dec[..., None, None] + st, h

    h0 = jnp.zeros_like(states[:, 0])
    _, prev = lax.scan(step, h0, (jnp.moveaxis(states, 1, 0), jnp.moveaxis(chunk_decay, 1, 0)))
    prev = jnp.moveaxis(prev, 0, 1)
    decay_out = jnp.moveaxis(jnp.exp(a_cs), -1, 2)
    y_off = jnp.einsum("bclgn,bcgrpn->bclgrp", cc, prev) * decay_out[..., None]
    return (y_diag + y_off).reshape(xh.shape)

def hybrid_mixer(h, w_in, conv_w, conv_b, dt_bias, a_log, d_skip, ssd_norm_g, v_norm_g, ws, bs, gm_out_g, w_out):
    bsz, s, _ = h.shape
    f32 = jnp.float32
    proj = h @ w_in
    z, xbc, dt_raw, gm = jnp.split(proj, [D_SSD, D_SSD + CONV_DIM, D_SSD + CONV_DIM + SSD_HEADS], axis=-1)
    xbc = jax.nn.silu(causal_dwconv(xbc, conv_w, conv_b))
    xs, bm, cm = jnp.split(xbc, [D_SSD, D_SSD + SSD_GROUPS * D_STATE], axis=-1)
    xs = xs.astype(f32).reshape(bsz, s, SSD_GROUPS, SSD_HEADS_PER_GROUP, SSD_HEAD_DIM)
    bm = bm.astype(f32).reshape(bsz, s, SSD_GROUPS, D_STATE)
    cm = cm.astype(f32).reshape(bsz, s, SSD_GROUPS, D_STATE)
    dt = jax.nn.softplus(dt_raw.astype(f32) + dt_bias.astype(f32)).reshape(bsz, s, SSD_GROUPS, SSD_HEADS_PER_GROUP)
    a = -jnp.exp(a_log.astype(f32)).reshape(SSD_GROUPS, SSD_HEADS_PER_GROUP)
    y = ssd_chunked(xs, dt, a, bm, cm) + d_skip.astype(f32).reshape(SSD_GROUPS, SSD_HEADS_PER_GROUP)[..., None] * xs
    gw = SSD_HEADS_PER_GROUP * SSD_HEAD_DIM
    y = y.reshape(bsz, s, SSD_GROUPS, gw) * jax.nn.silu(z.astype(f32)).reshape(bsz, s, SSD_GROUPS, gw)
    y = rmsnorm(y, ssd_norm_g.reshape(SSD_GROUPS, gw)).reshape(bsz, s, D_SSD).astype(h.dtype)
    u, v = jnp.split(jax.nn.gelu(gm, approximate=False), 2, axis=-1)
    v = rmsnorm(v, v_norm_g).reshape(bsz, s // GM_CHUNK, GM_CHUNK, GM_HEADS, GM_HEAD_DIM)
    ws_c = jnp.where(jnp.tril(jnp.ones((GM_CHUNK, GM_CHUNK), dtype=bool)), ws, jnp.zeros_like(ws))
    sv = jnp.einsum("hts,bcshd->bcthd", ws_c, v) + bs.T[:, :, None]
    g_out = rmsnorm(u * sv.reshape(bsz, s, D_GM), gm_out_g)
    return jnp.concatenate([y, g_out], axis=-1) @ w_out

def conv_gated_ffn(h, w_up, conv_w, conv_b, w_down):
    gate, val = jnp.split(h @ w_up, 2, axis=-1)
    gate = causal_dwconv(gate, conv_w, conv_b)
    return (jax.nn.silu(gate) * val) @ w_down

def setup_inputs(seed: int = 0) -> dict:
    key = jax.random.key(seed)
    ks = jax.random.split(key, 24)
    f32 = jnp.float32
    L = DEPTH
    nrm = lambda k, shape, sc: jax.random.normal(k, shape, f32) * sc
    gain = lambda k, shape: 1.0 + 0.1 * jax.random.normal(k, shape, f32)
    dt0 = jnp.exp(jax.random.uniform(ks[9], (L, SSD_HEADS), f32, math.log(1e-3), math.log(1e-1)))
    return {
        "x": nrm(ks[0], (BATCH, SEQ, D_MODEL), 1.0),
        "c": nrm(ks[1], (BATCH, D_MODEL), 1.0),
        "ada_w": nrm(ks[2], (L, D_MODEL, N_MOD * D_MODEL), 0.5 * D_MODEL ** -0.5),
        "ada_b": nrm(ks[3], (L, N_MOD * D_MODEL), 0.01),
        "norm1_g": gain(ks[4], (L, D_MODEL)),
        "norm2_g": gain(ks[5], (L, D_MODEL)),
        "w_in": nrm(ks[6], (L, D_MODEL, N_IN), D_MODEL ** -0.5),
        "ssd_conv_w": nrm(ks[7], (L, SSD_CONV, CONV_DIM), SSD_CONV ** -0.5),
        "ssd_conv_b": nrm(ks[8], (L, CONV_DIM), 0.01),
        "ssd_dt_bias": dt0 + jnp.log(-jnp.expm1(-dt0)),
        "ssd_a_log": jnp.log(jax.random.uniform(ks[10], (L, SSD_HEADS), f32, 1.0, 16.0)),
        "ssd_d": gain(ks[11], (L, SSD_HEADS)),
        "ssd_norm_g": gain(ks[12], (L, D_SSD)),
        "gm_vnorm_g": gain(ks[13], (L, D_GM)),
        "gm_ws": nrm(ks[14], (L, GM_HEADS, GM_CHUNK, GM_CHUNK), GM_CHUNK ** -0.5),
        "gm_bs": gain(ks[15], (L, GM_HEADS, GM_CHUNK)),
        "gm_out_g": gain(ks[16], (L, D_GM)),
        "w_out": nrm(ks[17], (L, D_MIX, D_MODEL), D_MIX ** -0.5),
        "ff_up": nrm(ks[18], (L, D_MODEL, 2 * D_FF), D_MODEL ** -0.5),
        "ff_conv_w": nrm(ks[19], (L, FF_CONV, D_FF), FF_CONV ** -0.5),
        "ff_conv_b": nrm(ks[20], (L, D_FF), 0.01),
        "ff_down": nrm(ks[21], (L, D_FF, D_MODEL), D_FF ** -0.5),
        "final_g": gain(ks[22], (D_MODEL,)),
    }

def reference(x, c, ada_w, ada_b, norm1_g, norm2_g, w_in, ssd_conv_w, ssd_conv_b, ssd_dt_bias, ssd_a_log, ssd_d, ssd_norm_g, gm_vnorm_g, gm_ws, gm_bs, gm_out_g, w_out, ff_up, ff_conv_w, ff_conv_b, ff_down, final_g):
    c_act = jax.nn.silu(c)
    for l in range(DEPTH):
        mod = (c_act @ ada_w[l] + ada_b[l])[:, None, :]
        sh1, sc1, g1, sh2, sc2, g2 = jnp.split(mod, N_MOD, axis=-1)
        h = rmsnorm(x, norm1_g[l]) * (1 + sc1) + sh1
        x = x + g1 * hybrid_mixer(h, w_in[l], ssd_conv_w[l], ssd_conv_b[l], ssd_dt_bias[l], ssd_a_log[l], ssd_d[l], ssd_norm_g[l], gm_vnorm_g[l], gm_ws[l], gm_bs[l], gm_out_g[l], w_out[l])
        h = rmsnorm(x, norm2_g[l]) * (1 + sc2) + sh2
        x = x + g2 * conv_gated_ffn(h, ff_up[l], ff_conv_w[l], ff_conv_b[l], ff_down[l])
    return rmsnorm(x, final_g)


_drawn_inputs = setup_inputs


def setup_inputs(seed=0):
    import zlib

    import numpy as np

    out = dict(_drawn_inputs(seed))
    spreads = {}
    factors = {'ada_b': 4.204,
     'ssd_conv_b': 8.0,
     'ssd_d': 3.812,
     'ssd_norm_g': 2.809,
     'gm_vnorm_g': 4.716,
     'gm_bs': 3.466,
     'gm_out_g': 2.724,
     'ff_conv_b': 37.749}
    for name, (base, spread) in spreads.items():
        noise = np.random.default_rng([zlib.crc32(name.encode()), seed]).standard_normal(out[name].shape)
        drawn = base * np.exp(spread * noise) if base else spread * noise
        out[name] = __import__('jax').numpy.asarray(drawn.astype(out[name].dtype))
    for name, factor in factors.items():
        out[name] = (out[name] * factor).astype(out[name].dtype)
    return out
```

```python
import concourse.bass as bass
from concourse import mybir
from contextlib import ExitStack


def hybrid_decoder_trunk(nc, x, c, ada_w, ada_b, norm1_g, norm2_g, w_in, ssd_conv_w, ssd_conv_b, ssd_dt_bias,
                         ssd_a_log, ssd_d, ssd_norm_g, gm_vnorm_g, gm_ws, gm_bs, gm_out_g, w_out, ff_up,
                         ff_conv_w, ff_conv_b, ff_down, final_g, out):
    F32, F32R, I32 = mybir.dt.float32, mybir.dt.float32r, mybir.dt.int32
    ALU, ACT = mybir.AluOpType, mybir.ActivationFunctionType

    P, W = 128, 512
    _, SEQ, D = x.shape
    BT = W
    NB, NT = SEQ // BT, BT // P
    KD = D // P
    NH = ssd_d.shape[1]
    HD = D // NH
    CONV = ssd_conv_w.shape[2]
    NST = (CONV - D) // 4
    KX = CONV // P
    GH = gm_ws.shape[1]
    DFF = ff_down.shape[1]
    KF = DFF // P
    EPS = 1e-6
    COL_XBC, COL_DT, COL_U = D, D + CONV, D + CONV + NH
    MODS = ada_b.shape[1]
    assert NT == 4 and NST == P and GH == KD and P == gm_ws.shape[2]

    XBC, UV, Z, OUT, UP, DOWN = 0, 3 * KD, 7 * KD, 9 * KD, 9 * KD + 4 * KD, 13 * KD + (KF // 2) * KD
    UNITS = DOWN + 2 * KF
    G_UV, G_Z, G_OUT, G_UP, G_DOWN = 3, 7, 9, 11, 11 + KF // 2
    GROUPS = G_DOWN + 2
    S_Z, S_OUT, S_UP, S_DOWN = 3, 5, 7, 7 + KF // 2
    STAGED = 4 * (S_DOWN + 2)
    CONVS = KX + KF
    RING, LEAD, SP_LEAD = 4, 3, 4
    assert UNITS % RING == 0 and XBC % RING == UV % RING == Z % RING == OUT % RING == UP % RING == DOWN % RING == 0

    ctx = ExitStack()
    with ctx:
        place = [nc.sbuf_base + 31 & ~31]

        def fixed(name, shape, dt, at=None):
            n = 4
            for s in shape[1:]:
                n *= s
            if at is None:
                at = place[0]
                place[0] += n + 31 & ~31
            return nc.alloc_sbuf_tensor_at(name, shape, dt, offset=at), at

        w_raw, _ = fixed("w_raw", [P, RING, W], F32)
        w_hi, _ = fixed("w_hi", [P, RING, W], F32R)
        w_lo, _ = fixed("w_lo", [P, RING, W], F32R)
        x2, _ = fixed("x2", [P, NT, D], F32)
        h_hi, h_at = fixed("h_hi", [P, KD, BT], F32R)
        h_lo, _ = fixed("h_lo", [P, KD, BT], F32R)
        region, r_at = fixed("region", [P, 24, 1024], F32)
        KB = 1024
        xT, _ = fixed("xT", [P, KD, BT], F32, r_at)
        bcT, _ = fixed("bcT", [P, 4, BT], F32, r_at + 16 * KB)
        arow, _ = fixed("arow", [P, NH, P], F32, r_at + 24 * KB)
        gmT_hi, _ = fixed("gmT_hi", [P, KD, BT], F32R, r_at)
        gmT_lo, _ = fixed("gmT_lo", [P, KD, BT], F32R, r_at + 16 * KB)
        u_sb, _ = fixed("u_sb", [P, 2, NT, W], F32, r_at + 32 * KB)
        xn2, _ = fixed("xn2", [P, NT, D], F32, r_at + 32 * KB)
        v_sb, _ = fixed("v_sb", [P, 2, NT, W], F32, r_at + 48 * KB)
        yT_hi, _ = fixed("yT_hi", [P, KD, BT], F32R, r_at + 48 * KB)
        yT_lo, _ = fixed("yT_lo", [P, KD, BT], F32R, r_at + 64 * KB)
        xs, _ = fixed("xs", [P, D], F32, r_at + 64 * KB)
        xdt, _ = fixed("xdt", [P, D], F32, r_at + 68 * KB)
        xdec, _ = fixed("xdec", [P, D], F32, r_at + 72 * KB)
        sv_tmp, _ = fixed("sv_tmp", [P, 2, D], F32, r_at + 64 * KB)
        vg_bc, _ = fixed("vg_bc", [P, D], F32, r_at + 72 * KB)
        b_tok, _ = fixed("b_tok", [P, 2, P], F32, r_at + 76 * KB)
        cbm, _ = fixed("cbm", [P, 2, P], F32, r_at + 77 * KB)
        dl, _ = fixed("dl", [P, 2, NH], F32, r_at + 78 * KB)
        dex, _ = fixed("dex", [P, 2, NH], F32, r_at + 78 * KB + 512)
        y_sb, _ = fixed("y_sb", [P, NT, D], F32, r_at + 80 * KB)
        g_hi, _ = fixed("g_hi", [P, KF, BT], F32R, r_at)
        g_lo, _ = fixed("g_lo", [P, KF, BT], F32R, r_at + 2 * KF * KB)
        ADA_RING = 8
        ada_t, _ = fixed("ada_t", [P, ADA_RING, MODS // 2], F32, r_at)
        xn01, xn_at = fixed("xn01", [P, 2, D], F32)
        acsT, _ = fixed("acsT", [NH, BT], F32, xn_at)
        daT, _ = fixed("daT", [NH, BT], F32, xn_at + 2 * KB)
        dt_t, _ = fixed("dt_t", [P, NT, NH], F32, xn_at + 4 * KB)
        dt_b, _ = fixed("dt_b", [P, NT, NH], F32, xn_at + 4 * KB + 256)
        da_t, _ = fixed("da_t", [P, NT, NH], F32, xn_at + 4 * KB + 512)
        acs_t, _ = fixed("acs_t", [P, NT, NH], F32, xn_at + 4 * KB + 768)
        eacs_t, _ = fixed("eacs_t", [P, NT, NH], F32, xn_at + 5 * KB)
        dt_e, _ = fixed("dt_e", [P, NT, NH], F32, xn_at + 5 * KB + 256)
        dt_s, _ = fixed("dt_s", [P, NT, NH], F32, xn_at + 5 * KB + 512)
        dt_q, _ = fixed("dt_q", [P, NT, NH], F32, xn_at + 5 * KB + 768)
        dt_p, _ = fixed("dt_p", [P, NT, NH], F32, xn_at + 7 * KB)
        HALO, SW = 3, W + 3
        stage, s_at = fixed("stage", [P, 4, SW], F32)
        xn23, _ = fixed("xn23", [P, 2, D], F32, s_at)
        acc, _ = fixed("acc", [P, 2, W], F32)
        g_bc, _ = fixed("g_bc", [P, D], F32)
        fg_bc, _ = fixed("fg_bc", [P, D], F32)
        state, _ = fixed("state", [P, D], F32)
        wsT, _ = fixed("wsT", [P, GH, P], F32)
        ident, _ = fixed("ident", [P, P], F32)
        tri, _ = fixed("tri", [P, P], F32)
        wdt_hi, _ = fixed("wdt_hi", [P, KD, NH], F32R)
        wdt_lo, _ = fixed("wdt_lo", [P, KD, NH], F32R)
        R_CONVW, R_CONVB = 0, 4 * KX
        R_SN, R_GO, R_N1, R_N2, R_C = 5 * KX, 5 * KX + KD, 5 * KX + 2 * KD, 5 * KX + 3 * KD, 5 * KX + 4 * KD
        ROWS_A = 5 * KX + 5 * KD
        R_FW, R_FB, R_BS = 0, 3 * KF, 4 * KF
        ROWS_B = 4 * KF + GH
        col_a, _ = fixed("col_a", [P, ROWS_A], F32)
        col_b, _ = fixed("col_b", [P, ROWS_B], F32)
        NM = MODS // P
        mod_c, _ = fixed("mod_c", [P, NM], F32)
        halo_x, _ = fixed("halo_x", [P, KX, 3], F32)
        halo_f, _ = fixed("halo_f", [P, KF, 2], F32)
        small, _ = fixed("small", [P, 3, NH], F32)
        stats, _ = fixed("stats", [P, 2, 6], F32)
        mv, _ = fixed("mv", [P, 8, 2], F32)
        ms, _ = fixed("ms", [P, 8], F32)
        rt, _ = fixed("rt", [P, 8], F32)
        rstd, _ = fixed("rstd", [P, 8], F32)
        c_act, _ = fixed("c_act", [P, KD], F32)
        zeros, _ = fixed("zeros", [NH, P], F32, xn_at + 6 * KB)
        assert place[0] <= nc.sbuf_usable_end, (place[0], nc.sbuf_usable_end)
        rows_a, _ = fixed("rows_a", [P, P], F32, xn_at)
        rows_b, _ = fixed("rows_b", [P, P], F32, xn_at + 512)
        rows_m, _ = fixed("rows_m", [P, P], F32, xn_at + KB)
        wdt_raw, _ = fixed("wdt_raw", [P, KD, NH], F32, xn_at + 2 * KB)
        ws_raw, _ = fixed("ws_raw", [P, GH, P], F32, xn_at + 4 * KB)
        mod_row, _ = fixed("mod_row", [1, MODS], F32, h_at)

        def bank(name):
            return ctx.enter_context(nc.psum_tensor(name, [P, W], F32))

        main = [bank(f"main{i}") for i in range(4)]
        pair = [ctx.enter_context(nc.psum_tensor(f"pair{i}", [P, 2, W], F32)) for i in range(2)]
        aux = [pair[i // 2][:, i % 2, :] for i in range(4)]

        mod_d = nc.dram_tensor("mod_scratch", [MODS], F32, kind="Internal").ap()
        acs_d = nc.dram_tensor("acs_scratch", [NB * NT, NH, P], F32, kind="Internal").ap()

        def sem(name):
            return ctx.enter_context(nc.semaphore(name))

        w_in_dma = [sem(f"w_loaded{i}") for i in range(RING)]
        w_hi_ok = sem("w_hi_ok")
        w_lo_ok = sem("w_lo_ok")
        w_used = sem("w_used")
        bank_done = sem("bank_done")
        evacuated = sem("evacuated")
        stage_used = sem("stage_used")
        conv_done = sem("conv_done")
        silu_done = sem("silu_done")
        x_in = sem("x_in")
        xn_ok = sem("xn_ok")
        h_tr = sem("h_tr")
        h_hi_ok, h_lo_ok = sem("h_hi_ok"), sem("h_lo_ok")
        x2_in = sem("x2_in")
        g2_in = sem("g2_in")
        vg_in = sem("vg_in")
        dt_mm, dt_biased, dt_soft = sem("dt_mm"), sem("dt_biased"), sem("dt_soft")
        da_ok, da_tr, acs_ok, acs_tr = sem("da_ok"), sem("da_tr"), sem("acs_ok"), sem("acs_tr")
        acs_t_ok, eacs_ok, acs_stored = sem("acs_t_ok"), sem("eacs_ok"), sem("acs_stored")
        arow_in = sem("arow_in")
        t_done = sem("t_done")
        xs_ok = sem("xs_ok")
        cbm_ok = sem("cbm_ok")
        dl_ok, seg_ok, dex_ok, exp_ok = sem("dl_ok"), sem("seg_ok"), sem("dex_ok"), sem("exp_ok")
        xdec_ok, att_ok = sem("xdec_ok"), sem("att_ok")
        yoff_done, yoff_used = sem("yoff_done"), sem("yoff_used")
        s_done, state_ok = sem("s_done"), sem("state_ok")
        yd_done, yd_used = sem("yd_done"), sem("yd_used")
        v_ok, sv_done, sv_used, gm_ok = sem("v_ok"), sem("sv_done"), sem("sv_used"), sem("gm_ok")
        gm_tr, gm_hi_ok, gm_lo_ok = sem("gm_tr"), sem("gm_hi_ok"), sem("gm_lo_ok")
        y_ok, y_tr, y_hi_ok, y_lo_ok = sem("y_ok"), sem("y_tr"), sem("y_hi_ok"), sem("y_lo_ok")
        out_ok, out_stored = sem("out_ok"), sem("out_stored")
        const_ok, rows_in, small_in, pro_dma = sem("const_ok"), sem("rows_in"), sem("small_in"), sem("pro_dma")
        ada_in = [sem(f"ada_in{i}") for i in range(ADA_RING)]
        ada_used, ada_done, mod_ok, mod_stored, mrow_in = (sem(n) for n in (
            "ada_used", "ada_done", "mod_ok", "mod_stored", "mrow_in"))
        col_tr, col_ok, cact_ok, ws_tr, ws_ok, mrow_tr, mod_c_ok = (sem(n) for n in (
            "col_tr", "col_ok", "cact_ok", "ws_tr", "ws_ok", "mrow_tr", "mod_c_ok"))
        wdt_h, wdt_l, a_exp = sem("wdt_h"), sem("wdt_l"), sem("a_exp")
        ready = sem("ready")
        pe_past = sem("pe_past")
        dve_step = sem("dve_step")

        def slot_full(b, n):
            return b * (16 * UNITS // RING) + 16 * (n // RING + 1)

        block = ctx.enter_context(nc.Block())

        @block.sync
        def _(sp):
            cw = ssd_conv_w[0].rearrange("k (j p) -> (k j) p", p=P)
            fw = ff_conv_w[0].rearrange("k (j p) -> (k j) p", p=P)
            for r, n, src in ((R_CONVW, 4 * KX, cw), (R_CONVB, KX, ssd_conv_b[0].rearrange("(j p) -> j p", p=P)),
                              (R_SN, KD, ssd_norm_g[0].rearrange("(j p) -> j p", p=P)),
                              (R_GO, KD, gm_out_g[0].rearrange("(j p) -> j p", p=P)),
                              (R_N1, KD, norm1_g[0].rearrange("(j p) -> j p", p=P)),
                              (R_N2, KD, norm2_g[0].rearrange("(j p) -> j p", p=P)),
                              (R_C, KD, c[0].rearrange("(j p) -> j p", p=P))):
                sp.dma_start(rows_a[r:r + n, :], src).then_inc(rows_in, 16)
            sp.dma_start(mod_row[0:1, :], ada_b).then_inc(pro_dma, 16)
            for r, n, src in ((R_FW, 3 * KF, fw), (R_FB, KF, ff_conv_b[0].rearrange("(j p) -> j p", p=P)),
                              (R_BS, GH, gm_bs[0])):
                sp.dma_start(rows_b[r:r + n, :], src).then_inc(rows_in, 16)
            for i in range(2 * KD):
                half, k = i // KD, i % KD
                if i >= ADA_RING:
                    sp.wait_ge(ada_used, i - ADA_RING + 1)
                sp.dma_start(ada_t[:, i % ADA_RING, :], ada_w[0, k * P:(k + 1) * P,
                                                              half * (MODS // 2):(half + 1) * (MODS // 2)]
                             ).then_inc(ada_in[i % ADA_RING], 16)
                if i == 0:
                    for s, src in enumerate((ssd_a_log, ssd_d, ssd_dt_bias)):
                        sp.dma_start(small[:, s, :], src.broadcast_to([P, NH])).then_inc(small_in, 16)
                    sp.dma_start(ws_raw[:], gm_ws[0].rearrange("h t s -> t h s")).then_inc(small_in, 16)
                    sp.dma_start(wdt_raw[:], w_in[0, :, COL_DT:COL_U].rearrange("(k p) n -> p k n", p=P)
                                 ).then_inc(small_in, 16)
                    sp.dma_start(fg_bc[:], final_g.unsqueeze(0).broadcast_to([P, D])).then_inc(small_in, 16)
            sp.wait_ge(mod_ok, 12)
            sp.dma_start(mod_d.unsqueeze(0), mod_row[0:1, :]).then_inc(mod_stored, 16)
            sp.wait_ge(mod_stored, 16)
            sp.dma_start(rows_m[0:NM, :], mod_d.rearrange("(j p) -> j p", p=P)).then_inc(mrow_in, 16)
            sp.wait_ge(mod_c_ok, 1)
            sp.wait_ge(ready, 1)
            xv = x[0].rearrange("(b t p) d -> b t p d", t=NT, p=P)

            def load_x(b):
                for t in range(NT):
                    dst = xn01[:, t, :] if t < 2 else xn23[:, t - 2, :]
                    sp.dma_start(dst, xv[bass.ds(b, 1), t, :, :].squeeze(0)).then_inc(x_in, 16)

            load_x(0)
            sp.sem_inc(out_stored, 64)

            def rows(w, k):
                return w[0, k * P:(k + 1) * P, :]

            def load(b, n, src, dst_view=None):
                sp.wait_ge(w_lo_ok, b * UNITS + (n + 1))
                dst = w_raw[:, n % RING, :]
                sp.dma_start(dst if dst_view is None else dst_view(dst), src).then_inc(w_in_dma[n % RING], 16)

            def xbc_unit(b, n):
                j, k = n // KD, n % KD
                load(b, n, rows(w_in, k)[:, COL_XBC + j * W:COL_XBC + (j + 1) * W])

            for n in range(SP_LEAD):
                xbc_unit(0, n)
            with sp.Fori(0, NB) as b:
                for n in range(SP_LEAD, 3 * KD):
                    xbc_unit(b, n)
                    if n == 12:
                        sp.wait_ge(out_stored, b * 64 + 64)
                        sp.dma_start(x2[:], x[0].rearrange("(b t p) d -> b p t d", t=NT, p=P)[bass.ds(b, 1)]
                                     .squeeze(0)).then_inc(x2_in, 16)
                        sp.dma_start(g_bc[:], mod_d[2 * D:3 * D].unsqueeze(0).broadcast_to([P, D])
                                     ).then_inc(x2_in, 16)
                for cc in range(NT):
                    for k in range(KD):
                        n = UV + cc * KD + k
                        load(b, n, rows(w_in, k)[:, COL_U + cc * W:COL_U + (cc + 1) * W])
                        if k == 5:
                            if cc == 0:
                                sp.wait_ge(acs_stored, b * 16 + 16)
                            else:
                                sp.wait_ge(yd_done, b * NT + cc)
                            sp.dma_start(arow[:], acs_d[bass.ds(b * NT + cc, 1)].rearrange("o h l -> o (h l)")
                                         .broadcast_to([P, NH * P])).then_inc(arow_in, 16)
                for j in range(2):
                    for k in range(KD):
                        load(b, Z + j * KD + k, rows(w_in, k)[:, j * W:(j + 1) * W])
                        if j == 0 and k == 3:
                            sp.wait_ge(s_done, b * NT + NT)
                            sp.dma_start(vg_bc[:], gm_vnorm_g.broadcast_to([P, D])).then_inc(vg_in, 16)
                for j in range(2):
                    for k in range(2 * KD):
                        kk = (k + KD) % (2 * KD)
                        load(b, OUT + j * 2 * KD + k, rows(w_out, kk)[:, j * W:(j + 1) * W])
                with sp.Fori(0, KF // 2) as j:
                    for k in range(KD):
                        n = UP + k
                        sp.wait_ge(w_lo_ok, b * UNITS + j * KD + (n + 1))
                        src = rows(ff_up, k).rearrange("p (g n) -> p g n", g=2)[:, :, bass.ds(j * (2 * P), 2 * P)]
                        sp.dma_start(w_raw[:, n % RING, :].rearrange("p (g n) -> p g n", g=2), src
                                     ).then_inc(w_in_dma[n % RING], 16)
                nxt = (b + 1) % NB
                for j in range(2):
                    for k in range(KF):
                        load(b, DOWN + j * KF + k, rows(ff_down, k)[:, j * W:(j + 1) * W])
                        if j == 0 and k == 7:
                            sp.wait_ge(stage_used, b * STAGED + (4 * S_DOWN + 4))
                            sp.dma_start(g_bc[:], mod_d[5 * D:6 * D].unsqueeze(0).broadcast_to([P, D])
                                         ).then_inc(g2_in, 16)
                            load_x(nxt)
                for n in range(SP_LEAD):
                    sp.wait_ge(w_lo_ok, b * UNITS + (UNITS + n + 1))
                    sp.dma_start(w_raw[:, n, :], rows(w_in, n)[:, COL_XBC:COL_XBC + W]).then_inc(w_in_dma[n], 16)
                for t in range(NT):
                    sp.wait_ge(out_ok, b * NT + (t + 1))
                    sp.dma_start(out[0].rearrange("(b t p) d -> b t p d", t=NT, p=P)[bass.ds(b, 1), t, :, :].squeeze(0),
                                 x2[:, t, :]).then_inc(out_stored, 16)
            sp.wait_ge(out_stored, 64 * (NB + 1))

        @block.gpsimd
        def _(pool):
            nc.gpsimd.memset(ident[:], 0.0).then_inc(const_ok, 1)
            nc.gpsimd.memset(tri[:], 1.0).then_inc(const_ok, 1)
            pool.wait_ge(const_ok, 2)
            nc.gpsimd.affine_select(out=ident[:], in_=ident[:], compare_op=ALU.not_equal, fill=1.0, base=0,
                                    pattern=[[-1, P]], channel_multiplier=1).then_inc(const_ok, 1)
            nc.gpsimd.affine_select(out=tri[:], in_=tri[:], compare_op=ALU.is_ge, fill=0.0, base=0,
                                    pattern=[[1, P]], channel_multiplier=-1).then_inc(const_ok, 1)
            pool.sem_inc(w_lo_ok, RING)
            with pool.Fori(0, NB * UNITS // RING) as q:
                for s in range(RING):
                    pool.wait_ge(w_hi_ok, q * RING + (s + 1))
                    pool.wait_ge(w_used, q * RING + (s + 1))
                    nc.gpsimd.tensor_tensor(w_lo[:, s, :], w_raw[:, s, :], w_hi[:, s, :].bitcast(F32),
                                            ALU.subtract).then_inc(w_lo_ok, 1)

        @block.scalar
        def _(act):
            act.wait_ge(small_in, 96)
            nc.scalar.activation(small[:, 0, :], small[:, 0, :], ACT.Exp).then_inc(a_exp, 1)
            nc.scalar.activation(wdt_hi[:], wdt_raw[:], ACT.Copy).then_inc(wdt_h, 1)
            act.wait_ge(col_ok, 2)
            nc.scalar.activation(c_act[:], col_a[:, R_C:R_C + KD], ACT.Silu).then_inc(cact_ok, 1)
            act.sem_inc(evacuated, 4)
            act.sem_inc(silu_done, 2)

            def split(b, n):
                act.wait_ge(w_in_dma[n % RING], slot_full(b, n))
                act.wait_ge(w_used, b * UNITS + (n + 1))
                nc.scalar.activation(w_hi[:, n % RING, :], w_raw[:, n % RING, :], ACT.Copy).then_inc(w_hi_ok, 1)

            def bank_ready(b, G, last, i):
                if i < 3:
                    act.wait_ge(bank_done, b * (3 * GROUPS) + (3 * G + i + 1))
                else:
                    act.wait_ge(w_used, b * UNITS + (last + 1 + RING))

            def evac_to_stage(b, G, S, last, func):
                for i in range(4):
                    bank_ready(b, G, last, i)
                    act.wait_ge(stage_used, b * STAGED + (4 * S + i + 1))
                    nc.scalar.activation(stage[:, i, HALO:], main[i][:], func).then_inc(evacuated, 1)

            def silu_tile(b, cv, src, dst):
                act.wait_ge(conv_done, b * CONVS + (cv + 1))
                nc.scalar.activation(dst, src, ACT.Silu).then_inc(silu_done, 1)

            def h_tiles(q, ks, col_scale, col_bias):
                for k in ks:
                    act.wait_ge(h_tr, q * KD + (k + 1))
                    nc.scalar.activation(h_hi[:, k, :], aux[k % 4], ACT.Identity, bias=mod_c[:, col_bias + k:col_bias + k + 1],
                                         scale=mod_c[:, col_scale + k:col_scale + k + 1]).then_inc(h_hi_ok, 1)

            act.wait_ge(ready, 1)
            h_tiles(0, range(KD), KD, 0)
            for n in range(LEAD):
                split(0, n)
            with act.Fori(0, NB) as b:
                at = LEAD
                for j in range(3):
                    for n in range(at, (j + 1) * KD + LEAD):
                        split(b, n)
                        if j == 0 and n == 5:
                            act.wait_ge(dt_biased, b + 1)
                            nc.scalar.activation(dt_e[:], dt_e[:], ACT.Exp, scale=-1.0).then_inc(dt_soft, 1)
                        if j == 1 and n == KD + 6:
                            act.wait_ge(acs_ok, b + 1)
                            act.dma_start(acs_d[bass.ds(b * NT, NT)].rearrange("c h l -> h c l"),
                                          acsT[:].rearrange("h (c l) -> h c l", l=P)).then_inc(acs_stored, 16)
                            act.wait_ge(acs_t_ok, b + 1)
                            nc.scalar.activation(eacs_t[:], acs_t[:], ACT.Exp).then_inc(eacs_ok, 1)
                    evac_to_stage(b, j, j, (j + 1) * KD - 1, ACT.Copy)
                    for i in range(4):
                        kx = 4 * j + i
                        silu_tile(b, kx, acc[:, kx % 2, :], xT[:, kx, :] if kx < KD else bcT[:, kx - KD, :])
                        if i in (1, 2):
                            split(b, (j + 1) * KD + LEAD + i - 1)
                    at = (j + 1) * KD + LEAD + 2
                for cc in range(NT):
                    n0, n1 = UV + cc * KD, UV + (cc + 1) * KD
                    at = max(at, n0 + LEAD)
                    for n in range(at, n1 + LEAD):
                        split(b, n)
                        if n == n0 + 7:
                            act.wait_ge(t_done, b * NT + (cc + 1))
                            for h in range(2):
                                nc.scalar.activation(xs[:, h * W:(h + 1) * W], aux[h], ACT.Copy).then_inc(xs_ok, 1)
                            nc.scalar.activation(b_tok[:], aux[2][:, 0:2 * P].rearrange("p (g n) -> p g n", g=2),
                                                 ACT.Copy).then_inc(xs_ok, 1)
                        if n == n0 + 8:
                            act.wait_ge(dl_ok, b * NT + (cc + 1))
                            nc.scalar.activation(dex[:], dl[:], ACT.Exp).then_inc(dex_ok, 1)
                            act.wait_ge(seg_ok, b * NT + (cc + 1))
                            nc.scalar.activation(arow[:], arow[:], ACT.Exp).then_inc(exp_ok, 1)
                    for i in range(4):
                        bank_ready(b, G_UV + cc, n1 - 1, i)
                        dst = (u_sb if cc < 2 else v_sb)[:, cc % 2, i, :]
                        nc.scalar.activation(dst, main[i][:], ACT.Gelu).then_inc(evacuated, 1)
                for j in range(2):
                    for n in range(Z + j * KD + LEAD, Z + (j + 1) * KD + LEAD):
                        split(b, n)
                        if j == 1 and n == OUT + LEAD - 1:
                            for k in range(KD):
                                act.wait_ge(gm_tr, b * KD + (k + 1))
                                nc.scalar.activation(gmT_hi[:, k, :], aux[k % 4], ACT.Copy,
                                                     scale=col_a[:, R_GO + k:R_GO + k + 1]).then_inc(gm_hi_ok, 1)
                    evac_to_stage(b, G_Z + j, S_Z + j, Z + (j + 1) * KD - 1, ACT.Silu)
                for j in range(2):
                    n0 = OUT + 2 * j * KD
                    for n in range(n0 + LEAD, n0 + 2 * KD + LEAD):
                        split(b, n)
                        if j == 0 and n in (n0 + LEAD + 6, n0 + LEAD + 7):
                            for k in range(4) if n == n0 + LEAD + 6 else range(4, KD):
                                act.wait_ge(y_tr, b * KD + (k + 1))
                                nc.scalar.activation(yT_hi[:, k, :], aux[k % 4], ACT.Copy,
                                                     scale=col_a[:, R_SN + k:R_SN + k + 1]).then_inc(y_hi_ok, 1)
                    evac_to_stage(b, G_OUT + j, S_OUT + j, n0 + 2 * KD - 1, ACT.Copy)
                h_tiles(b * 2 + 1, range(KD), 4 * KD, 3 * KD)
                with act.Fori(0, KF // 2) as j:
                    for m in range(KD):
                        n = UP + LEAD + m
                        act.wait_ge(w_in_dma[n % RING], b * (16 * UNITS // RING) + j * (16 * KD // RING) + 16 * (n // RING + 1))
                        act.wait_ge(w_used, b * UNITS + j * KD + (n + 1))
                        nc.scalar.activation(w_hi[:, n % RING, :], w_raw[:, n % RING, :], ACT.Copy).then_inc(w_hi_ok, 1)
                    for i in range(4):
                        if i < 3:
                            act.wait_ge(bank_done, b * (3 * GROUPS) + j * 3 + (3 * G_UP + i + 1))
                        else:
                            act.wait_ge(w_used, b * UNITS + j * KD + (UP + KD + RING))
                        act.wait_ge(stage_used, b * STAGED + j * 4 + (4 * S_UP + i + 1))
                        nc.scalar.activation(stage[:, i, HALO:], main[i][:], ACT.Copy).then_inc(evacuated, 1)
                    for i in range(2):
                        act.wait_ge(conv_done, b * CONVS + j * 2 + (KX + i + 1))
                        nc.scalar.activation(acc[:, i, :], acc[:, i, :], ACT.Silu).then_inc(silu_done, 1)
                for j in range(2):
                    n0 = DOWN + j * KF
                    for n in range(n0 + LEAD, n0 + KF + LEAD):
                        split(b, n)
                        if j == 0 and n == n0 + 13 + LEAD:
                            h_tiles(b * 2 + 2, range(4), KD, 0)
                        if j == 0 and n == n0 + 16 + LEAD:
                            h_tiles(b * 2 + 2, range(4, KD), KD, 0)
                    evac_to_stage(b, G_DOWN + j, S_DOWN + j, n0 + KF - 1, ACT.Copy)

        @block.vector
        def _(dve):
            steps = [0]

            def link(ins):
                steps[0] += 1
                ins.then_inc(dve_step, 1)
                dve.wait_ge(dve_step, steps[0])

            def fresh():
                dve.sem_clear(dve_step)
                steps[0] = 0

            V = nc.vector

            def rms_stats(i, parts):
                for s, part in enumerate(parts):
                    last = V.bn_stats(stats[:, s, :], part)
                link(last)
                link(V.bn_aggr(mv[:, i, :], stats[:, 0:len(parts), :]))

            def rms_rstd(n):
                link(V.tensor_copy(rt[:, 0:n], mv[:, 0:n, 0]))
                link(V.tensor_tensor(ms[:, 0:n], rt[:, 0:n], rt[:, 0:n], ALU.mult))
                link(V.scalar_tensor_tensor(out=ms[:, 0:n], in0=ms[:, 0:n], scalar=EPS, in1=mv[:, 0:n, 1],
                                            op0=ALU.add, op1=ALU.add))
                link(V.tensor_scalar(rt[:, 0:n].bitcast(I32), ms[:, 0:n].bitcast(I32), 1, None,
                                     ALU.arith_shift_right))
                link(V.tensor_scalar(rstd[:, 0:n].bitcast(I32), rt[:, 0:n].bitcast(I32), -1.0, float(0x5F3759DF),
                                     ALU.mult, ALU.add))
                for _ in range(3):
                    link(V.tensor_tensor(rt[:, 0:n], rstd[:, 0:n], rstd[:, 0:n], ALU.mult))
                    link(V.scalar_tensor_tensor(out=rt[:, 0:n], in0=rt[:, 0:n], scalar=-0.5, in1=ms[:, 0:n],
                                                op0=ALU.mult, op1=ALU.mult))
                    link(V.scalar_tensor_tensor(out=rstd[:, 0:n], in0=rt[:, 0:n], scalar=1.5, in1=rstd[:, 0:n],
                                                op0=ALU.add, op1=ALU.mult))

            def h_lows(q, ks, col_scale, col_bias):
                for k in ks:
                    dve.wait_ge(h_hi_ok, q * KD + (k + 1))
                    link(V.tensor_scalar(acc[:, k % 2, :], aux[k % 4], mod_c[:, col_scale + k:col_scale + k + 1],
                                         mod_c[:, col_bias + k:col_bias + k + 1], ALU.mult, ALU.add))
                    V.tensor_tensor(h_lo[:, k, :], acc[:, k % 2, :], h_hi[:, k, :].bitcast(F32),
                                    ALU.subtract).then_inc(h_lo_ok, 1)

            def norm_x(p):
                tiles = [xn01[:, 0, :], xn01[:, 1, :], xn23[:, 0, :], xn23[:, 1, :]]
                dve.wait_ge(x_in, p * (16 * NT) + 16 * NT)
                for t in range(NT):
                    rms_stats(t, [tiles[t][:, 0:W], tiles[t][:, W:D]])
                rms_rstd(NT)
                for t in range(NT):
                    V.tensor_scalar(tiles[t], tiles[t], rstd[:, t:t + 1], None, ALU.mult).then_inc(xn_ok, 1)

            V.memset(state[:], 0.0)
            V.memset(halo_x[:], 0.0)
            V.memset(halo_f[:], 0.0)
            link(V.memset(rt[:], 0.0))
            dve.wait_ge(col_tr, 2)
            V.tensor_copy(col_a[:], aux[0][:, 0:ROWS_A]).then_inc(col_ok, 1)
            V.tensor_copy(col_b[:], aux[0][:, P:P + ROWS_B]).then_inc(col_ok, 1)
            for g in range(2):
                dve.wait_ge(ws_tr, g + 1)
                V.tensor_tensor(wsT[:, 4 * g:4 * g + 4, :], aux[2 + g].rearrange("p (h n) -> p h n", h=4),
                                tri[:].unsqueeze(1).broadcast_to([P, 4, P]), ALU.mult).then_inc(ws_ok, 1)
            dve.wait_ge(wdt_h, 1)
            link(V.tensor_tensor(wdt_lo[:], wdt_raw[:], wdt_hi[:].bitcast(F32), ALU.subtract))
            dve.wait_ge(a_exp, 1)
            link(V.tensor_scalar(small[:, 0, :], small[:, 0, :], -1.0, None, ALU.mult))
            dve.wait_ge(pro_dma, 16)
            for half in range(2):
                for m in range(6):
                    if m == 0:
                        dve.wait_ge(ada_done, half + 1)
                    src = (main + aux)[m][0:1, :]
                    dst = mod_row[0:1, (6 * half + m) * W:(6 * half + m + 1) * W]
                    V.tensor_tensor(dst, src, dst, ALU.add).then_inc(mod_ok, 1)
            dve.wait_ge(mrow_tr, 1)
            link(V.tensor_copy(mod_c[:], aux[0][:, 0:NM]))
            V.scalar_tensor_tensor(out=mod_c[:, KD:2 * KD], in0=mod_c[:, KD:2 * KD], scalar=1.0,
                                   in1=col_a[:, R_N1:R_N1 + KD], op0=ALU.add, op1=ALU.mult)
            V.scalar_tensor_tensor(out=mod_c[:, 4 * KD:5 * KD], in0=mod_c[:, 4 * KD:5 * KD], scalar=1.0,
                                   in1=col_a[:, R_N2:R_N2 + KD], op0=ALU.add, op1=ALU.mult).then_inc(mod_c_ok, 1)
            dve.wait_ge(mod_c_ok, 1)
            V.tensor_copy(rt[:, 0:1], rt[:, 0:1]).then_inc(ready, 1)
            dve.wait_ge(ready, 1)
            norm_x(0)
            h_lows(0, range(KD), KD, 0)
            dve.sem_inc(stage_used, 4)

            with dve.Fori(0, NB) as b:
                fresh()
                dve.wait_ge(dt_mm, b + 1)
                link(V.tensor_tensor(dt_b[:], aux[3][:, 0:NT * NH].rearrange("p (t h) -> p t h", h=NH),
                                     small[:, 2, :].unsqueeze(1).broadcast_to([P, NT, NH]), ALU.add))
                V.scalar_tensor_tensor(out=dt_e[:], in0=dt_b[:], scalar=-1.0, in1=dt_b[:], op0=ALU.mult, op1=ALU.max
                                       ).then_inc(dt_biased, 1)
                dve.wait_ge(dt_soft, b + 1)
                link(V.tensor_scalar(dt_s[:], dt_e[:], 2.0, None, ALU.add))
                link(V.reciprocal(dt_s[:], dt_s[:]))
                link(V.tensor_tensor(dt_s[:], dt_s[:], dt_e[:], ALU.mult))
                link(V.tensor_tensor(dt_q[:], dt_s[:], dt_s[:], ALU.mult))
                link(V.tensor_scalar(dt_p[:], dt_q[:], 1.0 / 19.0, None, ALU.mult))
                for n in range(17, 1, -2):
                    link(V.scalar_tensor_tensor(out=dt_p[:], in0=dt_p[:], scalar=1.0 / n, in1=dt_q[:],
                                                op0=ALU.add, op1=ALU.mult))
                link(V.scalar_tensor_tensor(out=dt_p[:], in0=dt_p[:], scalar=1.0, in1=dt_s[:],
                                            op0=ALU.add, op1=ALU.mult))
                link(V.tensor_scalar(dt_b[:], dt_b[:], 0.0, None, ALU.max))
                link(V.scalar_tensor_tensor(out=dt_t[:], in0=dt_p[:], scalar=2.0, in1=dt_b[:],
                                            op0=ALU.mult, op1=ALU.add))
                V.tensor_tensor(da_t[:], dt_t[:], small[:, 0, :].unsqueeze(1).broadcast_to([P, NT, NH]),
                                ALU.mult).then_inc(da_ok, 1)
                dve.wait_ge(da_tr, b + 1)
                V.memset(zeros[:], 0.0)
                link(V.tensor_copy(daT[:], aux[3][0:NH, :]))
                for t in range(NT):
                    s = slice(t * P, (t + 1) * P)
                    last = V.tensor_tensor_scan(acsT[:, s], daT[:, s], zeros[:], 0.0,
                                                ALU.add, ALU.add)
                last.then_inc(acs_ok, 1)

                def conv(cv, i, taps, halo, wcol, bcol, a):
                    K = taps
                    link(V.tensor_copy(stage[:, i, HALO - (K - 1):HALO], halo))
                    dve.wait_ge(silu_done, cv)
                    link(V.tensor_scalar(acc[:, a, :], stage[:, i, HALO:], wcol(K - 1), bcol, ALU.mult, ALU.add))
                    for tap in range(K - 1):
                        lo = HALO - (K - 1) + tap
                        ins = V.scalar_tensor_tensor(out=acc[:, a, :], in0=stage[:, i, lo:lo + W], scalar=wcol(tap),
                                                     in1=acc[:, a, :], op0=ALU.mult, op1=ALU.add)
                        if tap < K - 2:
                            link(ins)
                        else:
                            ins.then_inc(conv_done, 1)

                def full(G, i):
                    dve.wait_ge(evacuated, b * (4 * GROUPS) + (4 * G + i + 5))

                for j in range(3):
                    for i in range(4):
                        kx = 4 * j + i
                        full(j, i)
                        conv(b * CONVS + (kx + 1), i, 4, halo_x[:, kx, :],
                             lambda tap: col_a[:, R_CONVW + tap * KX + kx:R_CONVW + tap * KX + kx + 1],
                             col_a[:, R_CONVB + kx:R_CONVB + kx + 1], kx % 2)
                        V.tensor_copy(halo_x[:, kx, :], stage[:, i, W:]).then_inc(stage_used, 1)
                    if j == 0:
                        dve.wait_ge(acs_tr, b + 1)
                        V.tensor_copy(acs_t[:], aux[3][:, 0:NT * NH].rearrange("p (t h) -> p t h", h=NH)
                                      ).then_inc(acs_t_ok, 1)

                def heads(ap):
                    return ap.rearrange("p (h d) -> p h d", h=NH)

                for cc in range(NT):
                    dve.wait_ge(arow_in, b * (16 * NT) + 16 * (cc + 1))
                    if cc == 0:
                        dve.wait_ge(acs_t_ok, b + 1)
                    V.tensor_tensor(dl[:, 0, :], arow[:, :, P - 1], acs_t[:, cc, :], ALU.subtract)
                    V.tensor_copy(dl[:, 1, :], arow[:, :, P - 1]).then_inc(dl_ok, 1)
                    dve.wait_ge(dl_ok, b * NT + (cc + 1))
                    for h in range(NH):
                        last = V.tensor_scalar(arow[:, h, :], arow[:, h, :], acs_t[:, cc, h:h + 1], 0.0,
                                               ALU.subtract, ALU.min)
                    last.then_inc(seg_ok, 1)
                    dve.wait_ge(xs_ok, b * (3 * NT) + 3 * (cc + 1))
                    V.tensor_tensor(cbm[:], aux[2][:, 2 * P:4 * P].rearrange("p (g n) -> p g n", g=2),
                                    tri[:].unsqueeze(1).broadcast_to([P, 2, P]), ALU.mult).then_inc(cbm_ok, 1)
                    link(V.tensor_tensor(heads(xdt[:]), heads(xs[:]), dt_t[:, cc, :].unsqueeze(2)
                                         .broadcast_to([P, NH, HD]), ALU.mult))
                    dve.wait_ge(dex_ok, b * NT + (cc + 1))
                    V.tensor_tensor(heads(xdec[:]), heads(xdt[:]), dex[:, 0, :].unsqueeze(2)
                                    .broadcast_to([P, NH, HD]), ALU.mult).then_inc(xdec_ok, 1)
                    dve.wait_ge(yoff_done, b * NT + (cc + 1))
                    if cc == 0:
                        dve.wait_ge(eacs_ok, b + 1)
                    V.tensor_tensor(heads(y_sb[:, cc, :]), pair[1][:].rearrange("p g (h d) -> p (g h) d", d=HD),
                                    eacs_t[:, cc, :].unsqueeze(2).broadcast_to([P, NH, HD]), ALU.mult
                                    ).then_inc(yoff_used, 1)
                    dve.wait_ge(exp_ok, b * NT + (cc + 1))
                    dve.wait_ge(cbm_ok, b * NT + (cc + 1))
                    for g in range(2):
                        hs = slice(g * NH // 2, (g + 1) * NH // 2)
                        last = V.tensor_tensor(arow[:, hs, :], arow[:, hs, :], cbm[:, g, :].unsqueeze(1)
                                               .broadcast_to([P, NH // 2, P]), ALU.mult)
                    last.then_inc(att_ok, 1)
                    link(V.tensor_tensor(heads(xs[:]), heads(xs[:]), small[:, 1, :].unsqueeze(2)
                                         .broadcast_to([P, NH, HD]), ALU.mult))
                    dve.wait_ge(yoff_used, b * NT + (cc + 1))
                    link(V.tensor_tensor(y_sb[:, cc, :], y_sb[:, cc, :], xs[:], ALU.add))
                    dve.wait_ge(s_done, b * NT + (cc + 1))
                    link(V.tensor_tensor(heads(state[:]), heads(state[:]), dex[:, 1, :].unsqueeze(2)
                                         .broadcast_to([P, NH, HD]), ALU.mult))
                    V.tensor_tensor(state[:], state[:], pair[0][:].rearrange("p g n -> p (g n)"), ALU.add
                                    ).then_inc(state_ok, 1)
                    dve.wait_ge(yd_done, b * NT + (cc + 1))
                    V.tensor_tensor(y_sb[:, cc, :], y_sb[:, cc, :], pair[1][:].rearrange("p g n -> p (g n)"),
                                    ALU.add).then_inc(yd_used, 1)

                full(G_UV + 3, 3)
                for t in range(NT):
                    rms_stats(t, [v_sb[:, 0, t, :], v_sb[:, 1, t, :]])
                rms_rstd(NT)
                for t in range(NT):
                    V.tensor_scalar(v_sb[:, :, t, :], v_sb[:, :, t, :], rstd[:, t:t + 1], None, ALU.mult
                                    ).then_inc(v_ok, 1)
                dve.wait_ge(vg_in, b * 16 + 16)
                for t in range(NT):
                    dve.wait_ge(sv_done, b * NT + (t + 1))
                    V.tensor_tensor(sv_tmp[:, t % 2, :], pair[t % 2][:].rearrange("p g n -> p (g n)"), vg_bc[:],
                                    ALU.mult).then_inc(sv_used, 1)
                    dve.wait_ge(sv_used, b * NT + (t + 1))
                    for h in range(GH):
                        uu = u_sb[:, h // 4, t, (h % 4) * P:(h % 4 + 1) * P]
                        last = V.scalar_tensor_tensor(out=uu, in0=sv_tmp[:, t % 2, h * P:(h + 1) * P],
                                                      scalar=col_b[:, R_BS + h:R_BS + h + 1], in1=uu,
                                                      op0=ALU.add, op1=ALU.mult)
                    link(last)
                    rms_stats(t, [u_sb[:, 0, t, :], u_sb[:, 1, t, :]])
                rms_rstd(NT)
                for t in range(NT):
                    V.tensor_scalar(u_sb[:, :, t, :], u_sb[:, :, t, :], rstd[:, t:t + 1], None, ALU.mult
                                    ).then_inc(gm_ok, 1)

                def gate_y(j):
                    for t in range(NT):
                        full(G_Z + j, t)
                        yy = y_sb[:, t, j * W:(j + 1) * W]
                        V.tensor_tensor(yy, yy, stage[:, t, HALO:], ALU.mult).then_inc(stage_used, 1)

                dve.wait_ge(yd_used, b * NT + NT)
                gate_y(0)
                for k in range(KD):
                    dve.wait_ge(gm_hi_ok, b * KD + (k + 1))
                    V.scalar_tensor_tensor(out=gmT_lo[:, k, :], in0=aux[k % 4], scalar=col_a[:, R_GO + k:R_GO + k + 1],
                                           in1=gmT_hi[:, k, :].bitcast(F32), op0=ALU.mult, op1=ALU.subtract
                                           ).then_inc(gm_lo_ok, 1)
                gate_y(1)
                dve.wait_ge(stage_used, b * STAGED + (4 * (S_Z + 2) + 4))
                for j in range(2):
                    for t in range(NT):
                        rms_stats(j * NT + t, [y_sb[:, t, j * W:(j + 1) * W]])
                rms_rstd(8)
                for t in range(NT):
                    for j in range(2):
                        yy = y_sb[:, t, j * W:(j + 1) * W]
                        last = V.tensor_scalar(yy, yy, rstd[:, j * NT + t:j * NT + t + 1], None, ALU.mult)
                    last.then_inc(y_ok, 1)
                for k in range(KD):
                    dve.wait_ge(y_hi_ok, b * KD + (k + 1))
                    V.scalar_tensor_tensor(out=yT_lo[:, k, :], in0=aux[k % 4], scalar=col_a[:, R_SN + k:R_SN + k + 1],
                                           in1=yT_hi[:, k, :].bitcast(F32), op0=ALU.mult, op1=ALU.subtract
                                           ).then_inc(y_lo_ok, 1)

                def residual(G, j):
                    for t in range(NT):
                        full(G, t)
                        link(V.tensor_tensor(stage[:, t, HALO:], stage[:, t, HALO:], g_bc[:, j * W:(j + 1) * W], ALU.mult))
                        V.tensor_tensor(x2[:, t, j * W:(j + 1) * W], x2[:, t, j * W:(j + 1) * W], stage[:, t, HALO:],
                                        ALU.add).then_inc(stage_used, 1)

                dve.wait_ge(x2_in, b * 32 + 32)
                residual(G_OUT, 0)
                residual(G_OUT + 1, 1)
                dve.wait_ge(stage_used, b * STAGED + (4 * (S_OUT + 2) + 4))
                for t in range(NT):
                    rms_stats(t, [x2[:, t, 0:W], x2[:, t, W:D]])
                rms_rstd(NT)
                for t in range(NT):
                    V.tensor_scalar(xn2[:, t, :], x2[:, t, :], rstd[:, t:t + 1], None, ALU.mult).then_inc(xn_ok, 1)
                h_lows(b * 2 + 1, range(KD), 4 * KD, 3 * KD)

                with dve.Fori(0, KF // 2) as j:
                    fresh()
                    for i in range(2):
                        m = j * 2 + i
                        dve.wait_ge(evacuated, b * (4 * GROUPS) + j * 4 + (4 * G_UP + i + 5))
                        conv(b * CONVS + j * 2 + (KX + i + 1), i, 3, halo_f[:, bass.ds(m, 1), :].squeeze(1),
                             lambda tap: col_b[:, bass.ds(m + (R_FW + tap * KF), 1)],
                             col_b[:, bass.ds(m + R_FB, 1)], i)
                        V.tensor_copy(halo_f[:, bass.ds(m, 1), :].squeeze(1), stage[:, i, W + 1:]).then_inc(stage_used, 1)
                    for i in range(2):
                        m = j * 2 + i
                        dve.wait_ge(evacuated, b * (4 * GROUPS) + j * 4 + (4 * G_UP + i + 7))
                        dve.wait_ge(silu_done, b * CONVS + j * 2 + (KX + i + 3))
                        val = stage[:, 2 + i, HALO:]
                        link(V.tensor_tensor(val, val, acc[:, i, :], ALU.mult))
                        link(V.tensor_copy(g_hi[:, bass.ds(m, 1), :].squeeze(1), val))
                        V.tensor_tensor(g_lo[:, bass.ds(m, 1), :].squeeze(1), val,
                                        g_hi[:, bass.ds(m, 1), :].squeeze(1).bitcast(F32), ALU.subtract
                                        ).then_inc(stage_used, 1)
                fresh()
                norm_x(b + 1)
                h_lows(b * 2 + 2, range(KD), KD, 0)
                dve.wait_ge(g2_in, b * 16 + 16)
                residual(G_DOWN, 0)
                residual(G_DOWN + 1, 1)
                dve.wait_ge(stage_used, b * STAGED + (4 * (S_DOWN + 2) + 4))
                for t in range(NT):
                    rms_stats(t, [x2[:, t, 0:W], x2[:, t, W:D]])
                rms_rstd(NT)
                for t in range(NT):
                    V.scalar_tensor_tensor(out=x2[:, t, :], in0=x2[:, t, :], scalar=rstd[:, t:t + 1], in1=fg_bc[:],
                                           op0=ALU.mult, op1=ALU.mult).then_inc(out_ok, 1)

        @block.tensor
        def _(pe):
            T = nc.tensor
            pe.wait_ge(const_ok, 4)
            pe.wait_ge(rows_in, 160)
            T.transpose(aux[0][:, 0:ROWS_A], rows_a[0:ROWS_A, :], ident[0:ROWS_A, 0:ROWS_A]).then_inc(col_tr, 1)
            T.transpose(aux[0][:, P:P + ROWS_B], rows_b[0:ROWS_B, :], ident[0:ROWS_B, 0:ROWS_B]).then_inc(col_tr, 1)
            pe.wait_ge(small_in, 96)
            for h in range(GH):
                last = T.transpose(aux[2 + h // 4][:, (h % 4) * P:(h % 4 + 1) * P], ws_raw[:, h, :], ident[:])
                if h % 4 == 3:
                    last.then_inc(ws_tr, 1)
            pe.wait_ge(cact_ok, 1)
            pe.wait_ge(col_ok, 2)
            pe.wait_ge(ws_ok, 2)
            banks = main + aux
            for half in range(2):
                if half:
                    pe.wait_ge(mod_ok, 6)
                for k in range(KD):
                    i = half * KD + k
                    pe.wait_ge(ada_in[i % ADA_RING], 16 * (i // ADA_RING + 1))
                    for m in range(6):
                        last = T.matmul(banks[m][0:1, :], c_act[:, k:k + 1], ada_t[:, i % ADA_RING, m * W:(m + 1) * W],
                                        start=k == 0, stop=k == KD - 1)
                    last.then_inc(ada_done if k == KD - 1 else ada_used, 1)
            pe.wait_ge(mrow_in, 16)
            T.transpose(aux[0][:, 0:NM], rows_m[0:NM, :], ident[0:NM, 0:NM]).then_inc(mrow_tr, 1)

            def h_transpose(q, ks, tiles):
                for k in ks:
                    if k >= 4:
                        pe.wait_ge(h_lo_ok, q * KD + (k - 3))
                    for t in range(NT):
                        last = T.transpose(aux[k % 4][:, t * P:(t + 1) * P], tiles[t][:, k * P:(k + 1) * P], ident[:])
                    last.then_inc(h_tr, 1)

            xn = [xn01[:, 0, :], xn01[:, 1, :], xn23[:, 0, :], xn23[:, 1, :]]
            pe.wait_ge(mod_c_ok, 1)
            pe.wait_ge(xn_ok, NT)
            h_transpose(0, range(KD), xn)
            pe.wait_ge(h_lo_ok, KD)
            pe.sem_inc(w_used, RING)

            def unit(n_at, n, G_at, first, last, mms):
                pe.wait_ge(w_lo_ok, n_at)
                for i in range(4):
                    if first:
                        pe.wait_ge(evacuated, G_at + (i + 1))
                    for p, (a, w) in enumerate(mms(i)):
                        ins = T.matmul(main[i][:], a, w, start=first and p == 0, stop=last and p == 2)
                    if last and i < 3:
                        ins.then_inc(bank_done, 1)
                ins.then_inc(w_used, 1)

            def tokens_out(hi, lo, k, s):
                return lambda i: ((hi[:, k, i * P:(i + 1) * P], w_hi[:, s, :]), (hi[:, k, i * P:(i + 1) * P], w_lo[:, s, :]),
                                  (lo[:, k, i * P:(i + 1) * P], w_hi[:, s, :]))

            def channels_out(k, s):
                return lambda i: ((w_hi[:, s, i * P:(i + 1) * P], h_hi[:, k, :]), (w_hi[:, s, i * P:(i + 1) * P], h_lo[:, k, :]),
                                  (w_lo[:, s, i * P:(i + 1) * P], h_hi[:, k, :]))

            with pe.Fori(0, NB) as b:
                def run(n, G, k, K, mms):
                    unit(b * UNITS + (n + 1 + RING), n, b * (4 * GROUPS) + 4 * G, k == 0, k == K - 1, mms)

                for j in range(3):
                    for k in range(KD):
                        run(j * KD + k, j, k, KD, channels_out(k, k % RING))
                        if j == 0 and k == 1:
                            for t in range(NT):
                                ts = slice(t * P, (t + 1) * P)
                                for kk in range(KD):
                                    for p, (a, w) in enumerate(((h_hi, wdt_hi), (h_hi, wdt_lo), (h_lo, wdt_hi))):
                                        last = T.matmul(aux[3][:, t * NH:(t + 1) * NH], a[:, kk, ts], w[:, kk, :],
                                                        start=kk == 0 and p == 0, stop=kk == KD - 1 and p == 2)
                            last.then_inc(dt_mm, 1)
                        if j == 0 and k == 5:
                            pe.wait_ge(da_ok, b + 1)
                            for t in range(NT):
                                last = T.transpose(aux[3][0:NH, t * P:(t + 1) * P], da_t[:, t, :], ident[:])
                            last.then_inc(da_tr, 1)
                        if j == 1 and k == 1:
                            pe.wait_ge(acs_ok, b + 1)
                            pe.sem_inc(pe_past, 1)
                            for t in range(NT):
                                last = T.transpose(aux[3][:, t * NH:(t + 1) * NH], acsT[:, t * P:(t + 1) * P],
                                                   ident[0:NH, 0:NH])
                            last.then_inc(acs_tr, 1)

                def chunk_scores(cc):
                    ts = slice(cc * P, (cc + 1) * P)
                    if cc == 0:
                        pe.wait_ge(silu_done, b * CONVS + (KX + 2))
                    else:
                        pe.wait_ge(state_ok, b * NT + cc)
                        pe.wait_ge(yd_used, b * NT + cc)
                    for k in range(KD):
                        T.transpose(aux[k // 4][:, (k % 4) * P:(k % 4 + 1) * P], xT[:, k, ts], ident[:])
                    for g in range(2):
                        T.transpose(aux[2][:, g * P:(g + 1) * P], bcT[:, g, ts], ident[:])
                    for g in range(2):
                        last = T.matmul(aux[2][:, (2 + g) * P:(3 + g) * P], bcT[:, g, ts], bcT[:, 2 + g, ts],
                                        start=True, stop=True)
                    last.then_inc(t_done, 1)

                def chunk_yoff(cc):
                    pe.wait_ge(xs_ok, b * (3 * NT) + 3 * (cc + 1))
                    pe.wait_ge(cbm_ok, b * NT + (cc + 1))
                    pe.wait_ge(acs_t_ok, b + 1)
                    if cc:
                        pe.wait_ge(state_ok, b * NT + cc)
                    for g in range(2):
                        last = T.matmul(aux[2 + g], bcT[:, 2 + g, cc * P:(cc + 1) * P], state[:, g * W:(g + 1) * W],
                                        start=True, stop=True)
                    last.then_inc(yoff_done, 1)

                def chunk_state(cc):
                    pe.wait_ge(xdec_ok, b * NT + (cc + 1))
                    for g in range(2):
                        last = T.matmul(aux[g], b_tok[:, g, :], xdec[:, g * W:(g + 1) * W], start=True, stop=True)
                    last.then_inc(s_done, 1)

                def chunk_ydiag(cc):
                    pe.wait_ge(att_ok, b * NT + (cc + 1))
                    pe.wait_ge(yoff_used, b * NT + (cc + 1))
                    for h in range(NH):
                        o = (h % (NH // 2)) * HD
                        last = T.matmul(aux[2 + h // (NH // 2)][:, o:o + HD], arow[:, h, :], xdt[:, h * HD:(h + 1) * HD],
                                        start=True, stop=True)
                    last.then_inc(yd_done, 1)

                for cc in range(NT):
                    for k in range(KD):
                        run(UV + cc * KD + k, G_UV + cc, k, KD, tokens_out(h_hi, h_lo, k, k % RING))
                        if k == 1 and cc:
                            chunk_ydiag(cc - 1)
                        if k == 3:
                            chunk_scores(cc)
                        if k == 5:
                            chunk_yoff(cc)
                        if k == 7:
                            chunk_state(cc)

                def spatial(t):
                    pe.wait_ge(v_ok, b * NT + (t + 1))
                    if t < 2:
                        pe.wait_ge(state_ok, b * NT + NT)
                        pe.wait_ge(yd_used, b * NT + NT)
                    else:
                        pe.wait_ge(sv_used, b * NT + (t - 1))
                    for h in range(GH):
                        last = T.matmul(aux[2 * (t % 2) + h // 4][:, (h % 4) * P:(h % 4 + 1) * P], wsT[:, h, :],
                                        v_sb[:, h // 4, t, (h % 4) * P:(h % 4 + 1) * P], start=True, stop=True)
                    last.then_inc(sv_done, 1)

                def gm_transpose(ks):
                    for k in ks:
                        if k == 0:
                            pe.wait_ge(gm_ok, b * NT + NT)
                        if k >= 4:
                            pe.wait_ge(gm_lo_ok, b * KD + (k - 3))
                        for t in range(NT):
                            last = T.transpose(aux[k % 4][:, t * P:(t + 1) * P],
                                               u_sb[:, k // 4, t, (k % 4) * P:(k % 4 + 1) * P], ident[:])
                        last.then_inc(gm_tr, 1)

                def y_transpose(ks):
                    for k in ks:
                        if k == 0:
                            pe.wait_ge(y_ok, b * NT + NT)
                        if k >= 4:
                            pe.wait_ge(y_lo_ok, b * KD + (k - 3))
                        for t in range(NT):
                            last = T.transpose(aux[k % 4][:, t * P:(t + 1) * P], y_sb[:, t, k * P:(k + 1) * P], ident[:])
                        last.then_inc(y_tr, 1)

                for j in range(2):
                    for k in range(KD):
                        run(Z + j * KD + k, G_Z + j, k, KD, tokens_out(h_hi, h_lo, k, k % RING))
                        if j == 0 and k == 1:
                            chunk_ydiag(NT - 1)
                        if j == 0 and k == 5:
                            spatial(0)
                            spatial(1)
                        if j == 0 and k == 7:
                            spatial(2)
                        if j == 1 and k == 1:
                            spatial(3)
                        if j == 1 and k == 6:
                            gm_transpose(range(4))
                        if j == 1 and k == 7:
                            gm_transpose(range(4, KD))
                for j in range(2):
                    for k in range(2 * KD):
                        if j == 0 and k < KD:
                            pe.wait_ge(gm_lo_ok, b * KD + (k + 1))
                        if j == 0 and k >= KD:
                            pe.wait_ge(y_lo_ok, b * KD + (k - KD + 1))
                        ops = (gmT_hi, gmT_lo) if k < KD else (yT_hi, yT_lo)
                        run(OUT + j * 2 * KD + k, G_OUT + j, k, 2 * KD, tokens_out(*ops, k % KD, k % RING))
                        if j == 0 and k == 6:
                            y_transpose(range(4))
                        if j == 0 and k == 7:
                            y_transpose(range(4, KD))
                pe.wait_ge(xn_ok, b * (2 * NT) + 2 * NT)
                h_transpose(b * 2 + 1, range(KD), [xn2[:, t, :] for t in range(NT)])
                pe.wait_ge(h_lo_ok, b * (2 * KD) + 2 * KD)
                pe.sem_inc(pe_past, 1)
                with pe.Fori(0, KF // 2) as j:
                    for k in range(KD):
                        unit(b * UNITS + j * KD + (UP + k + 1 + RING), UP + k, b * (4 * GROUPS) + j * 4 + 4 * G_UP,
                             k == 0, k == KD - 1, channels_out(k, k % RING))
                for j in range(2):
                    for k in range(KF):
                        if j == 0:
                            if k == 0:
                                pe.wait_ge(stage_used, b * STAGED + (4 * S_DOWN))
                            if k >= KF - 2:
                                pe.wait_ge(stage_used, b * STAGED + (4 * S_DOWN + 4 - (KF - 1 - k)))
                        run(DOWN + j * KF + k, G_DOWN + j, k, KF, tokens_out(g_hi, g_lo, k, (j * KF + k) % RING))
                        if j == 0 and k == 13:
                            pe.wait_ge(xn_ok, b * (2 * NT) + 3 * NT)
                            h_transpose(b * 2 + 2, range(4), xn)
                        if j == 0 and k == 16:
                            h_transpose(b * 2 + 2, range(4, KD), xn)
                pe.wait_ge(h_lo_ok, b * (2 * KD) + 3 * KD)


_INS = ['x', 'c', 'ada_w', 'ada_b', 'norm1_g', 'norm2_g', 'w_in', 'ssd_conv_w', 'ssd_conv_b', 'ssd_dt_bias',
        'ssd_a_log', 'ssd_d', 'ssd_norm_g', 'gm_vnorm_g', 'gm_ws', 'gm_bs', 'gm_out_g', 'w_out', 'ff_up',
        'ff_conv_w', 'ff_conv_b', 'ff_down', 'final_g']


def kernel(**inputs):
    import numpy as _np
    import concourse.bacc as _bacc
    from concourse import mybir as _mybir
    from concourse.bass_utils import run_bass_kernel_spmd as _run

    nc = _bacc.Bacc("TRN2", target_bir_lowering=False, num_devices=1)
    arrays, args = {}, []
    for name in _INS:
        a = _np.ascontiguousarray(inputs[name])
        arrays[f"in_{name}_dram"] = a
        args.append(nc.dram_tensor(f"in_{name}_dram", a.shape, _mybir.dt.from_np(a.dtype), kind="ExternalInput").ap())
    out = nc.dram_tensor("out_dram", inputs["x"].shape, _mybir.dt.float32, kind="ExternalOutput").ap()
    hybrid_decoder_trunk(nc, *args, out)
    r = _run(nc, [arrays], core_ids=[0])
    return r.results[0]["out_dram"]
```

```python
import concourse.bass as bass
from concourse import mybir
from contextlib import ExitStack


def hybrid_decoder_trunk(nc, x, c, ada_w, ada_b, norm1_g, norm2_g, w_in, ssd_conv_w, ssd_conv_b, ssd_dt_bias,
                         ssd_a_log, ssd_d, ssd_norm_g, gm_vnorm_g, gm_ws, gm_bs, gm_out_g, w_out, ff_up,
                         ff_conv_w, ff_conv_b, ff_down, final_g, out):
    F32, F32R, I32 = mybir.dt.float32, mybir.dt.float32r, mybir.dt.int32
    ALU, ACT = mybir.AluOpType, mybir.ActivationFunctionType

    P, W = 128, 512
    _, SEQ, D = x.shape
    BT = W
    NB, NT = SEQ // BT, BT // P
    KD = D // P
    NH = ssd_d.shape[1]
    HD = D // NH
    CONV = ssd_conv_w.shape[2]
    NST = (CONV - D) // 4
    KX = CONV // P
    GH = gm_ws.shape[1]
    DFF = ff_down.shape[1]
    KF = DFF // P
    EPS = 1e-6
    COL_XBC, COL_DT, COL_U = D, D + CONV, D + CONV + NH
    MODS = ada_b.shape[1]
    assert NT == 4 and NST == P and GH == KD and P == gm_ws.shape[2]

    XBC, UV, Z, OUT, UP, DOWN = 0, 3 * KD, 7 * KD, 9 * KD, 9 * KD + 4 * KD, 13 * KD + (KF // 2) * KD
    UNITS = DOWN + 2 * KF
    G_UV, G_Z, G_OUT, G_UP, G_DOWN = 3, 7, 9, 11, 11 + KF // 2
    GROUPS = G_DOWN + 2
    S_Z, S_OUT, S_UP, S_DOWN = 3, 5, 7, 7 + KF // 2
    STAGED = 4 * (S_DOWN + 2)
    CONVS = KX + KF
    RING, LEAD, SP_LEAD = 4, 3, 4
    assert UNITS % RING == 0 and XBC % RING == UV % RING == Z % RING == OUT % RING == UP % RING == DOWN % RING == 0

    ctx = ExitStack()
    with ctx:
        place = [nc.sbuf_base + 31 & ~31]

        def fixed(name, shape, dt, at=None):
            n = 4
            for s in shape[1:]:
                n *= s
            if at is None:
                at = place[0]
                place[0] += n + 31 & ~31
            return nc.alloc_sbuf_tensor_at(name, shape, dt, offset=at), at

        w_raw, _ = fixed("w_raw", [P, RING, W], F32)
        w_hi, _ = fixed("w_hi", [P, RING, W], F32R)
        w_lo, _ = fixed("w_lo", [P, RING, W], F32R)
        x2, x2_at = fixed("x2", [P, NT, D], F32)
        h_hi, h_at = fixed("h_hi", [P, KD, BT], F32R)
        h_lo, _ = fixed("h_lo", [P, KD, BT], F32R)
        region, r_at = fixed("region", [P, 24, 1024], F32)
        KB = 1024
        xT, _ = fixed("xT", [P, KD, BT], F32, r_at)
        bcT, _ = fixed("bcT", [P, 4, BT], F32, r_at + 16 * KB)
        arow, _ = fixed("arow", [P, NH, P], F32, r_at + 24 * KB)
        gmT_hi, _ = fixed("gmT_hi", [P, KD, BT], F32R, r_at)
        gmT_lo, _ = fixed("gmT_lo", [P, KD, BT], F32R, r_at + 16 * KB)
        u_sb, _ = fixed("u_sb", [P, 2, NT, W], F32, r_at + 32 * KB)
        xn2, _ = fixed("xn2", [P, NT, D], F32, r_at + 32 * KB)
        v_sb, _ = fixed("v_sb", [P, 2, NT, W], F32, r_at + 48 * KB)
        yT_hi, _ = fixed("yT_hi", [P, KD, BT], F32R, r_at + 48 * KB)
        yT_lo, _ = fixed("yT_lo", [P, KD, BT], F32R, r_at + 64 * KB)
        xs, _ = fixed("xs", [P, D], F32, r_at + 64 * KB)
        xdt, _ = fixed("xdt", [P, D], F32, r_at + 68 * KB)
        xdec, _ = fixed("xdec", [P, D], F32, r_at + 72 * KB)
        sv_tmp, _ = fixed("sv_tmp", [P, 2, D], F32, r_at + 64 * KB)
        vg_bc, _ = fixed("vg_bc", [P, D], F32, r_at + 72 * KB)
        b_tok, _ = fixed("b_tok", [P, 2, P], F32, r_at + 76 * KB)
        cbm, _ = fixed("cbm", [P, 2, P], F32, r_at + 77 * KB)
        dl, _ = fixed("dl", [P, 2, NH], F32, r_at + 78 * KB)
        dex, _ = fixed("dex", [P, 2, NH], F32, r_at + 78 * KB + 512)
        y_sb, _ = fixed("y_sb", [P, NT, D], F32, r_at + 80 * KB)
        g_hi, _ = fixed("g_hi", [P, KF, BT], F32R, r_at)
        g_lo, _ = fixed("g_lo", [P, KF, BT], F32R, r_at + 2 * KF * KB)
        ADA_RING = 11
        ada_t, _ = fixed("ada_t", [P, ADA_RING, 2 * D], F32, r_at)
        gate_rows, _ = fixed("gate_rows", [1, 2 * D], F32, r_at + ADA_RING * 8 * KB)
        xn01, xn_at = fixed("xn01", [P, 2, D], F32)
        acsT, _ = fixed("acsT", [NH, BT], F32, xn_at)
        daT, _ = fixed("daT", [NH, BT], F32, xn_at + 2 * KB)
        dt_t, _ = fixed("dt_t", [P, NT, NH], F32, xn_at + 4 * KB)
        dt_b, _ = fixed("dt_b", [P, NT, NH], F32, xn_at + 4 * KB + 256)
        da_t, _ = fixed("da_t", [P, NT, NH], F32, xn_at + 4 * KB + 512)
        acs_t, _ = fixed("acs_t", [P, NT, NH], F32, xn_at + 4 * KB + 768)
        eacs_t, _ = fixed("eacs_t", [P, NT, NH], F32, xn_at + 5 * KB)
        dt_e, _ = fixed("dt_e", [P, NT, NH], F32, xn_at + 5 * KB + 256)
        dt_s, _ = fixed("dt_s", [P, NT, NH], F32, xn_at + 5 * KB + 512)
        dt_q, _ = fixed("dt_q", [P, NT, NH], F32, xn_at + 5 * KB + 768)
        dt_p, _ = fixed("dt_p", [P, NT, NH], F32, xn_at + 7 * KB)
        stats2, _ = fixed("stats2", [P, NT, 2, 6], F32, xn_at + 7 * KB + 256)
        HALO, SW = 3, W + 3
        stage, s_at = fixed("stage", [P, 4, SW], F32)
        xn23, _ = fixed("xn23", [P, 2, D], F32, s_at)
        acc, _ = fixed("acc", [P, 2, W], F32)
        g_bc, g_at = fixed("g_bc", [P, D], F32)
        fg_bc, _ = fixed("fg_bc", [P, D], F32, r_at + 92 * KB)
        state, st_at = fixed("state", [P, D], F32)
        wsT, _ = fixed("wsT", [P, GH, P], F32)
        ident, _ = fixed("ident", [P, P], F32)
        tri, _ = fixed("tri", [P, P], F32)
        wdt, _ = fixed("wdt", [P, 2 * KD * NH + P - NH], F32R)
        R_CONVW, R_CONVB = 0, 4 * KX
        R_SN, R_GO, R_N1, R_N2 = 5 * KX, 5 * KX + KD, 5 * KX + 2 * KD, 5 * KX + 3 * KD
        ROWS_A = 5 * KX + 4 * KD
        R_FW, R_FB, R_BS, R_AB = 0, 3 * KF, 4 * KF, 4 * KF + GH
        ROWS_B = 4 * KF + GH + 4 * KD
        assert ROWS_A <= P and ROWS_B <= P
        col_a, _ = fixed("col_a", [P, ROWS_A], F32)
        col_b, _ = fixed("col_b", [P, ROWS_B], F32)
        C_SH1, C_SC1, C_SH2, C_SC2 = 0, KD, 2 * KD, 3 * KD
        mod_c, _ = fixed("mod_c", [P, 4 * KD], F32)
        halo_x, _ = fixed("halo_x", [P, KX, 3], F32)
        halo_f, _ = fixed("halo_f", [P, KF, 2], F32)
        small, _ = fixed("small", [P, 3, NH], F32)
        stats, _ = fixed("stats", [P, 2, 6], F32)
        mv, _ = fixed("mv", [P, 8, 2], F32)
        ms, _ = fixed("ms", [P, 8], F32)
        rt, _ = fixed("rt", [P, 8], F32)
        rstd, _ = fixed("rstd", [P, 8], F32)
        c_act, _ = fixed("c_act", [P, KD], F32)
        zeros, _ = fixed("zeros", [NH, P], F32, xn_at + 6 * KB)
        assert place[0] <= nc.sbuf_usable_end, (place[0], nc.sbuf_usable_end)
        rows_a, _ = fixed("rows_a", [P, P], F32, st_at)
        rows_b, _ = fixed("rows_b", [P, P], F32, st_at + 512)
        wdt_raw, _ = fixed("wdt_raw", [P, KD, NH], F32, st_at + KB)
        c_rows, _ = fixed("c_rows", [KD, P], F32, st_at + 1536)
        ws_raw, _ = fixed("ws_raw", [P, GH, P], F32, g_at)
        mod_sum, _ = fixed("mod_sum", [P, 4, D], F32, x2_at)
        assert MODS == 6 * D

        def bank(name):
            return ctx.enter_context(nc.psum_tensor(name, [P, W], F32))

        main = [bank(f"main{i}") for i in range(4)]
        pair = [ctx.enter_context(nc.psum_tensor(f"pair{i}", [P, 2, W], F32)) for i in range(2)]
        aux = [pair[i // 2][:, i % 2, :] for i in range(4)]

        gate_d = nc.dram_tensor("gate_scratch", [2, D], F32, kind="Internal").ap()
        acs_d = nc.dram_tensor("acs_scratch", [NB * NT, NH, P], F32, kind="Internal").ap()

        def sem(name):
            return ctx.enter_context(nc.semaphore(name))

        w_in_dma = [sem(f"w_loaded{i}") for i in range(RING)]
        w_hi_ok = sem("w_hi_ok")
        w_lo_ok = sem("w_lo_ok")
        w_used = sem("w_used")
        bank_done = sem("bank_done")
        evacuated = sem("evacuated")
        stage_used = sem("stage_used")
        conv_done = sem("conv_done")
        silu_done = sem("silu_done")
        x_in = sem("x_in")
        xn_ok = sem("xn_ok")
        rstd_ok, xn_act_ok = sem("rstd_ok"), sem("xn_act_ok")
        h_tr = sem("h_tr")
        h_hi_ok, h_lo_ok = sem("h_hi_ok"), sem("h_lo_ok")
        x2_in = sem("x2_in")
        g2_in = sem("g2_in")
        vg_in = sem("vg_in")
        dt_mm, dtT_ok, dt_tr, dt_biased, dt_soft = (sem(n) for n in ("dt_mm", "dtT_ok", "dt_tr", "dt_biased", "dt_soft"))
        da_ok, da_tr, acs_ok, acs_tr = sem("da_ok"), sem("da_tr"), sem("acs_ok"), sem("acs_tr")
        acs_t_ok, eacs_ok, acs_stored = sem("acs_t_ok"), sem("eacs_ok"), sem("acs_stored")
        arow_in = sem("arow_in")
        t_done = sem("t_done")
        xs_ok = sem("xs_ok")
        cbm_ok = sem("cbm_ok")
        dl_ok, seg_ok, dex_ok, exp_ok = sem("dl_ok"), sem("seg_ok"), sem("dex_ok"), sem("exp_ok")
        xdec_ok, att_ok = sem("xdec_ok"), sem("att_ok")
        yoff_done, yoff_used = sem("yoff_done"), sem("yoff_used")
        s_done, state_ok = sem("s_done"), sem("state_ok")
        yd_done, yd_used = sem("yd_done"), sem("yd_used")
        v_ok, sv_done, sv_used, gm_ok = sem("v_ok"), sem("sv_done"), sem("sv_used"), sem("gm_ok")
        gm_tr, gm_hi_ok, gm_lo_ok = sem("gm_tr"), sem("gm_hi_ok"), sem("gm_lo_ok")
        y_ok, y_tr, y_hi_ok, y_lo_ok = sem("y_ok"), sem("y_tr"), sem("y_hi_ok"), sem("y_lo_ok")
        out_ok, out_stored = sem("out_ok"), sem("out_stored")
        const_ok, rows_in, small_in, pro_dma = sem("const_ok"), sem("rows_in"), sem("small_in"), sem("pro_dma")
        ada_in = [sem(f"ada_in{i}") for i in range(ADA_RING)]
        ada_summed, ada_gated = sem("ada_summed"), sem("ada_gated")
        gate_ok, gate_stored = sem("gate_ok"), sem("gate_stored")
        c_in, c_tr = sem("c_in"), sem("c_tr")
        col_tr, col_ok, cact_ok, ws_tr, ws_ok, mod_col = (sem(n) for n in (
            "col_tr", "col_ok", "cact_ok", "ws_tr", "ws_ok", "mod_col"))
        wdt_h, wdt_l, a_exp = sem("wdt_h"), sem("wdt_l"), sem("a_exp")
        ready = sem("ready")
        pe_past = sem("pe_past")
        dve_step = sem("dve_step")

        def slot_full(b, n):
            return b * (16 * UNITS // RING) + 16 * (n // RING + 1)

        block = ctx.enter_context(nc.Block())

        @block.sync
        def _(sp):
            xv = x[0].rearrange("(b t p) d -> b t p d", t=NT, p=P)

            def load_x(b):
                for t in range(NT):
                    dst = xn01[:, t, :] if t < 2 else xn23[:, t - 2, :]
                    sp.dma_start(dst, xv[bass.ds(b, 1), t, :, :].squeeze(0)).then_inc(x_in, 16)

            def rows(w, k):
                return w[0, k * P:(k + 1) * P, :]

            def load(b, n, src, dst_view=None):
                sp.wait_ge(w_lo_ok, b * UNITS + (n + 1))
                dst = w_raw[:, n % RING, :]
                sp.dma_start(dst if dst_view is None else dst_view(dst), src).then_inc(w_in_dma[n % RING], 16)

            def xbc_unit(b, n):
                j, k = n // KD, n % KD
                load(b, n, rows(w_in, k)[:, COL_XBC + j * W:COL_XBC + (j + 1) * W])

            sp.dma_start(c_rows[:], c[0].rearrange("(k p) -> k p", p=P)).then_inc(c_in, 16)
            for i in range(3 * KD):
                third, k = i // KD, i % KD
                if i >= ADA_RING:
                    sp.wait_ge(ada_summed, i - ADA_RING + 1)
                if i >= ADA_RING + KD:
                    sp.wait_ge(ada_gated, i - ADA_RING - KD + 1)
                sp.dma_start(ada_t[:, i % ADA_RING, :], ada_w[0, k * P:(k + 1) * P, third * 2 * D:(third + 1) * 2 * D]
                             ).then_inc(ada_in[i % ADA_RING], 16)
                if i == 2 * KD:
                    for n in range(SP_LEAD):
                        xbc_unit(0, n)
            sp.sem_inc(out_stored, 64)
            sp.wait_ge(gate_ok, 4)
            sp.dma_start(gate_d.rearrange("g d -> (g d)").unsqueeze(0), gate_rows[0:1, :]).then_inc(gate_stored, 16)
            with sp.Fori(0, NB) as b:
                for n in range(SP_LEAD, 3 * KD):
                    xbc_unit(b, n)
                    if n == 12:
                        sp.wait_ge(out_stored, b * 64 + 64)
                        sp.dma_start(x2[:], x[0].rearrange("(b t p) d -> b p t d", t=NT, p=P)[bass.ds(b, 1)]
                                     .squeeze(0)).then_inc(x2_in, 16)
                        sp.wait_ge(gate_stored, 16)
                        sp.dma_start(g_bc[:], gate_d[0:1, :].broadcast_to([P, D])
                                     ).then_inc(x2_in, 16)
                for cc in range(NT):
                    for k in range(KD):
                        n = UV + cc * KD + k
                        load(b, n, rows(w_in, k)[:, COL_U + cc * W:COL_U + (cc + 1) * W])
                        if k == 5:
                            if cc == 0:
                                sp.wait_ge(acs_stored, b * 16 + 16)
                            else:
                                sp.wait_ge(yd_done, b * NT + cc)
                            sp.dma_start(arow[:], acs_d[bass.ds(b * NT + cc, 1)].rearrange("o h l -> o (h l)")
                                         .broadcast_to([P, NH * P])).then_inc(arow_in, 16)
                for j in range(2):
                    for k in range(KD):
                        load(b, Z + j * KD + k, rows(w_in, k)[:, j * W:(j + 1) * W])
                        if j == 0 and k == 3:
                            sp.wait_ge(s_done, b * NT + NT)
                            sp.dma_start(vg_bc[:], gm_vnorm_g.broadcast_to([P, D])).then_inc(vg_in, 16)
                for j in range(2):
                    for k in range(2 * KD):
                        kk = (k + KD) % (2 * KD)
                        load(b, OUT + j * 2 * KD + k, rows(w_out, kk)[:, j * W:(j + 1) * W])
                with sp.Fori(0, KF // 2) as j:
                    for k in range(KD):
                        n = UP + k
                        sp.wait_ge(w_lo_ok, b * UNITS + j * KD + (n + 1))
                        src = rows(ff_up, k).rearrange("p (g n) -> p g n", g=2)[:, :, bass.ds(j * (2 * P), 2 * P)]
                        sp.dma_start(w_raw[:, n % RING, :].rearrange("p (g n) -> p g n", g=2), src
                                     ).then_inc(w_in_dma[n % RING], 16)
                nxt = (b + 1) % NB
                for j in range(2):
                    for k in range(KF):
                        load(b, DOWN + j * KF + k, rows(ff_down, k)[:, j * W:(j + 1) * W])
                        if j == 0 and k == 7:
                            sp.wait_ge(stage_used, b * STAGED + (4 * S_DOWN + 4))
                            sp.dma_start(g_bc[:], gate_d[1:2, :].broadcast_to([P, D])
                                         ).then_inc(g2_in, 16)
                            sp.dma_start(fg_bc[:], final_g.unsqueeze(0).broadcast_to([P, D])).then_inc(g2_in, 16)
                            load_x(nxt)
                for n in range(SP_LEAD):
                    sp.wait_ge(w_lo_ok, b * UNITS + (UNITS + n + 1))
                    sp.dma_start(w_raw[:, n, :], rows(w_in, n)[:, COL_XBC:COL_XBC + W]).then_inc(w_in_dma[n], 16)
                for t in range(NT):
                    sp.wait_ge(out_ok, b * NT + (t + 1))
                    sp.dma_start(out[0].rearrange("(b t p) d -> b t p d", t=NT, p=P)[bass.ds(b, 1), t, :, :].squeeze(0),
                                 x2[:, t, :]).then_inc(out_stored, 16)
            sp.wait_ge(out_stored, 64 * (NB + 1))

        @block.gpsimd
        def _(pool):
            nc.gpsimd.memset(ident[:], 0.0).then_inc(const_ok, 1)
            nc.gpsimd.memset(tri[:], 1.0).then_inc(const_ok, 1)
            pool.wait_ge(const_ok, 2)
            nc.gpsimd.affine_select(out=ident[:], in_=ident[:], compare_op=ALU.not_equal, fill=1.0, base=0,
                                    pattern=[[-1, P]], channel_multiplier=1).then_inc(const_ok, 1)
            nc.gpsimd.affine_select(out=tri[:], in_=tri[:], compare_op=ALU.is_ge, fill=0.0, base=0,
                                    pattern=[[1, P]], channel_multiplier=-1).then_inc(const_ok, 1)
            pool.sem_inc(w_lo_ok, RING)
            with pool.Fori(0, NB * UNITS // RING) as q:
                for s in range(RING):
                    pool.wait_ge(w_hi_ok, q * RING + (s + 1))
                    pool.wait_ge(w_used, q * RING + (s + 1))
                    nc.gpsimd.tensor_tensor(w_lo[:, s, :], w_raw[:, s, :], w_hi[:, s, :].bitcast(F32),
                                            ALU.subtract).then_inc(w_lo_ok, 1)

        @block.scalar
        def _(act):
            for r, n, src in ((R_CONVW, 4 * KX, ssd_conv_w[0].rearrange("k (j p) -> (k j) p", p=P)),
                              (R_CONVB, KX, ssd_conv_b[0].rearrange("(j p) -> j p", p=P)),
                              (R_SN, KD, ssd_norm_g[0].rearrange("(j p) -> j p", p=P)),
                              (R_GO, KD, gm_out_g[0].rearrange("(j p) -> j p", p=P)),
                              (R_N1, KD, norm1_g[0].rearrange("(j p) -> j p", p=P)),
                              (R_N2, KD, norm2_g[0].rearrange("(j p) -> j p", p=P))):
                act.dma_start(rows_a[r:r + n, :], src).then_inc(rows_in, 16)
            bias_rows = ada_b[0].rearrange("(h j p) -> h j p", h=2, p=P)
            for r, n, src in ((R_FW, 3 * KF, ff_conv_w[0].rearrange("k (j p) -> (k j) p", p=P)),
                              (R_FB, KF, ff_conv_b[0].rearrange("(j p) -> j p", p=P)), (R_BS, GH, gm_bs[0]),
                              (R_AB, 2 * KD, bias_rows[0, 0:2 * KD, :]), (R_AB + 2 * KD, 2 * KD, bias_rows[1, 0:2 * KD, :])):
                act.dma_start(rows_b[r:r + n, :], src).then_inc(rows_in, 16)
            act.dma_start(ws_raw[:], gm_ws[0].rearrange("h t s -> t h s")).then_inc(small_in, 16)
            act.dma_start(wdt_raw[:], w_in[0, :, COL_DT:COL_U].rearrange("(k p) n -> p k n", p=P)).then_inc(small_in, 16)
            for n, src in enumerate((ssd_a_log, ssd_d, ssd_dt_bias)):
                act.dma_start(small[:, n, :], src.broadcast_to([P, NH])).then_inc(small_in, 16)
            act.wait_ge(c_tr, 1)
            nc.scalar.activation(c_act[:], aux[1][:, 0:KD], ACT.Silu).then_inc(cact_ok, 1)
            for t in range(NT):
                act.dma_start(xn01[:, t, :] if t < 2 else xn23[:, t - 2, :], x[0, t * P:(t + 1) * P, :]).then_inc(x_in, 16)
            for g in range(2):
                act.dma_start(gate_rows[0:1, g * D:(g + 1) * D], ada_b[:, (2 + 3 * g) * D:(3 + 3 * g) * D]
                              ).then_inc(pro_dma, 16)
            act.wait_ge(small_in, 80)
            nc.scalar.activation(small[:, 0, :], small[:, 0, :], ACT.Exp).then_inc(a_exp, 1)
            nc.scalar.activation(wdt[:, 0:KD * NH].rearrange("p (k n) -> p k n", k=KD), wdt_raw[:], ACT.Copy).then_inc(wdt_h, 1)
            act.sem_inc(evacuated, 4)
            act.sem_inc(silu_done, 2)

            def split(b, n):
                act.wait_ge(w_in_dma[n % RING], slot_full(b, n))
                act.wait_ge(w_used, b * UNITS + (n + 1))
                nc.scalar.activation(w_hi[:, n % RING, :], w_raw[:, n % RING, :], ACT.Copy).then_inc(w_hi_ok, 1)

            def bank_ready(b, G, last, i):
                if i < 3:
                    act.wait_ge(bank_done, b * (3 * GROUPS) + (3 * G + i + 1))
                else:
                    act.wait_ge(w_used, b * UNITS + (last + 1 + RING))

            def evac_to_stage(b, G, S, last, func, banks=range(4)):
                for i in banks:
                    bank_ready(b, G, last, i)
                    act.wait_ge(stage_used, b * STAGED + (4 * S + i + 1))
                    nc.scalar.activation(stage[:, i, HALO:], main[i][:], func).then_inc(evacuated, 1)

            def silu_tile(b, cv, src, dst):
                act.wait_ge(conv_done, b * CONVS + (cv + 1))
                nc.scalar.activation(dst, src, ACT.Silu).then_inc(silu_done, 1)

            def h_tiles(q, ks, col_scale, col_bias):
                for k in ks:
                    act.wait_ge(h_tr, q * KD + (k + 1))
                    nc.scalar.activation(h_hi[:, k, :], aux[k % 4], ACT.Identity, bias=mod_c[:, col_bias + k:col_bias + k + 1],
                                         scale=mod_c[:, col_scale + k:col_scale + k + 1]).then_inc(h_hi_ok, 1)

            act.wait_ge(ready, 1)
            h_tiles(0, range(KD), C_SC1, C_SH1)
            for n in range(LEAD):
                split(0, n)
            act.wait_ge(ready, 2)
            with act.Fori(0, NB) as b:
                at = LEAD
                for j in range(3):
                    for n in range(at, (j + 1) * KD + LEAD):
                        split(b, n)
                        if j == 0 and n == 9:
                            act.wait_ge(dt_biased, b + 1)
                            nc.scalar.activation(dt_e[:], dt_e[:], ACT.Exp, scale=-1.0).then_inc(dt_soft, 1)
                        if j == 2 and n == 2 * KD + 6:
                            act.wait_ge(acs_ok, b + 1)
                            act.dma_start(acs_d[bass.ds(b * NT, NT)].rearrange("c h l -> h c l"),
                                          acsT[:].rearrange("h (c l) -> h c l", l=P)).then_inc(acs_stored, 16)
                            act.wait_ge(acs_t_ok, b + 1)
                            nc.scalar.activation(eacs_t[:], acs_t[:], ACT.Exp).then_inc(eacs_ok, 1)
                    evac_to_stage(b, j, j, (j + 1) * KD - 1, ACT.Copy)
                    for i in range(4):
                        kx = 4 * j + i
                        silu_tile(b, kx, acc[:, kx % 2, :], xT[:, kx, :] if kx < KD else bcT[:, kx - KD, :])
                        if i in (1, 2):
                            split(b, (j + 1) * KD + LEAD + i - 1)
                    at = (j + 1) * KD + LEAD + 2
                for cc in range(NT):
                    n0, n1 = UV + cc * KD, UV + (cc + 1) * KD
                    at = max(at, n0 + LEAD)
                    for n in range(at, n1 + LEAD):
                        split(b, n)
                        if n == n0 + (8 if cc == 0 else 7):
                            act.wait_ge(t_done, b * NT + (cc + 1))
                            for h in range(2):
                                nc.scalar.activation(xs[:, h * W:(h + 1) * W], aux[h], ACT.Copy).then_inc(xs_ok, 1)
                            nc.scalar.activation(b_tok[:], aux[2][:, 0:2 * P].rearrange("p (g n) -> p g n", g=2),
                                                 ACT.Copy).then_inc(xs_ok, 1)
                        if n == n0 + (9 if cc == 0 else 8):
                            act.wait_ge(dl_ok, b * NT + (cc + 1))
                            nc.scalar.activation(dex[:], dl[:], ACT.Exp).then_inc(dex_ok, 1)
                            act.wait_ge(seg_ok, b * NT + (cc + 1))
                            nc.scalar.activation(arow[:], arow[:], ACT.Exp).then_inc(exp_ok, 1)
                    for i in range(4):
                        bank_ready(b, G_UV + cc, n1 - 1, i)
                        dst = (u_sb if cc < 2 else v_sb)[:, cc % 2, i, :]
                        nc.scalar.activation(dst, main[i][:], ACT.Gelu).then_inc(evacuated, 1)
                for j in range(2):
                    for n in range(Z + j * KD + LEAD, Z + (j + 1) * KD + LEAD):
                        split(b, n)
                        if j == 1 and n == OUT + LEAD - 1:
                            for k in range(KD):
                                act.wait_ge(gm_tr, b * KD + (k + 1))
                                nc.scalar.activation(gmT_hi[:, k, :], aux[k % 4], ACT.Copy,
                                                     scale=col_a[:, R_GO + k:R_GO + k + 1]).then_inc(gm_hi_ok, 1)
                    evac_to_stage(b, G_Z + j, S_Z + j, Z + (j + 1) * KD - 1, ACT.Silu)
                for j in range(2):
                    n0 = OUT + 2 * j * KD
                    for n in range(n0 + LEAD, n0 + 2 * KD + (0 if j else LEAD)):
                        split(b, n)
                        if j == 0 and n in (n0 + LEAD + 6, n0 + LEAD + 7):
                            for k in range(4) if n == n0 + LEAD + 6 else range(4, KD):
                                act.wait_ge(y_tr, b * KD + (k + 1))
                                nc.scalar.activation(yT_hi[:, k, :], aux[k % 4], ACT.Copy,
                                                     scale=col_a[:, R_SN + k:R_SN + k + 1]).then_inc(y_hi_ok, 1)
                    if j == 0:
                        evac_to_stage(b, G_OUT, S_OUT, n0 + 2 * KD - 1, ACT.Copy)
                evac_to_stage(b, G_OUT + 1, S_OUT + 1, UP - 1, ACT.Copy, range(3))
                split(b, UP)
                split(b, UP + 1)
                evac_to_stage(b, G_OUT + 1, S_OUT + 1, UP - 1, ACT.Copy, (3,))
                split(b, UP + 2)
                act.wait_ge(rstd_ok, b + 1)
                for t in (2, 3):
                    nc.scalar.activation(xn2[:, t, :], x2[:, t, :], ACT.Copy, scale=rstd[:, t:t + 1]
                                         ).then_inc(xn_act_ok, 1)
                h_tiles(b * 2 + 1, range(KD), C_SC2, C_SH2)
                with act.Fori(0, KF // 2) as j:
                    for m in range(KD):
                        n = UP + LEAD + m
                        act.wait_ge(w_in_dma[n % RING], b * (16 * UNITS // RING) + j * (16 * KD // RING) + 16 * (n // RING + 1))
                        act.wait_ge(w_used, b * UNITS + j * KD + (n + 1))
                        nc.scalar.activation(w_hi[:, n % RING, :], w_raw[:, n % RING, :], ACT.Copy).then_inc(w_hi_ok, 1)
                    for i in range(4):
                        if i < 3:
                            act.wait_ge(bank_done, b * (3 * GROUPS) + j * 3 + (3 * G_UP + i + 1))
                        else:
                            act.wait_ge(w_used, b * UNITS + j * KD + (UP + KD + RING))
                        act.wait_ge(stage_used, b * STAGED + j * 4 + (4 * S_UP + i + 1))
                        nc.scalar.activation(stage[:, i, HALO:], main[i][:], ACT.Copy).then_inc(evacuated, 1)
                    for i in range(2):
                        act.wait_ge(conv_done, b * CONVS + j * 2 + (KX + i + 1))
                        nc.scalar.activation(acc[:, i, :], acc[:, i, :], ACT.Silu).then_inc(silu_done, 1)
                for j in range(2):
                    n0 = DOWN + j * KF
                    for n in range(n0 + LEAD, n0 + KF + LEAD):
                        split(b, n)
                        if j == 0 and n == n0 + 13 + LEAD:
                            h_tiles(b * 2 + 2, range(4), C_SC1, C_SH1)
                        if j == 0 and n == n0 + 16 + LEAD:
                            h_tiles(b * 2 + 2, range(4, KD), C_SC1, C_SH1)
                    evac_to_stage(b, G_DOWN + j, S_DOWN + j, n0 + KF - 1, ACT.Copy)

        @block.vector
        def _(dve):
            steps = [0]

            def link(ins):
                steps[0] += 1
                ins.then_inc(dve_step, 1)
                dve.wait_ge(dve_step, steps[0])

            def fresh():
                dve.sem_clear(dve_step)
                steps[0] = 0

            V = nc.vector

            def rms_stats(i, parts):
                for s, part in enumerate(parts):
                    last = V.bn_stats(stats[:, s, :], part)
                link(last)
                link(V.bn_aggr(mv[:, i, :], stats[:, 0:len(parts), :]))

            def rms_rstd(n, done=None):
                link(V.tensor_tensor(ms[:, 0:n], mv[:, 0:n, 0], mv[:, 0:n, 0], ALU.mult))
                link(V.scalar_tensor_tensor(out=ms[:, 0:n], in0=ms[:, 0:n], scalar=EPS, in1=mv[:, 0:n, 1],
                                            op0=ALU.add, op1=ALU.add))
                link(V.tensor_scalar(rt[:, 0:n].bitcast(I32), ms[:, 0:n].bitcast(I32), 1, None,
                                     ALU.arith_shift_right))
                link(V.tensor_scalar(rstd[:, 0:n].bitcast(I32), rt[:, 0:n].bitcast(I32), -1.0, float(0x5F3759DF),
                                     ALU.mult, ALU.add))
                for it in range(3):
                    link(V.tensor_tensor(rt[:, 0:n], rstd[:, 0:n], rstd[:, 0:n], ALU.mult))
                    link(V.scalar_tensor_tensor(out=rt[:, 0:n], in0=rt[:, 0:n], scalar=-0.5, in1=ms[:, 0:n],
                                                op0=ALU.mult, op1=ALU.mult))
                    ins = V.scalar_tensor_tensor(out=rstd[:, 0:n], in0=rt[:, 0:n], scalar=1.5, in1=rstd[:, 0:n],
                                                 op0=ALU.add, op1=ALU.mult)
                    if it == 2 and done is not None:
                        ins.then_inc(done, 1)
                    else:
                        link(ins)

            def h_lows(q, ks, col_scale, col_bias):
                for k in ks:
                    dve.wait_ge(h_hi_ok, q * KD + (k + 1))
                    link(V.tensor_scalar(acc[:, k % 2, :], aux[k % 4], mod_c[:, col_scale + k:col_scale + k + 1],
                                         mod_c[:, col_bias + k:col_bias + k + 1], ALU.mult, ALU.add))
                    V.tensor_tensor(h_lo[:, k, :], acc[:, k % 2, :], h_hi[:, k, :].bitcast(F32),
                                    ALU.subtract).then_inc(h_lo_ok, 1)

            def norm_x(p):
                tiles = [xn01[:, 0, :], xn01[:, 1, :], xn23[:, 0, :], xn23[:, 1, :]]
                dve.wait_ge(x_in, p * (16 * NT) + 16 * NT)
                for t in range(NT):
                    rms_stats(t, [tiles[t][:, 0:W], tiles[t][:, W:D]])
                rms_rstd(NT)
                for t in range(NT):
                    V.tensor_scalar(tiles[t], tiles[t], rstd[:, t:t + 1], None, ALU.mult).then_inc(xn_ok, 1)

            def ada_sum(i):
                third, k = i // KD, i % KD
                piece = ada_t[:, i % ADA_RING, :]
                cols, dst = ((slice(0, 2 * D), mod_sum[:, 0:2, :].rearrange("p m d -> p (m d)")),
                             (slice(D, 2 * D), mod_sum[:, 2, :]), (slice(0, D), mod_sum[:, 3, :]))[third]
                dve.wait_ge(ada_in[i % ADA_RING], 16 * (i // ADA_RING + 1))
                if k:
                    dve.wait_ge(ada_summed, i)
                    V.scalar_tensor_tensor(out=dst, in0=piece[:, cols], scalar=c_act[:, k:k + 1], in1=dst,
                                           op0=ALU.mult, op1=ALU.add).then_inc(ada_summed, 1)
                else:
                    V.tensor_scalar(dst, piece[:, cols], c_act[:, k:k + 1], None, ALU.mult).then_inc(ada_summed, 1)

            def mod_columns(n, gain_at):
                dve.wait_ge(mod_col, n + 1)
                cols = mod_c[:, 2 * n * KD:(2 * n + 2) * KD]
                link(V.tensor_tensor(cols, aux[0][:, 0:2 * KD], col_b[:, R_AB + 2 * n * KD:R_AB + (2 * n + 2) * KD], ALU.add))
                V.scalar_tensor_tensor(out=cols[:, KD:], in0=cols[:, KD:], scalar=1.0, in1=col_a[:, gain_at:gain_at + KD],
                                       op0=ALU.add, op1=ALU.mult).then_inc(ready, 1)
                dve.wait_ge(ready, n + 1)

            V.memset(halo_x[:], 0.0)
            V.memset(halo_f[:], 0.0)
            dve.wait_ge(cact_ok, 1)
            for i in range(3):
                ada_sum(i)
            dve.wait_ge(col_tr, 2)
            V.tensor_copy(col_a[:], aux[0][:, 0:ROWS_A]).then_inc(col_ok, 1)
            V.tensor_copy(col_b[:], aux[0][:, P:P + ROWS_B]).then_inc(col_ok, 1)
            for i in range(3, KD - 1):
                ada_sum(i)
            for g in range(2):
                dve.wait_ge(ws_tr, g + 1)
                V.tensor_tensor(wsT[:, 4 * g:4 * g + 4, :], aux[2 + g].rearrange("p (h n) -> p h n", h=4),
                                tri[:].unsqueeze(1).broadcast_to([P, 4, P]), ALU.mult).then_inc(ws_ok, 1)
            dve.wait_ge(wdt_h, 1)
            V.memset(wdt[:, 2 * KD * NH:].bitcast(F32), 0.0)
            link(V.tensor_tensor(wdt[:, KD * NH:2 * KD * NH].rearrange("p (k n) -> p k n", k=KD), wdt_raw[:],
                                 wdt[:, 0:KD * NH].rearrange("p (k n) -> p k n", k=KD).bitcast(F32), ALU.subtract))
            V.memset(state[:], 0.0)
            dve.wait_ge(a_exp, 1)
            link(V.tensor_scalar(small[:, 0, :], small[:, 0, :], -1.0, None, ALU.mult))
            ada_sum(KD - 1)
            norm_x(0)
            dve.wait_ge(col_ok, 2)
            mod_columns(0, R_N1)
            for i in range(KD, 3 * KD):
                ada_sum(i)
                if i < 2 * KD:
                    h_lows(0, (i - KD,), C_SC1, C_SH1)
                if i in (2 * KD, 3 * KD - 1):
                    g = i // (3 * KD - 1)
                    dve.wait_ge(pro_dma, 32)
                    dve.wait_ge(ada_gated, (g + 1) * KD)
                    for m in (2 * g, 2 * g + 1):
                        row = gate_rows[0:1, m * W:(m + 1) * W]
                        V.tensor_tensor(row, main[m][0:1, :], row, ALU.add).then_inc(gate_ok, 1)
            mod_columns(1, R_N2)
            dve.sem_inc(stage_used, 4)

            with dve.Fori(0, NB) as b:
                fresh()
                dve.wait_ge(dt_mm, b + 1)
                V.tensor_copy(daT[:], aux[3][0:NH, :]).then_inc(dtT_ok, 1)
                dve.wait_ge(dt_tr, b + 1)
                link(V.tensor_tensor(dt_b[:], aux[3][:, 0:NT * NH].rearrange("p (t h) -> p t h", h=NH),
                                     small[:, 2, :].unsqueeze(1).broadcast_to([P, NT, NH]), ALU.add))
                V.scalar_tensor_tensor(out=dt_e[:], in0=dt_b[:], scalar=-1.0, in1=dt_b[:], op0=ALU.mult, op1=ALU.max
                                       ).then_inc(dt_biased, 1)
                dve.wait_ge(dt_soft, b + 1)
                link(V.tensor_scalar(dt_s[:], dt_e[:], 2.0, None, ALU.add))
                link(V.reciprocal(dt_s[:], dt_s[:]))
                link(V.tensor_tensor(dt_s[:], dt_s[:], dt_e[:], ALU.mult))
                link(V.tensor_tensor(dt_q[:], dt_s[:], dt_s[:], ALU.mult))
                link(V.tensor_scalar(dt_p[:], dt_q[:], 1.0 / 19.0, None, ALU.mult))
                for n in range(17, 1, -2):
                    link(V.scalar_tensor_tensor(out=dt_p[:], in0=dt_p[:], scalar=1.0 / n, in1=dt_q[:],
                                                op0=ALU.add, op1=ALU.mult))
                link(V.scalar_tensor_tensor(out=dt_p[:], in0=dt_p[:], scalar=1.0, in1=dt_s[:],
                                            op0=ALU.add, op1=ALU.mult))
                link(V.tensor_scalar(dt_b[:], dt_b[:], 0.0, None, ALU.max))
                link(V.scalar_tensor_tensor(out=dt_t[:], in0=dt_p[:], scalar=2.0, in1=dt_b[:],
                                            op0=ALU.mult, op1=ALU.add))
                V.tensor_tensor(da_t[:], dt_t[:], small[:, 0, :].unsqueeze(1).broadcast_to([P, NT, NH]),
                                ALU.mult).then_inc(da_ok, 1)

                def conv(cv, i, taps, halo, wcol, bcol, a):
                    K = taps
                    link(V.tensor_copy(stage[:, i, HALO - (K - 1):HALO], halo))
                    dve.wait_ge(silu_done, cv)
                    link(V.tensor_scalar(acc[:, a, :], stage[:, i, HALO:], wcol(K - 1), bcol, ALU.mult, ALU.add))
                    for tap in range(K - 1):
                        lo = HALO - (K - 1) + tap
                        ins = V.scalar_tensor_tensor(out=acc[:, a, :], in0=stage[:, i, lo:lo + W], scalar=wcol(tap),
                                                     in1=acc[:, a, :], op0=ALU.mult, op1=ALU.add)
                        if tap < K - 2:
                            link(ins)
                        else:
                            ins.then_inc(conv_done, 1)

                def full(G, i):
                    dve.wait_ge(evacuated, b * (4 * GROUPS) + (4 * G + i + 5))

                for j in range(3):
                    for i in range(4):
                        kx = 4 * j + i
                        full(j, i)
                        conv(b * CONVS + (kx + 1), i, 4, halo_x[:, kx, :],
                             lambda tap: col_a[:, R_CONVW + tap * KX + kx:R_CONVW + tap * KX + kx + 1],
                             col_a[:, R_CONVB + kx:R_CONVB + kx + 1], kx % 2)
                        V.tensor_copy(halo_x[:, kx, :], stage[:, i, W:]).then_inc(stage_used, 1)
                    if j == 0:
                        dve.wait_ge(da_tr, b + 1)
                        V.memset(zeros[:], 0.0)
                        link(V.tensor_copy(daT[:], aux[3][0:NH, :]))
                        for t in range(NT):
                            s = slice(t * P, (t + 1) * P)
                            last = V.tensor_tensor_scan(acsT[:, s], daT[:, s], zeros[:], 0.0,
                                                        ALU.add, ALU.add)
                        last.then_inc(acs_ok, 1)
                        dve.wait_ge(acs_tr, b + 1)
                        V.tensor_copy(acs_t[:], aux[3][:, 0:NT * NH].rearrange("p (t h) -> p t h", h=NH)
                                      ).then_inc(acs_t_ok, 1)

                def heads(ap):
                    return ap.rearrange("p (h d) -> p h d", h=NH)

                for cc in range(NT):
                    dve.wait_ge(arow_in, b * (16 * NT) + 16 * (cc + 1))
                    if cc == 0:
                        dve.wait_ge(acs_t_ok, b + 1)
                    V.tensor_tensor(dl[:, 0, :], arow[:, :, P - 1], acs_t[:, cc, :], ALU.subtract)
                    V.tensor_copy(dl[:, 1, :], arow[:, :, P - 1]).then_inc(dl_ok, 1)
                    dve.wait_ge(dl_ok, b * NT + (cc + 1))
                    for h in range(NH):
                        last = V.tensor_scalar(arow[:, h, :], arow[:, h, :], acs_t[:, cc, h:h + 1], 0.0,
                                               ALU.subtract, ALU.min)
                    last.then_inc(seg_ok, 1)
                    dve.wait_ge(xs_ok, b * (3 * NT) + 3 * (cc + 1))
                    V.tensor_tensor(cbm[:], aux[2][:, 2 * P:4 * P].rearrange("p (g n) -> p g n", g=2),
                                    tri[:].unsqueeze(1).broadcast_to([P, 2, P]), ALU.mult).then_inc(cbm_ok, 1)
                    link(V.tensor_tensor(heads(xdt[:]), heads(xs[:]), dt_t[:, cc, :].unsqueeze(2)
                                         .broadcast_to([P, NH, HD]), ALU.mult))
                    dve.wait_ge(dex_ok, b * NT + (cc + 1))
                    V.tensor_tensor(heads(xdec[:]), heads(xdt[:]), dex[:, 0, :].unsqueeze(2)
                                    .broadcast_to([P, NH, HD]), ALU.mult).then_inc(xdec_ok, 1)
                    dve.wait_ge(yoff_done, b * NT + (cc + 1))
                    if cc == 0:
                        dve.wait_ge(eacs_ok, b + 1)
                    V.tensor_tensor(heads(y_sb[:, cc, :]), pair[1][:].rearrange("p g (h d) -> p (g h) d", d=HD),
                                    eacs_t[:, cc, :].unsqueeze(2).broadcast_to([P, NH, HD]), ALU.mult
                                    ).then_inc(yoff_used, 1)
                    dve.wait_ge(exp_ok, b * NT + (cc + 1))
                    dve.wait_ge(cbm_ok, b * NT + (cc + 1))
                    for g in range(2):
                        hs = slice(g * NH // 2, (g + 1) * NH // 2)
                        last = V.tensor_tensor(arow[:, hs, :], arow[:, hs, :], cbm[:, g, :].unsqueeze(1)
                                               .broadcast_to([P, NH // 2, P]), ALU.mult)
                    last.then_inc(att_ok, 1)
                    link(V.tensor_tensor(heads(xs[:]), heads(xs[:]), small[:, 1, :].unsqueeze(2)
                                         .broadcast_to([P, NH, HD]), ALU.mult))
                    dve.wait_ge(yoff_used, b * NT + (cc + 1))
                    link(V.tensor_tensor(y_sb[:, cc, :], y_sb[:, cc, :], xs[:], ALU.add))
                    dve.wait_ge(s_done, b * NT + (cc + 1))
                    link(V.tensor_tensor(heads(state[:]), heads(state[:]), dex[:, 1, :].unsqueeze(2)
                                         .broadcast_to([P, NH, HD]), ALU.mult))
                    V.tensor_tensor(state[:], state[:], pair[0][:].rearrange("p g n -> p (g n)"), ALU.add
                                    ).then_inc(state_ok, 1)
                    dve.wait_ge(yd_done, b * NT + (cc + 1))
                    V.tensor_tensor(y_sb[:, cc, :], y_sb[:, cc, :], pair[1][:].rearrange("p g n -> p (g n)"),
                                    ALU.add).then_inc(yd_used, 1)

                full(G_UV + 3, 3)
                for t in range(NT):
                    rms_stats(t, [v_sb[:, 0, t, :], v_sb[:, 1, t, :]])
                rms_rstd(NT)
                for t in range(NT):
                    V.tensor_scalar(v_sb[:, :, t, :], v_sb[:, :, t, :], rstd[:, t:t + 1], None, ALU.mult
                                    ).then_inc(v_ok, 1)
                dve.wait_ge(vg_in, b * 16 + 16)
                for t in range(NT):
                    dve.wait_ge(sv_done, b * NT + (t + 1))
                    V.tensor_tensor(sv_tmp[:, t % 2, :], pair[t % 2][:].rearrange("p g n -> p (g n)"), vg_bc[:],
                                    ALU.mult).then_inc(sv_used, 1)
                    dve.wait_ge(sv_used, b * NT + (t + 1))
                    for h in range(GH):
                        uu = u_sb[:, h // 4, t, (h % 4) * P:(h % 4 + 1) * P]
                        last = V.scalar_tensor_tensor(out=uu, in0=sv_tmp[:, t % 2, h * P:(h + 1) * P],
                                                      scalar=col_b[:, R_BS + h:R_BS + h + 1], in1=uu,
                                                      op0=ALU.add, op1=ALU.mult)
                    link(last)
                    rms_stats(t, [u_sb[:, 0, t, :], u_sb[:, 1, t, :]])
                rms_rstd(NT)
                for t in range(NT):
                    V.tensor_scalar(u_sb[:, :, t, :], u_sb[:, :, t, :], rstd[:, t:t + 1], None, ALU.mult
                                    ).then_inc(gm_ok, 1)

                def gate_y(j):
                    for t in range(NT):
                        full(G_Z + j, t)
                        yy = y_sb[:, t, j * W:(j + 1) * W]
                        V.tensor_tensor(yy, yy, stage[:, t, HALO:], ALU.mult).then_inc(stage_used, 1)

                dve.wait_ge(yd_used, b * NT + NT)
                gate_y(0)
                for k in range(KD):
                    dve.wait_ge(gm_hi_ok, b * KD + (k + 1))
                    V.scalar_tensor_tensor(out=gmT_lo[:, k, :], in0=aux[k % 4], scalar=col_a[:, R_GO + k:R_GO + k + 1],
                                           in1=gmT_hi[:, k, :].bitcast(F32), op0=ALU.mult, op1=ALU.subtract
                                           ).then_inc(gm_lo_ok, 1)
                gate_y(1)
                dve.wait_ge(stage_used, b * STAGED + (4 * (S_Z + 2) + 4))
                for j in range(2):
                    for t in range(NT):
                        rms_stats(j * NT + t, [y_sb[:, t, j * W:(j + 1) * W]])
                rms_rstd(8)
                for t in range(NT):
                    for j in range(2):
                        yy = y_sb[:, t, j * W:(j + 1) * W]
                        last = V.tensor_scalar(yy, yy, rstd[:, j * NT + t:j * NT + t + 1], None, ALU.mult)
                    last.then_inc(y_ok, 1)
                for k in range(KD):
                    dve.wait_ge(y_hi_ok, b * KD + (k + 1))
                    V.scalar_tensor_tensor(out=yT_lo[:, k, :], in0=aux[k % 4], scalar=col_a[:, R_SN + k:R_SN + k + 1],
                                           in1=yT_hi[:, k, :].bitcast(F32), op0=ALU.mult, op1=ALU.subtract
                                           ).then_inc(y_lo_ok, 1)

                def residual(G, j, tiles=range(NT)):
                    for t in tiles:
                        full(G, t)
                        link(V.tensor_tensor(stage[:, t, HALO:], stage[:, t, HALO:], g_bc[:, j * W:(j + 1) * W], ALU.mult))
                        V.tensor_tensor(x2[:, t, j * W:(j + 1) * W], x2[:, t, j * W:(j + 1) * W], stage[:, t, HALO:],
                                        ALU.add).then_inc(stage_used, 1)

                dve.wait_ge(x2_in, b * 32 + 32)
                residual(G_OUT, 0)
                dve.wait_ge(stage_used, b * STAGED + (4 * (S_OUT + 1) + 4))
                for t in range(NT):
                    V.bn_stats(stats2[:, t, 0, :], x2[:, t, 0:W])
                for t in range(NT):
                    residual(G_OUT + 1, 1, (t,))
                    dve.wait_ge(stage_used, b * STAGED + (4 * (S_OUT + 1) + t + 5))
                    link(V.bn_stats(stats2[:, t, 1, :], x2[:, t, W:D]))
                    link(V.bn_aggr(mv[:, t, :], stats2[:, t, :, :]))
                rms_rstd(NT, rstd_ok)
                dve.wait_ge(rstd_ok, b + 1)
                for t in range(2):
                    V.tensor_scalar(xn2[:, t, :], x2[:, t, :], rstd[:, t:t + 1], None, ALU.mult).then_inc(xn_ok, 1)
                h_lows(b * 2 + 1, range(KD), C_SC2, C_SH2)

                with dve.Fori(0, KF // 2) as j:
                    fresh()
                    for i in range(2):
                        m = j * 2 + i
                        dve.wait_ge(evacuated, b * (4 * GROUPS) + j * 4 + (4 * G_UP + i + 5))
                        conv(b * CONVS + j * 2 + (KX + i + 1), i, 3, halo_f[:, bass.ds(m, 1), :].squeeze(1),
                             lambda tap: col_b[:, bass.ds(m + (R_FW + tap * KF), 1)],
                             col_b[:, bass.ds(m + R_FB, 1)], i)
                        V.tensor_copy(halo_f[:, bass.ds(m, 1), :].squeeze(1), stage[:, i, W + 1:]).then_inc(stage_used, 1)
                    for i in range(2):
                        m = j * 2 + i
                        dve.wait_ge(evacuated, b * (4 * GROUPS) + j * 4 + (4 * G_UP + i + 7))
                        dve.wait_ge(silu_done, b * CONVS + j * 2 + (KX + i + 3))
                        val = stage[:, 2 + i, HALO:]
                        link(V.tensor_tensor(val, val, acc[:, i, :], ALU.mult))
                        link(V.tensor_copy(g_hi[:, bass.ds(m, 1), :].squeeze(1), val))
                        V.tensor_tensor(g_lo[:, bass.ds(m, 1), :].squeeze(1), val,
                                        g_hi[:, bass.ds(m, 1), :].squeeze(1).bitcast(F32), ALU.subtract
                                        ).then_inc(stage_used, 1)
                fresh()
                norm_x(b + 1)
                h_lows(b * 2 + 2, range(KD), C_SC1, C_SH1)
                dve.wait_ge(g2_in, b * 32 + 32)
                residual(G_DOWN, 0)
                residual(G_DOWN + 1, 1)
                dve.wait_ge(stage_used, b * STAGED + (4 * (S_DOWN + 2) + 4))
                for t in range(NT):
                    rms_stats(t, [x2[:, t, 0:W], x2[:, t, W:D]])
                rms_rstd(NT)
                for t in range(NT):
                    V.scalar_tensor_tensor(out=x2[:, t, :], in0=x2[:, t, :], scalar=rstd[:, t:t + 1], in1=fg_bc[:],
                                           op0=ALU.mult, op1=ALU.mult).then_inc(out_ok, 1)

        @block.tensor
        def _(pe):
            T = nc.tensor
            pe.wait_ge(const_ok, 4)
            pe.wait_ge(c_in, 16)
            T.transpose(aux[1][:, 0:KD], c_rows[:], ident[0:KD, 0:KD]).then_inc(c_tr, 1)
            pe.wait_ge(rows_in, 176)
            T.transpose(aux[0][:, 0:ROWS_A], rows_a[0:ROWS_A, :], ident[0:ROWS_A, 0:ROWS_A]).then_inc(col_tr, 1)
            T.transpose(aux[0][:, P:P + ROWS_B], rows_b[0:ROWS_B, :], ident[0:ROWS_B, 0:ROWS_B]).then_inc(col_tr, 1)
            pe.wait_ge(small_in, 80)
            for h in range(GH):
                last = T.transpose(aux[2 + h // 4][:, (h % 4) * P:(h % 4 + 1) * P], ws_raw[:, h, :], ident[:])
                if h % 4 == 3:
                    last.then_inc(ws_tr, 1)
            def h_transpose(q, ks, tiles):
                for k in ks:
                    if k >= 4:
                        pe.wait_ge(h_lo_ok, q * KD + (k - 3))
                    for t in range(NT):
                        last = T.transpose(aux[k % 4][:, t * P:(t + 1) * P], tiles[t][:, k * P:(k + 1) * P], ident[:])
                    last.then_inc(h_tr, 1)

            xn = [xn01[:, 0, :], xn01[:, 1, :], xn23[:, 0, :], xn23[:, 1, :]]
            def mod_column(n):
                ones = tri[:, P - 1:P]
                for m in range(2 * KD):
                    last = T.matmul(aux[0][:, m:m + 1], mod_sum[:, 2 * n + m // KD, (m % KD) * P:(m % KD + 1) * P], ones,
                                    start=True, stop=True)
                last.then_inc(mod_col, 1)

            pe.sem_inc(w_used, RING)
            pe.wait_ge(cact_ok, 1)
            pe.wait_ge(col_ok, 2)
            pe.wait_ge(ada_summed, KD)
            mod_column(0)
            for i in range(KD, 3 * KD):
                g, k = i // KD - 1, i % KD
                pe.wait_ge(ada_in[i % ADA_RING], 16 * (i // ADA_RING + 1))
                for m in range(2):
                    last = T.matmul(main[2 * g + m][0:1, :], c_act[:, k:k + 1],
                                    ada_t[:, i % ADA_RING, g * D + m * W:g * D + (m + 1) * W],
                                    start=k == 0, stop=k == KD - 1)
                last.then_inc(ada_gated, 1)
                if KD + 3 <= i < 2 * KD + 3:
                    if i == KD + 3:
                        pe.wait_ge(ready, 1)
                        pe.wait_ge(ws_ok, 2)
                        pe.wait_ge(xn_ok, NT)
                    h_transpose(0, (i - KD - 3,), xn)
            pe.wait_ge(h_lo_ok, KD)
            pe.wait_ge(ada_summed, 3 * KD)
            mod_column(1)
            pe.wait_ge(gate_ok, 4)

            def unit(n_at, n, G_at, first, last, mms):
                pe.wait_ge(w_lo_ok, n_at)
                for i in range(4):
                    if first:
                        pe.wait_ge(evacuated, G_at + (i + 1))
                    for p, (a, w) in enumerate(mms(i)):
                        ins = T.matmul(main[i][:], a, w, start=first and p == 0, stop=last and p == 2)
                    if last and i < 3:
                        ins.then_inc(bank_done, 1)
                ins.then_inc(w_used, 1)

            def tokens_out(hi, lo, k, s):
                return lambda i: ((hi[:, k, i * P:(i + 1) * P], w_hi[:, s, :]), (hi[:, k, i * P:(i + 1) * P], w_lo[:, s, :]),
                                  (lo[:, k, i * P:(i + 1) * P], w_hi[:, s, :]))

            def channels_out(k, s):
                return lambda i: ((w_hi[:, s, i * P:(i + 1) * P], h_hi[:, k, :]), (w_hi[:, s, i * P:(i + 1) * P], h_lo[:, k, :]),
                                  (w_lo[:, s, i * P:(i + 1) * P], h_hi[:, k, :]))

            with pe.Fori(0, NB) as b:
                def run(n, G, k, K, mms):
                    unit(b * UNITS + (n + 1 + RING), n, b * (4 * GROUPS) + 4 * G, k == 0, k == K - 1, mms)

                for j in range(3):
                    for k in range(KD):
                        run(j * KD + k, j, k, KD, channels_out(k, k % RING))
                        if j == 0 and k == 1:
                            for kk in range(KD):
                                for p, (w, a) in enumerate(((0, h_hi), (0, h_lo), (1, h_hi))):
                                    last = T.matmul(aux[3], wdt[:, (w * KD + kk) * NH:(w * KD + kk) * NH + P],
                                                    a[:, kk, :], start=kk == 0 and p == 0,
                                                    stop=kk == KD - 1 and p == 2)
                            last.then_inc(dt_mm, 1)
                        if j == 0 and k == 5:
                            pe.wait_ge(dtT_ok, b + 1)
                            pe.sem_inc(pe_past, 1)
                            for t in range(NT):
                                last = T.transpose(aux[3][:, t * NH:(t + 1) * NH], daT[:, t * P:(t + 1) * P],
                                                   ident[0:NH, 0:NH])
                            last.then_inc(dt_tr, 1)
                        if j == 1 and k == 1:
                            pe.wait_ge(da_ok, b + 1)
                            for t in range(NT):
                                last = T.transpose(aux[3][0:NH, t * P:(t + 1) * P], da_t[:, t, :], ident[:])
                            last.then_inc(da_tr, 1)
                        if j == 1 and k == 6:
                            pe.wait_ge(acs_ok, b + 1)
                            pe.sem_inc(pe_past, 1)
                            for t in range(NT):
                                last = T.transpose(aux[3][:, t * NH:(t + 1) * NH], acsT[:, t * P:(t + 1) * P],
                                                   ident[0:NH, 0:NH])
                            last.then_inc(acs_tr, 1)

                def chunk_scores(cc):
                    ts = slice(cc * P, (cc + 1) * P)
                    if cc == 0:
                        pe.wait_ge(silu_done, b * CONVS + (KX + 2))
                    else:
                        pe.wait_ge(state_ok, b * NT + cc)
                        pe.wait_ge(yd_used, b * NT + cc)
                    for k in range(KD):
                        T.transpose(aux[k // 4][:, (k % 4) * P:(k % 4 + 1) * P], xT[:, k, ts], ident[:])
                    for g in range(2):
                        T.transpose(aux[2][:, g * P:(g + 1) * P], bcT[:, g, ts], ident[:])
                    for g in range(2):
                        last = T.matmul(aux[2][:, (2 + g) * P:(3 + g) * P], bcT[:, g, ts], bcT[:, 2 + g, ts],
                                        start=True, stop=True)
                    last.then_inc(t_done, 1)

                def chunk_yoff(cc):
                    pe.wait_ge(xs_ok, b * (3 * NT) + 3 * (cc + 1))
                    pe.wait_ge(cbm_ok, b * NT + (cc + 1))
                    pe.wait_ge(acs_t_ok, b + 1)
                    if cc:
                        pe.wait_ge(state_ok, b * NT + cc)
                    for g in range(2):
                        last = T.matmul(aux[2 + g], bcT[:, 2 + g, cc * P:(cc + 1) * P], state[:, g * W:(g + 1) * W],
                                        start=True, stop=True)
                    last.then_inc(yoff_done, 1)

                def chunk_state(cc):
                    pe.wait_ge(xdec_ok, b * NT + (cc + 1))
                    for g in range(2):
                        last = T.matmul(aux[g], b_tok[:, g, :], xdec[:, g * W:(g + 1) * W], start=True, stop=True)
                    last.then_inc(s_done, 1)

                def chunk_ydiag(cc):
                    pe.wait_ge(att_ok, b * NT + (cc + 1))
                    pe.wait_ge(yoff_used, b * NT + (cc + 1))
                    for h in range(NH):
                        o = (h % (NH // 2)) * HD
                        last = T.matmul(aux[2 + h // (NH // 2)][:, o:o + HD], arow[:, h, :], xdt[:, h * HD:(h + 1) * HD],
                                        start=True, stop=True)
                    last.then_inc(yd_done, 1)

                for cc in range(NT):
                    for k in range(KD):
                        run(UV + cc * KD + k, G_UV + cc, k, KD, tokens_out(h_hi, h_lo, k, k % RING))
                        if k == 1 and cc:
                            chunk_ydiag(cc - 1)
                        if k == (4 if cc == 0 else 3):
                            chunk_scores(cc)
                        if k == 5:
                            chunk_yoff(cc)
                        if k == 7:
                            chunk_state(cc)

                def spatial(t):
                    pe.wait_ge(v_ok, b * NT + (t + 1))
                    if t < 2:
                        pe.wait_ge(state_ok, b * NT + NT)
                        pe.wait_ge(yd_used, b * NT + NT)
                    else:
                        pe.wait_ge(sv_used, b * NT + (t - 1))
                    for h in range(GH):
                        last = T.matmul(aux[2 * (t % 2) + h // 4][:, (h % 4) * P:(h % 4 + 1) * P], wsT[:, h, :],
                                        v_sb[:, h // 4, t, (h % 4) * P:(h % 4 + 1) * P], start=True, stop=True)
                    last.then_inc(sv_done, 1)

                def gm_transpose(ks):
                    for k in ks:
                        if k == 0:
                            pe.wait_ge(gm_ok, b * NT + NT)
                        if k >= 4:
                            pe.wait_ge(gm_lo_ok, b * KD + (k - 3))
                        for t in range(NT):
                            last = T.transpose(aux[k % 4][:, t * P:(t + 1) * P],
                                               u_sb[:, k // 4, t, (k % 4) * P:(k % 4 + 1) * P], ident[:])
                        last.then_inc(gm_tr, 1)

                def y_transpose(ks):
                    for k in ks:
                        if k == 0:
                            pe.wait_ge(y_ok, b * NT + NT)
                        if k >= 4:
                            pe.wait_ge(y_lo_ok, b * KD + (k - 3))
                        for t in range(NT):
                            last = T.transpose(aux[k % 4][:, t * P:(t + 1) * P], y_sb[:, t, k * P:(k + 1) * P], ident[:])
                        last.then_inc(y_tr, 1)

                for j in range(2):
                    for k in range(KD):
                        run(Z + j * KD + k, G_Z + j, k, KD, tokens_out(h_hi, h_lo, k, k % RING))
                        if j == 0 and k == 1:
                            chunk_ydiag(NT - 1)
                        if j == 0 and k == 5:
                            spatial(0)
                            spatial(1)
                        if j == 0 and k == 7:
                            spatial(2)
                        if j == 1 and k == 1:
                            spatial(3)
                        if j == 1 and k == 6:
                            gm_transpose(range(4))
                        if j == 1 and k == 7:
                            gm_transpose(range(4, KD))
                def out_ops(k):
                    ops = (gmT_hi, gmT_lo) if k < KD else (yT_hi, yT_lo)
                    return tokens_out(*ops, k % KD, k % RING)

                for j in range(2):
                    for k in range(2 * KD - (RING if j else 0)):
                        if j == 0 and k < KD:
                            pe.wait_ge(gm_lo_ok, b * KD + (k + 1))
                        if j == 0 and k >= KD:
                            pe.wait_ge(y_lo_ok, b * KD + (k - KD + 1))
                        run(OUT + j * 2 * KD + k, G_OUT + j, k, 2 * KD, out_ops(k))
                        if j == 0 and k == 6:
                            y_transpose(range(4))
                        if j == 0 and k == 7:
                            y_transpose(range(4, KD))
                for i in range(4):
                    for k in range(2 * KD - RING, 2 * KD):
                        if i == 0:
                            pe.wait_ge(w_lo_ok, b * UNITS + (UP - 2 * KD + k + 1 + RING))
                        for p, (a, w) in enumerate(out_ops(k)(i)):
                            ins = T.matmul(main[i][:], a, w, start=False, stop=k == 2 * KD - 1 and p == 2)
                        if i == 3:
                            ins.then_inc(w_used, 1)
                        elif k == 2 * KD - 1:
                            ins.then_inc(bank_done, 1)
                pe.wait_ge(xn_ok, b * (NT + 2) + (NT + 2))
                pe.wait_ge(xn_act_ok, b * 2 + 2)
                h_transpose(b * 2 + 1, range(KD), [xn2[:, t, :] for t in range(NT)])
                with pe.Fori(0, KF // 2) as j:
                    for k in range(KD):
                        pe.wait_ge(h_lo_ok, b * (2 * KD) + (KD + k + 1))
                        unit(b * UNITS + j * KD + (UP + k + 1 + RING), UP + k, b * (4 * GROUPS) + j * 4 + 4 * G_UP,
                             k == 0, k == KD - 1, channels_out(k, k % RING))
                for j in range(2):
                    for k in range(KF):
                        if j == 0:
                            if k == 0:
                                pe.wait_ge(stage_used, b * STAGED + (4 * S_DOWN))
                            if k >= KF - 2:
                                pe.wait_ge(stage_used, b * STAGED + (4 * S_DOWN + 4 - (KF - 1 - k)))
                        run(DOWN + j * KF + k, G_DOWN + j, k, KF, tokens_out(g_hi, g_lo, k, (j * KF + k) % RING))
                        if j == 0 and k == 13:
                            pe.wait_ge(xn_ok, b * (NT + 2) + (NT + 2 + NT))
                            h_transpose(b * 2 + 2, range(4), xn)
                        if j == 0 and k == 16:
                            h_transpose(b * 2 + 2, range(4, KD), xn)
                pe.wait_ge(h_lo_ok, b * (2 * KD) + 3 * KD)


_INS = ['x', 'c', 'ada_w', 'ada_b', 'norm1_g', 'norm2_g', 'w_in', 'ssd_conv_w', 'ssd_conv_b', 'ssd_dt_bias',
        'ssd_a_log', 'ssd_d', 'ssd_norm_g', 'gm_vnorm_g', 'gm_ws', 'gm_bs', 'gm_out_g', 'w_out', 'ff_up',
        'ff_conv_w', 'ff_conv_b', 'ff_down', 'final_g']


def kernel(**inputs):
    import numpy as _np
    import concourse.bacc as _bacc
    from concourse import mybir as _mybir
    from concourse.bass_utils import run_bass_kernel_spmd as _run

    nc = _bacc.Bacc("TRN2", target_bir_lowering=False, num_devices=1)
    arrays, args = {}, []
    for name in _INS:
        a = _np.ascontiguousarray(inputs[name])
        arrays[f"in_{name}_dram"] = a
        args.append(nc.dram_tensor(f"in_{name}_dram", a.shape, _mybir.dt.from_np(a.dtype), kind="ExternalInput").ap())
    out = nc.dram_tensor("out_dram", inputs["x"].shape, _mybir.dt.float32, kind="ExternalOutput").ap()
    hybrid_decoder_trunk(nc, *args, out)
    r = _run(nc, [arrays], core_ids=[0])
    return r.results[0]["out_dram"]
```

```python
import concourse.bass as bass
from concourse import mybir
from contextlib import ExitStack


def hybrid_decoder_trunk(nc, x, c, ada_w, ada_b, norm1_g, norm2_g, w_in, ssd_conv_w, ssd_conv_b, ssd_dt_bias,
                         ssd_a_log, ssd_d, ssd_norm_g, gm_vnorm_g, gm_ws, gm_bs, gm_out_g, w_out, ff_up,
                         ff_conv_w, ff_conv_b, ff_down, final_g, out):
    F32, F32R, I32 = mybir.dt.float32, mybir.dt.float32r, mybir.dt.int32
    ALU, ACT = mybir.AluOpType, mybir.ActivationFunctionType

    P, W = 128, 512
    _, SEQ, D = x.shape
    BT = W
    NB, NT = SEQ // BT, BT // P
    KD = D // P
    NH = ssd_d.shape[1]
    HD = D // NH
    CONV = ssd_conv_w.shape[2]
    NST = (CONV - D) // 4
    KX = CONV // P
    GH = gm_ws.shape[1]
    DFF = ff_down.shape[1]
    KF = DFF // P
    EPS = 1e-6
    COL_XBC, COL_DT, COL_U = D, D + CONV, D + CONV + NH
    MODS = ada_b.shape[1]
    assert NT == 4 and NST == P and GH == KD and P == gm_ws.shape[2]

    XBC, UV, Z, OUT, UP, DOWN = 0, 3 * KD, 7 * KD, 9 * KD, 9 * KD + 4 * KD, 13 * KD + (KF // 2) * KD
    UNITS = DOWN + 2 * KF
    G_UV, G_Z, G_OUT, G_UP, G_DOWN = 3, 7, 9, 11, 11 + KF // 2
    GROUPS = G_DOWN + 2
    S_Z, S_OUT, S_UP, S_DOWN = 3, 5, 7, 7 + KF // 2
    STAGED = 4 * (S_DOWN + 2)
    CONVS = KX + KF
    WARM = 22
    RING, LEAD, SP_LEAD = 4, 3, 4
    assert UNITS % RING == 0 and XBC % RING == UV % RING == Z % RING == OUT % RING == UP % RING == DOWN % RING == 0

    ctx = ExitStack()
    with ctx:
        place = [nc.sbuf_base + 31 & ~31]

        def fixed(name, shape, dt, at=None):
            n = 4
            for s in shape[1:]:
                n *= s
            if at is None:
                at = place[0]
                place[0] += n + 31 & ~31
            return nc.alloc_sbuf_tensor_at(name, shape, dt, offset=at), at

        w_raw, _ = fixed("w_raw", [P, RING, W], F32)
        w_hi, _ = fixed("w_hi", [P, RING, W], F32R)
        w_lo, _ = fixed("w_lo", [P, RING, W], F32R)
        x2, x2_at = fixed("x2", [P, NT, D], F32)
        h_hi, h_at = fixed("h_hi", [P, KD, BT], F32R)
        h_lo, _ = fixed("h_lo", [P, KD, BT], F32R)
        _, r_at = fixed("region", [P, 24, 1024], F32)
        KB = 1024
        xT, _ = fixed("xT", [P, KD, BT], F32, r_at)
        bcT, _ = fixed("bcT", [P, 4, BT], F32, r_at + 16 * KB)
        arow, _ = fixed("arow", [P, NH, P], F32, r_at + 24 * KB)
        gmT_hi, _ = fixed("gmT_hi", [P, KD, BT], F32R, r_at)
        gmT_lo, _ = fixed("gmT_lo", [P, KD, BT], F32R, r_at + 16 * KB)
        u_sb, _ = fixed("u_sb", [P, 2, NT, W], F32, r_at + 32 * KB)
        xn2, _ = fixed("xn2", [P, NT, D], F32, r_at + 32 * KB)
        v_sb, _ = fixed("v_sb", [P, 2, NT, W], F32, r_at + 48 * KB)
        yT_hi, _ = fixed("yT_hi", [P, KD, BT], F32R, r_at + 48 * KB)
        yT_lo, _ = fixed("yT_lo", [P, KD, BT], F32R, r_at + 64 * KB)
        xs, _ = fixed("xs", [P, D], F32, r_at + 64 * KB)
        xdt, _ = fixed("xdt", [P, D], F32, r_at + 68 * KB)
        xdec, _ = fixed("xdec", [P, D], F32, r_at + 72 * KB)
        sv_tmp, _ = fixed("sv_tmp", [P, 2, D], F32, r_at + 64 * KB)
        vg_bc, _ = fixed("vg_bc", [P, D], F32, r_at + 72 * KB)
        b_tok, _ = fixed("b_tok", [P, 2, P], F32, r_at + 76 * KB)
        cbm, _ = fixed("cbm", [P, 2, P], F32, r_at + 77 * KB)
        dl, _ = fixed("dl", [P, 2, NH], F32, r_at + 78 * KB)
        dex, _ = fixed("dex", [P, 2, NH], F32, r_at + 78 * KB + 512)
        y_sb, _ = fixed("y_sb", [P, NT, D], F32, r_at + 80 * KB)
        g_hi, _ = fixed("g_hi", [P, KF, BT], F32R, r_at)
        g_lo, _ = fixed("g_lo", [P, KF, BT], F32R, r_at + 2 * KF * KB)
        ADA_RING = 11
        ada_t, _ = fixed("ada_t", [P, ADA_RING, 2 * D], F32, r_at)
        gate_rows, _ = fixed("gate_rows", [1, 2 * D], F32, r_at + ADA_RING * 8 * KB)
        xn01, xn_at = fixed("xn01", [P, 2, D], F32)
        acsT, _ = fixed("acsT", [NH, BT], F32, xn_at)
        daT, _ = fixed("daT", [NH, BT], F32, xn_at + 2 * KB)
        dtT, _ = fixed("dtT", [2 * NH, BT], F32, xn_at + 2 * KB)
        dt_t, _ = fixed("dt_t", [P, NT, NH], F32, xn_at + 4 * KB)
        dt_b, _ = fixed("dt_b", [P, NT, NH], F32, xn_at + 4 * KB + 256)
        da_t, _ = fixed("da_t", [P, NT, NH], F32, xn_at + 4 * KB + 512)
        acs_t, _ = fixed("acs_t", [P, NT, NH], F32, xn_at + 4 * KB + 768)
        eacs_t, _ = fixed("eacs_t", [P, NT, NH], F32, xn_at + 5 * KB)
        dt_e, _ = fixed("dt_e", [P, NT, NH], F32, xn_at + 5 * KB + 256)
        dt_s, _ = fixed("dt_s", [P, NT, NH], F32, xn_at + 5 * KB + 512)
        dt_q, _ = fixed("dt_q", [P, NT, NH], F32, xn_at + 5 * KB + 768)
        dt_p, _ = fixed("dt_p", [P, NT, NH], F32, xn_at + 7 * KB)
        HALO, SW = 3, W + 3
        stage, s_at = fixed("stage", [P, 4, SW], F32)
        xn23, _ = fixed("xn23", [P, 2, D], F32, s_at)
        acc, _ = fixed("acc", [P, 2, W], F32)
        g_bc, g_at = fixed("g_bc", [P, D], F32)
        fg_bc, _ = fixed("fg_bc", [P, D], F32, r_at + 92 * KB)
        state, st_at = fixed("state", [P, D], F32)
        wsT, _ = fixed("wsT", [P, GH, P], F32)
        ident, _ = fixed("ident", [P, P], F32)
        tri, _ = fixed("tri", [P, P], F32)
        wdt, _ = fixed("wdt", [P, 2 * KD * NH + P - 2 * NH], F32R)
        wdt_parts = wdt[:, 0:2 * KD * NH].rearrange("p (k g n) -> p k g n", k=KD, g=2)
        R_CONVW, R_CONVB = 0, 4 * KX
        R_SN, R_GO, R_N1, R_N2 = 5 * KX, 5 * KX + KD, 5 * KX + 2 * KD, 5 * KX + 3 * KD
        ROWS_A = 5 * KX + 4 * KD
        R_FW, R_FB, R_BS, R_AB = 0, 3 * KF, 4 * KF, 4 * KF + GH
        ROWS_B = 4 * KF + GH + 4 * KD
        assert ROWS_A <= P and ROWS_B <= P
        col_a, _ = fixed("col_a", [P, ROWS_A], F32)
        col_b, _ = fixed("col_b", [P, ROWS_B], F32)
        C_SH1, C_SC1, C_SH2, C_SC2 = 0, KD, 2 * KD, 3 * KD
        mod_c, _ = fixed("mod_c", [P, 4 * KD], F32)
        halo_x, _ = fixed("halo_x", [P, KX, 3], F32)
        halo_f, _ = fixed("halo_f", [P, KF, 2], F32)
        small, _ = fixed("small", [P, 3, NH], F32)
        stats, _ = fixed("stats", [P, 2, 6], F32)
        stats2, _ = fixed("stats2", [P, NT, 2, 6], F32)
        mv, _ = fixed("mv", [P, 8, 2], F32)
        ms, _ = fixed("ms", [P, 8], F32)
        rt, _ = fixed("rt", [P, 8], F32)
        rstd, _ = fixed("rstd", [P, 8], F32)
        c_act, _ = fixed("c_act", [P, KD], F32)
        zeros, _ = fixed("zeros", [NH, P], F32, xn_at + 6 * KB)
        assert place[0] <= nc.sbuf_usable_end, (place[0], nc.sbuf_usable_end)
        rows_a, _ = fixed("rows_a", [P, P], F32, st_at)
        rows_b, _ = fixed("rows_b", [P, P], F32, st_at + 512)
        wdt_raw, _ = fixed("wdt_raw", [P, KD, NH], F32, st_at + KB)
        c_rows, _ = fixed("c_rows", [KD, P], F32, st_at + 1536)
        ws_raw, _ = fixed("ws_raw", [P, GH, P], F32, g_at)
        mod_sum, _ = fixed("mod_sum", [P, 4, D], F32, x2_at)
        assert MODS == 6 * D

        def bank(name):
            return ctx.enter_context(nc.psum_tensor(name, [P, W], F32))

        main = [bank(f"main{i}") for i in range(4)]
        pair = [ctx.enter_context(nc.psum_tensor(f"pair{i}", [P, 2, W], F32)) for i in range(2)]
        aux = [pair[i // 2][:, i % 2, :] for i in range(4)]

        gate_d = nc.dram_tensor("gate_scratch", [2, D], F32, kind="Internal").ap()
        acs_d = nc.dram_tensor("acs_scratch", [NB * NT, NH, P], F32, kind="Internal").ap()

        def sem(name):
            return ctx.enter_context(nc.semaphore(name))

        w_in_dma = [sem(f"w_loaded{i}") for i in range(RING)]
        w_hi_ok = sem("w_hi_ok")
        w_lo_ok = sem("w_lo_ok")
        w_used = sem("w_used")
        bank_done = sem("bank_done")
        evacuated = sem("evacuated")
        stage_used = sem("stage_used")
        conv_done = sem("conv_done")
        silu_done = sem("silu_done")
        x_in = sem("x_in")
        xn_ok = sem("xn_ok")
        rstd_ok, xn_act_ok = sem("rstd_ok"), sem("xn_act_ok")
        h_tr = sem("h_tr")
        h_hi_ok, h_lo_ok = sem("h_hi_ok"), sem("h_lo_ok")
        x2_in = sem("x2_in")
        g2_in = sem("g2_in")
        vg_in = sem("vg_in")
        dt_mm, dtT_ok, dt_tr, dt_biased, dt_soft = (sem(n) for n in ("dt_mm", "dtT_ok", "dt_tr", "dt_biased", "dt_soft"))
        da_ok, da_tr, acs_ok, acs_tr = sem("da_ok"), sem("da_tr"), sem("acs_ok"), sem("acs_tr")
        acs_t_ok, eacs_ok, acs_stored = sem("acs_t_ok"), sem("eacs_ok"), sem("acs_stored")
        arow_in = sem("arow_in")
        t_done = sem("t_done")
        xs_ok = sem("xs_ok")
        cbm_ok = sem("cbm_ok")
        dl_ok, seg_ok, dex_ok, exp_ok = sem("dl_ok"), sem("seg_ok"), sem("dex_ok"), sem("exp_ok")
        xdec_ok, att_ok = sem("xdec_ok"), sem("att_ok")
        yoff_done, yoff_used = sem("yoff_done"), sem("yoff_used")
        s_done, state_ok = sem("s_done"), sem("state_ok")
        yd_done, yd_used = sem("yd_done"), sem("yd_used")
        v_ok, sv_done, sv_used, gm_ok = sem("v_ok"), sem("sv_done"), sem("sv_used"), sem("gm_ok")
        gm_tr, gm_hi_ok, gm_lo_ok = sem("gm_tr"), sem("gm_hi_ok"), sem("gm_lo_ok")
        y_ok, y_tr, y_hi_ok, y_lo_ok = sem("y_ok"), sem("y_tr"), sem("y_hi_ok"), sem("y_lo_ok")
        out_ok, out_stored = sem("out_ok"), sem("out_stored")
        const_ok, rows_in, small_in, pro_dma = sem("const_ok"), sem("rows_in"), sem("small_in"), sem("pro_dma")
        ada_in = [sem(f"ada_in{i}") for i in range(ADA_RING)]
        ada_summed = sem("ada_summed")
        gate_mm = sem("gate_mm")
        gate_ok, gate_stored = sem("gate_ok"), sem("gate_stored")
        h_full_ok = sem("h_full_ok")
        c_in, c_tr, cact_ok = sem("c_in"), sem("c_tr"), sem("cact_ok")
        col_tr, col_ok, ws_tr, ws_ok, mod_col = (sem(n) for n in ("col_tr", "col_ok", "ws_tr", "ws_ok", "mod_col"))
        wdt_h, a_exp = sem("wdt_h"), sem("a_exp")
        ready = sem("ready")
        pe_past = sem("pe_past")
        dve_step = sem("dve_step")

        def slot_full(b, n):
            return b * (16 * UNITS // RING) + 16 * (n // RING + 1)

        block = ctx.enter_context(nc.Block())

        @block.sync
        def _(sp):
            xv = x[0].rearrange("(b t p) d -> b t p d", t=NT, p=P)

            def load_x(b, t):
                dst = xn01[:, t, :] if t < 2 else xn23[:, t - 2, :]
                sp.dma_start(dst, xv[bass.ds(b, 1), t, :, :].squeeze(0)).then_inc(x_in, 16)

            def rows(w, k):
                return w[0, k * P:(k + 1) * P, :]

            def load(b, n, src, dst_view=None):
                sp.wait_ge(w_lo_ok, b * UNITS + (n + 1))
                dst = w_raw[:, n % RING, :]
                sp.dma_start(dst if dst_view is None else dst_view(dst), src).then_inc(w_in_dma[n % RING], 16)

            def xbc_unit(b, n):
                j, k = n // KD, n % KD
                load(b, n, rows(w_in, k)[:, COL_XBC + j * W:COL_XBC + (j + 1) * W])

            sp.dma_start(c_rows[:], c[0].rearrange("(k p) -> k p", p=P)).then_inc(c_in, 16)
            for i in range(3 * KD):
                third, k = i // KD, i % KD
                if i == 5:
                    sp.wait_ge(rows_in, 176)
                if i >= ADA_RING:
                    sp.wait_ge(ada_summed, i - ADA_RING + 1)
                src = ada_w[0, k * P:(k + 1) * P, :].rearrange("p (m d) -> p m d", d=D)
                src = (src[:, 0:2, :], src[:, 3:5, :], src[:, 2::3, :])[third]
                sp.dma_start(ada_t[:, i % ADA_RING, :].rearrange("p (m d) -> p m d", d=D), src
                             ).then_inc(ada_in[i % ADA_RING], 16)
                if i == 2 * KD:
                    for n in range(SP_LEAD):
                        xbc_unit(0, n)
            sp.sem_inc(out_stored, 64)
            sp.wait_ge(gate_ok, 4)
            sp.dma_start(gate_d.rearrange("g d -> (g d)").unsqueeze(0), gate_rows[0:1, :]).then_inc(gate_stored, 16)
            def store(b):
                for t in range(NT):
                    sp.wait_ge(out_ok, b * NT + (t + 1))
                    sp.dma_start(out[0].rearrange("(b t p) d -> b t p d", t=NT, p=P)[bass.ds(b, 1), t, :, :].squeeze(0),
                                 x2[:, t, :]).then_inc(out_stored, 16)

            def block_loads(b, first):
                for n in range(SP_LEAD, 3 * KD):
                    xbc_unit(b, n)
                    if n == 11 and not first:
                        store(b - 1)
                    if n == 20:
                        sp.wait_ge(out_stored, b * 64 + 64)
                        sp.dma_start(x2[:], x[0].rearrange("(b t p) d -> b p t d", t=NT, p=P)[bass.ds(b, 1)]
                                     .squeeze(0)).then_inc(x2_in, 16)
                        sp.wait_ge(gate_stored, 16)
                        sp.dma_start(g_bc[:], gate_d[0:1, :].broadcast_to([P, D])
                                     ).then_inc(x2_in, 16)
                for cc in range(NT):
                    for k in range(KD):
                        n = UV + cc * KD + k
                        load(b, n, rows(w_in, k)[:, COL_U + cc * W:COL_U + (cc + 1) * W])
                        if k == 5:
                            if cc == 0:
                                sp.wait_ge(acs_stored, b * 16 + 16)
                            else:
                                sp.wait_ge(yd_done, b * NT + cc)
                            sp.dma_start(arow[:], acs_d[bass.ds(b * NT + cc, 1)].rearrange("o h l -> o (h l)")
                                         .broadcast_to([P, NH * P])).then_inc(arow_in, 16)
                for j in range(2):
                    for k in range(KD):
                        load(b, Z + j * KD + k, rows(w_in, k)[:, j * W:(j + 1) * W])
                        if j == 0 and k == 3:
                            sp.wait_ge(s_done, b * NT + NT)
                            sp.dma_start(vg_bc[:], gm_vnorm_g.broadcast_to([P, D])).then_inc(vg_in, 16)
                for j in range(2):
                    for k in range(2 * KD):
                        kk = (k + KD) % (2 * KD)
                        load(b, OUT + j * 2 * KD + k, rows(w_out, kk)[:, j * W:(j + 1) * W])
                with sp.Fori(0, KF // 2) as j:
                    for k in range(KD):
                        n = UP + k
                        sp.wait_ge(w_lo_ok, b * UNITS + j * KD + (n + 1))
                        src = rows(ff_up, k).rearrange("p (g n) -> p g n", g=2)[:, :, bass.ds(j * (2 * P), 2 * P)]
                        sp.dma_start(w_raw[:, n % RING, :].rearrange("p (g n) -> p g n", g=2), src
                                     ).then_inc(w_in_dma[n % RING], 16)
                nxt = (b + 1) % NB
                for j in range(2):
                    for k in range(KF):
                        load(b, DOWN + j * KF + k, rows(ff_down, k)[:, j * W:(j + 1) * W])
                        if j == 0 and k == 7:
                            sp.wait_ge(stage_used, b * STAGED + (4 * S_DOWN + 4))
                            sp.dma_start(g_bc[:], gate_d[1:2, :].broadcast_to([P, D])
                                         ).then_inc(g2_in, 16)
                            sp.dma_start(fg_bc[:], final_g.unsqueeze(0).broadcast_to([P, D])).then_inc(g2_in, 16)
                        if j == 0 and 8 <= k < 8 + NT:
                            load_x(nxt, k - 8)
                for n in range(SP_LEAD):
                    sp.wait_ge(w_lo_ok, b * UNITS + (UNITS + n + 1))
                    sp.dma_start(w_raw[:, n, :], rows(w_in, n)[:, COL_XBC:COL_XBC + W]).then_inc(w_in_dma[n], 16)

            block_loads(0, True)
            with sp.Fori(1, NB) as b:
                block_loads(b, False)
            store(NB - 1)
            sp.wait_ge(out_stored, 64 * (NB + 1))

        @block.gpsimd
        def _(pool):
            nc.gpsimd.memset(ident[:], 0.0).then_inc(const_ok, 1)
            nc.gpsimd.memset(tri[:], 1.0).then_inc(const_ok, 1)
            pool.wait_ge(const_ok, 2)
            nc.gpsimd.affine_select(out=ident[:], in_=ident[:], compare_op=ALU.not_equal, fill=1.0, base=0,
                                    pattern=[[-1, P]], channel_multiplier=1).then_inc(const_ok, 1)
            nc.gpsimd.affine_select(out=tri[:], in_=tri[:], compare_op=ALU.is_ge, fill=0.0, base=0,
                                    pattern=[[1, P]], channel_multiplier=-1).then_inc(const_ok, 1)
            pool.sem_inc(w_lo_ok, RING)
            for k in range(KD):
                pool.wait_ge(h_hi_ok, k + 1)
                pool.wait_ge(h_full_ok, k + 1)
                nc.gpsimd.tensor_tensor(h_lo[:, k, :], acc[:, k % 2, :], h_hi[:, k, :].bitcast(F32),
                                        ALU.subtract).then_inc(h_lo_ok, 1)
            with pool.Fori(0, NB * UNITS // RING) as q:
                for s in range(RING):
                    pool.wait_ge(w_hi_ok, q * RING + (s + 1))
                    pool.wait_ge(w_used, q * RING + (s + 1))
                    nc.gpsimd.tensor_tensor(w_lo[:, s, :], w_raw[:, s, :], w_hi[:, s, :].bitcast(F32),
                                            ALU.subtract).then_inc(w_lo_ok, 1)

        @block.scalar
        def _(act):
            act.wait_ge(c_tr, 1)
            nc.scalar.activation(c_act[:], aux[1][:, 0:KD], ACT.Silu).then_inc(cact_ok, 1)
            for r, n, src in ((R_CONVW, 4 * KX, ssd_conv_w[0].rearrange("k (j p) -> (k j) p", p=P)),
                              (R_CONVB, KX, ssd_conv_b[0].rearrange("(j p) -> j p", p=P)),
                              (R_SN, KD, ssd_norm_g[0].rearrange("(j p) -> j p", p=P)),
                              (R_GO, KD, gm_out_g[0].rearrange("(j p) -> j p", p=P)),
                              (R_N1, KD, norm1_g[0].rearrange("(j p) -> j p", p=P)),
                              (R_N2, KD, norm2_g[0].rearrange("(j p) -> j p", p=P))):
                act.dma_start(rows_a[r:r + n, :], src).then_inc(rows_in, 16)
            bias_rows = ada_b[0].rearrange("(h j p) -> h j p", h=2, p=P)
            for r, n, src in ((R_FW, 3 * KF, ff_conv_w[0].rearrange("k (j p) -> (k j) p", p=P)),
                              (R_FB, KF, ff_conv_b[0].rearrange("(j p) -> j p", p=P)), (R_BS, GH, gm_bs[0]),
                              (R_AB, 2 * KD, bias_rows[0, 0:2 * KD, :]), (R_AB + 2 * KD, 2 * KD, bias_rows[1, 0:2 * KD, :])):
                act.dma_start(rows_b[r:r + n, :], src).then_inc(rows_in, 16)
            for t in range(NT):
                act.dma_start(xn01[:, t, :] if t < 2 else xn23[:, t - 2, :], x[0, t * P:(t + 1) * P, :]).then_inc(x_in, 16)
            act.dma_start(ws_raw[:], gm_ws[0].rearrange("h t s -> t h s")).then_inc(small_in, 16)
            act.dma_start(wdt_raw[:], w_in[0, :, COL_DT:COL_U].rearrange("(k p) n -> p k n", p=P)).then_inc(small_in, 16)
            for n, src in enumerate((ssd_a_log, ssd_d, ssd_dt_bias)):
                act.dma_start(small[:, n, :], src.broadcast_to([P, NH])).then_inc(small_in, 16)
            for g in range(2):
                act.dma_start(gate_rows[0:1, g * D:(g + 1) * D], ada_b[:, (2 + 3 * g) * D:(3 + 3 * g) * D]
                              ).then_inc(pro_dma, 16)
            act.wait_ge(col_tr, 2)
            nc.scalar.activation(col_a[:], aux[0][:, 0:ROWS_A], ACT.Copy).then_inc(col_ok, 1)
            nc.scalar.activation(col_b[:], aux[0][:, P:P + ROWS_B], ACT.Copy).then_inc(col_ok, 1)
            act.wait_ge(small_in, 80)
            nc.scalar.activation(small[:, 0, :], small[:, 0, :], ACT.Exp).then_inc(a_exp, 1)
            nc.scalar.activation(wdt_parts[:, :, 0, :], wdt_raw[:], ACT.Copy).then_inc(wdt_h, 1)
            act.sem_inc(silu_done, 2)

            def split(b, n):
                act.wait_ge(w_in_dma[n % RING], slot_full(b, n))
                act.wait_ge(w_used, b * UNITS + (n + 1))
                nc.scalar.activation(w_hi[:, n % RING, :], w_raw[:, n % RING, :], ACT.Copy).then_inc(w_hi_ok, 1)

            def bank_ready(b, G, last, i):
                if i < 3:
                    act.wait_ge(bank_done, b * (3 * GROUPS) + (3 * G + i + 1))
                else:
                    act.wait_ge(w_used, b * UNITS + (last + 1 + RING))

            def evac_to_stage(b, G, S, last, func, banks=range(4)):
                for i in banks:
                    bank_ready(b, G, last, i)
                    act.wait_ge(stage_used, b * STAGED + (4 * S + i + 1))
                    nc.scalar.activation(stage[:, i, HALO:], main[i][:], func).then_inc(evacuated, 1)

            def silu_tile(b, cv, src, dst):
                act.wait_ge(conv_done, b * CONVS + (cv + 1))
                nc.scalar.activation(dst, src, ACT.Silu).then_inc(silu_done, 1)

            def h_tiles(q, ks, col_scale, col_bias):
                for k in ks:
                    act.wait_ge(h_tr, q * KD + (k + 1))
                    nc.scalar.activation(h_hi[:, k, :], aux[k % 4], ACT.Identity, bias=mod_c[:, col_bias + k:col_bias + k + 1],
                                         scale=mod_c[:, col_scale + k:col_scale + k + 1]).then_inc(h_hi_ok, 1)

            act.wait_ge(ready, 1)
            for k in range(KD):
                h_tiles(0, (k,), C_SC1, C_SH1)
                if k >= 2:
                    act.wait_ge(h_lo_ok, k - 1)
                nc.scalar.activation(acc[:, k % 2, :], aux[k % 4], ACT.Identity, bias=mod_c[:, C_SH1 + k:C_SH1 + k + 1],
                                     scale=mod_c[:, C_SC1 + k:C_SC1 + k + 1]).then_inc(h_full_ok, 1)
            for n in range(LEAD):
                split(0, n)
            act.wait_ge(ready, 2)
            for m in range(4):
                act.wait_ge(gate_ok, m + 1)
                act.sem_inc(evacuated, 1)
            with act.Fori(0, NB) as b:
                at = LEAD
                for j in range(3):
                    for n in range(at, (j + 1) * KD + LEAD):
                        split(b, n)
                        if j == 0 and n == 9:
                            act.wait_ge(dt_biased, b + 1)
                            nc.scalar.activation(dt_e[:], dt_e[:], ACT.Exp, scale=-1.0).then_inc(dt_soft, 1)
                        if j == 2 and n == 2 * KD + 7:
                            act.wait_ge(acs_ok, b + 1)
                            act.dma_start(acs_d[bass.ds(b * NT, NT)].rearrange("c h l -> h c l"),
                                          acsT[:].rearrange("h (c l) -> h c l", l=P)).then_inc(acs_stored, 16)
                            act.wait_ge(acs_t_ok, b + 1)
                            nc.scalar.activation(eacs_t[:], acs_t[:], ACT.Exp).then_inc(eacs_ok, 1)
                    evac_to_stage(b, j, j, (j + 1) * KD - 1, ACT.Copy)
                    for i in range(4):
                        kx = 4 * j + i
                        silu_tile(b, kx, acc[:, kx % 2, :], xT[:, kx, :] if kx < KD else bcT[:, kx - KD, :])
                        split(b, (j + 1) * KD + LEAD + i)
                    at = (j + 1) * KD + LEAD + 4
                for cc in range(NT):
                    n0, n1 = UV + cc * KD, UV + (cc + 1) * KD
                    at = max(at, n0 + LEAD)
                    for n in range(at, n1 + LEAD):
                        split(b, n)
                        if n == n0 + (8 if cc == 0 else 7):
                            act.wait_ge(t_done, b * NT + (cc + 1))
                            for h in range(2):
                                nc.scalar.activation(xs[:, h * W:(h + 1) * W], aux[h], ACT.Copy).then_inc(xs_ok, 1)
                            nc.scalar.activation(b_tok[:], aux[2][:, 0:2 * P].rearrange("p (g n) -> p g n", g=2),
                                                 ACT.Copy).then_inc(xs_ok, 1)
                        if n == n0 + (9 if cc == 0 else 8):
                            act.wait_ge(dl_ok, b * NT + (cc + 1))
                            nc.scalar.activation(dex[:], dl[:], ACT.Exp).then_inc(dex_ok, 1)
                            act.wait_ge(seg_ok, b * NT + (cc + 1))
                            nc.scalar.activation(arow[:], arow[:], ACT.Exp).then_inc(exp_ok, 1)
                    for i in range(4):
                        bank_ready(b, G_UV + cc, n1 - 1, i)
                        dst = (u_sb if cc < 2 else v_sb)[:, cc % 2, i, :]
                        nc.scalar.activation(dst, main[i][:], ACT.Gelu).then_inc(evacuated, 1)
                for j in range(2):
                    for n in range(Z + j * KD + LEAD, Z + (j + 1) * KD + LEAD):
                        split(b, n)
                        if j == 1 and n in (OUT + LEAD - 2, OUT + LEAD - 1):
                            for k in range(4) if n == OUT + LEAD - 2 else range(4, KD):
                                act.wait_ge(gm_tr, b * KD + (k + 1))
                                nc.scalar.activation(gmT_hi[:, k, :], aux[k % 4], ACT.Copy,
                                                     scale=col_a[:, R_GO + k:R_GO + k + 1]).then_inc(gm_hi_ok, 1)
                    evac_to_stage(b, G_Z + j, S_Z + j, Z + (j + 1) * KD - 1, ACT.Silu)
                for j in range(2):
                    n0 = OUT + 2 * j * KD
                    for n in range(n0 + LEAD, n0 + 2 * KD + (0 if j else LEAD)):
                        split(b, n)
                        if j == 0 and n in (n0 + LEAD + 6, n0 + LEAD + 7):
                            for k in range(4) if n == n0 + LEAD + 6 else range(4, KD):
                                act.wait_ge(y_tr, b * KD + (k + 1))
                                nc.scalar.activation(yT_hi[:, k, :], aux[k % 4], ACT.Copy,
                                                     scale=col_a[:, R_SN + k:R_SN + k + 1]).then_inc(y_hi_ok, 1)
                    if j == 0:
                        evac_to_stage(b, G_OUT, S_OUT, n0 + 2 * KD - 1, ACT.Copy)
                for n in range(UP, UP + LEAD):
                    split(b, n)
                act.wait_ge(rstd_ok, b + 1)
                for c in (slice(0, W), slice(W, D)):
                    nc.scalar.activation(xn2[:, NT - 1, c], x2[:, NT - 1, c], ACT.Copy, scale=rstd[:, NT - 1:NT]
                                         ).then_inc(xn_act_ok, 1)
                h_tiles(b * 2 + 1, range(4), C_SC2, C_SH2)
                split(b, UP + LEAD)
                h_tiles(b * 2 + 1, range(4, KD), C_SC2, C_SH2)
                with act.Fori(0, KF // 2) as j:
                    def split_up(n):
                        act.wait_ge(w_in_dma[n % RING], b * (16 * UNITS // RING) + j * (16 * KD // RING) + 16 * (n // RING + 1))
                        act.wait_ge(w_used, b * UNITS + j * KD + (n + 1))
                        nc.scalar.activation(w_hi[:, n % RING, :], w_raw[:, n % RING, :], ACT.Copy).then_inc(w_hi_ok, 1)

                    for n in range(UP + LEAD + 1, UP + LEAD + KD):
                        split_up(n)
                    for i in range(4):
                        if i < 3:
                            act.wait_ge(bank_done, b * (3 * GROUPS) + j * 3 + (3 * G_UP + i + 1))
                        else:
                            act.wait_ge(w_used, b * UNITS + j * KD + (UP + KD + RING))
                        act.wait_ge(stage_used, b * STAGED + j * 4 + (4 * S_UP + i + 1))
                        nc.scalar.activation(stage[:, i, HALO:], main[i][:], ACT.Copy).then_inc(evacuated, 1)
                    split_up(UP + LEAD + KD)
                    for i in range(2):
                        act.wait_ge(conv_done, b * CONVS + j * 2 + (KX + i + 1))
                        nc.scalar.activation(acc[:, i, :], acc[:, i, :], ACT.Silu).then_inc(silu_done, 1)
                for j in range(2):
                    n0 = DOWN + j * KF
                    for n in range(n0 + LEAD + (1 - j), n0 + KF + (0 if j else LEAD)):
                        split(b, n)
                        if j == 0 and n == n0 + 15 + LEAD:
                            h_tiles(b * 2 + 2, range(4), C_SC1, C_SH1)
                        if j == 0 and n == n0 + 18 + LEAD:
                            h_tiles(b * 2 + 2, range(4, KD), C_SC1, C_SH1)
                    if j == 0:
                        evac_to_stage(b, G_DOWN, S_DOWN, n0 + KF - 1, ACT.Copy)
                for n in range(UNITS, UNITS + LEAD):
                    split(b, n)

        @block.vector
        def _(dve):
            steps = [0]

            def link(ins):
                steps[0] += 1
                ins.then_inc(dve_step, 1)
                dve.wait_ge(dve_step, steps[0])

            def fresh():
                dve.sem_clear(dve_step)
                steps[0] = 0

            V = nc.vector

            def rms_stats(i, parts):
                for s, part in enumerate(parts):
                    last = V.bn_stats(stats[:, s, :], part)
                link(last)
                link(V.bn_aggr(mv[:, i, :], stats[:, 0:len(parts), :]))

            def rms_rstd(n, done=None):
                link(V.tensor_tensor(ms[:, 0:n], mv[:, 0:n, 0], mv[:, 0:n, 0], ALU.mult))
                link(V.scalar_tensor_tensor(out=ms[:, 0:n], in0=ms[:, 0:n], scalar=EPS, in1=mv[:, 0:n, 1],
                                            op0=ALU.add, op1=ALU.add))
                link(V.tensor_scalar(rstd[:, 0:n].bitcast(I32), ms[:, 0:n].bitcast(I32), -0.5, float(0x5F3759DF),
                                     ALU.mult, ALU.add))
                for it in range(3):
                    link(V.tensor_tensor(rt[:, 0:n], rstd[:, 0:n], rstd[:, 0:n], ALU.mult))
                    link(V.scalar_tensor_tensor(out=rt[:, 0:n], in0=rt[:, 0:n], scalar=-0.5, in1=ms[:, 0:n],
                                                op0=ALU.mult, op1=ALU.mult))
                    ins = V.scalar_tensor_tensor(out=rstd[:, 0:n], in0=rt[:, 0:n], scalar=1.5, in1=rstd[:, 0:n],
                                                 op0=ALU.add, op1=ALU.mult)
                    if it == 2 and done is not None:
                        ins.then_inc(done, 1)
                    else:
                        link(ins)

            def h_lows(q, ks, col_scale, col_bias):
                for k in ks:
                    dve.wait_ge(h_hi_ok, q * KD + (k + 1))
                    link(V.tensor_scalar(acc[:, k % 2, :], aux[k % 4], mod_c[:, col_scale + k:col_scale + k + 1],
                                         mod_c[:, col_bias + k:col_bias + k + 1], ALU.mult, ALU.add))
                    V.tensor_tensor(h_lo[:, k, :], acc[:, k % 2, :], h_hi[:, k, :].bitcast(F32),
                                    ALU.subtract).then_inc(h_lo_ok, 1)

            def norm_x(p):
                tiles = [xn01[:, 0, :], xn01[:, 1, :], xn23[:, 0, :], xn23[:, 1, :]]
                dve.wait_ge(x_in, p * (16 * NT) + 16 * NT)
                for t in range(NT):
                    rms_stats(t, [tiles[t][:, 0:W], tiles[t][:, W:D]])
                rms_rstd(NT)
                for t in range(NT):
                    V.tensor_scalar(tiles[t], tiles[t], rstd[:, t:t + 1], None, ALU.mult).then_inc(xn_ok, 1)

            def ada_sum(i):
                third, k = i // KD, i % KD
                piece = ada_t[:, i % ADA_RING, :]
                cols = slice(D, 2 * D) if third == 2 else slice(0, 2 * D)
                dst = (mod_sum[:, 0:2, :].rearrange("p m d -> p (m d)"), mod_sum[:, 2:4, :].rearrange("p m d -> p (m d)"),
                       mod_sum[:, 0, :])[third]
                dve.wait_ge(ada_in[i % ADA_RING], 16 * (i // ADA_RING + 1))
                if k:
                    dve.wait_ge(ada_summed, i)
                    V.scalar_tensor_tensor(out=dst, in0=piece[:, cols], scalar=c_act[:, k:k + 1], in1=dst,
                                           op0=ALU.mult, op1=ALU.add).then_inc(ada_summed, 1)
                else:
                    V.tensor_scalar(dst, piece[:, cols], c_act[:, k:k + 1], None, ALU.mult).then_inc(ada_summed, 1)

            def mod_columns(n, gain_at):
                dve.wait_ge(mod_col, n + 1)
                cols = mod_c[:, 2 * n * KD:(2 * n + 2) * KD]
                link(V.tensor_tensor(cols, aux[0][:, 0:2 * KD], col_b[:, R_AB + 2 * n * KD:R_AB + (2 * n + 2) * KD], ALU.add))
                V.scalar_tensor_tensor(out=cols[:, KD:], in0=cols[:, KD:], scalar=1.0, in1=col_a[:, gain_at:gain_at + KD],
                                       op0=ALU.add, op1=ALU.mult).then_inc(ready, 1)
                dve.wait_ge(ready, n + 1)

            V.memset(halo_x[:], 0.0)
            V.memset(halo_f[:], 0.0)
            dve.wait_ge(cact_ok, 1)
            for i in range(KD):
                ada_sum(i)
            for g in range(2):
                dve.wait_ge(ws_tr, g + 1)
                V.tensor_tensor(wsT[:, 4 * g:4 * g + 4, :], aux[2 + g].rearrange("p (h n) -> p h n", h=4),
                                tri[:].unsqueeze(1).broadcast_to([P, 4, P]), ALU.mult).then_inc(ws_ok, 1)
            dve.wait_ge(wdt_h, 1)
            V.memset(wdt[:, 2 * KD * NH:].bitcast(F32), 0.0)
            link(V.tensor_tensor(wdt_parts[:, :, 1, :], wdt_raw[:], wdt_parts[:, :, 0, :].bitcast(F32), ALU.subtract))
            V.memset(state[:], 0.0)
            dve.wait_ge(a_exp, 1)
            link(V.tensor_scalar(small[:, 0, :], small[:, 0, :], -1.0, None, ALU.mult))
            norm_x(0)
            dve.wait_ge(col_ok, 2)
            mod_columns(0, R_N1)
            for i in range(KD, 3 * KD):
                ada_sum(i)
                if i == 2 * KD + 5:
                    mod_columns(1, R_N2)
            dve.wait_ge(pro_dma, 32)
            for m in range(4):
                dve.wait_ge(gate_mm, m + 1)
                row = gate_rows[0:1, m * W:(m + 1) * W]
                V.tensor_tensor(row, main[m][0:1, :], row, ALU.add).then_inc(gate_ok, 1)
            dve.sem_inc(stage_used, 4)

            with dve.Fori(0, NB) as b:
                fresh()
                dve.wait_ge(dt_mm, b + 1)
                V.tensor_copy(dtT[:], aux[3][0:2 * NH, :]).then_inc(dtT_ok, 1)
                dve.wait_ge(dt_tr, b + 1)
                dt_parts = aux[3][:, 0:2 * NT * NH].rearrange("p (t g h) -> p t g h", g=2, h=NH)
                link(V.tensor_tensor(dt_b[:], dt_parts[:, :, 0, :],
                                     small[:, 2, :].unsqueeze(1).broadcast_to([P, NT, NH]), ALU.add))
                link(V.tensor_tensor(dt_b[:], dt_b[:], dt_parts[:, :, 1, :], ALU.add))
                V.scalar_tensor_tensor(out=dt_e[:], in0=dt_b[:], scalar=-1.0, in1=dt_b[:], op0=ALU.mult, op1=ALU.max
                                       ).then_inc(dt_biased, 1)
                dve.wait_ge(dt_soft, b + 1)
                link(V.tensor_scalar(dt_s[:], dt_e[:], 2.0, None, ALU.add))
                link(V.reciprocal(dt_s[:], dt_s[:]))
                link(V.tensor_tensor(dt_s[:], dt_s[:], dt_e[:], ALU.mult))
                link(V.tensor_tensor(dt_q[:], dt_s[:], dt_s[:], ALU.mult))
                link(V.tensor_scalar(dt_p[:], dt_q[:], 1.0 / 19.0, None, ALU.mult))
                for n in range(17, 1, -2):
                    link(V.scalar_tensor_tensor(out=dt_p[:], in0=dt_p[:], scalar=1.0 / n, in1=dt_q[:],
                                                op0=ALU.add, op1=ALU.mult))
                link(V.scalar_tensor_tensor(out=dt_p[:], in0=dt_p[:], scalar=1.0, in1=dt_s[:],
                                            op0=ALU.add, op1=ALU.mult))
                link(V.tensor_scalar(dt_b[:], dt_b[:], 0.0, None, ALU.max))
                link(V.scalar_tensor_tensor(out=dt_t[:], in0=dt_p[:], scalar=2.0, in1=dt_b[:],
                                            op0=ALU.mult, op1=ALU.add))
                V.tensor_tensor(da_t[:], dt_t[:], small[:, 0, :].unsqueeze(1).broadcast_to([P, NT, NH]),
                                ALU.mult).then_inc(da_ok, 1)

                def conv(cv, i, taps, halo, wcol, bcol, a):
                    K = taps
                    link(V.tensor_copy(stage[:, i, HALO - (K - 1):HALO], halo))
                    dve.wait_ge(silu_done, cv)
                    link(V.tensor_scalar(acc[:, a, :], stage[:, i, HALO:], wcol(K - 1), bcol, ALU.mult, ALU.add))
                    for tap in range(K - 1):
                        lo = HALO - (K - 1) + tap
                        ins = V.scalar_tensor_tensor(out=acc[:, a, :], in0=stage[:, i, lo:lo + W], scalar=wcol(tap),
                                                     in1=acc[:, a, :], op0=ALU.mult, op1=ALU.add)
                        if tap < K - 2:
                            link(ins)
                        else:
                            ins.then_inc(conv_done, 1)

                def full(G, i):
                    dve.wait_ge(evacuated, b * (4 * GROUPS) + (4 * G + i + 5))

                for j in range(3):
                    for i in range(4):
                        kx = 4 * j + i
                        full(j, i)
                        conv(b * CONVS + (kx + 1), i, 4, halo_x[:, kx, :],
                             lambda tap: col_a[:, R_CONVW + tap * KX + kx:R_CONVW + tap * KX + kx + 1],
                             col_a[:, R_CONVB + kx:R_CONVB + kx + 1], kx % 2)
                        V.tensor_copy(halo_x[:, kx, :], stage[:, i, W:]).then_inc(stage_used, 1)
                    if j == 0:
                        dve.wait_ge(da_tr, b + 1)
                        V.memset(zeros[:], 0.0)
                        link(V.tensor_copy(daT[:], aux[3][0:NH, :]))
                        for t in range(NT):
                            s = slice(t * P, (t + 1) * P)
                            last = V.tensor_tensor_scan(acsT[:, s], daT[:, s], zeros[:], 0.0,
                                                        ALU.add, ALU.add)
                        last.then_inc(acs_ok, 1)
                        dve.wait_ge(acs_tr, b + 1)
                        V.tensor_copy(acs_t[:], aux[3][:, 0:NT * NH].rearrange("p (t h) -> p t h", h=NH)
                                      ).then_inc(acs_t_ok, 1)

                def heads(ap):
                    return ap.rearrange("p (h d) -> p h d", h=NH)

                for cc in range(NT):
                    dve.wait_ge(arow_in, b * (16 * NT) + 16 * (cc + 1))
                    if cc == 0:
                        dve.wait_ge(acs_t_ok, b + 1)
                    V.tensor_tensor(dl[:, 0, :], arow[:, :, P - 1], acs_t[:, cc, :], ALU.subtract)
                    V.tensor_copy(dl[:, 1, :], arow[:, :, P - 1]).then_inc(dl_ok, 1)
                    dve.wait_ge(dl_ok, b * NT + (cc + 1))
                    for h in range(NH):
                        last = V.tensor_scalar(arow[:, h, :], arow[:, h, :], acs_t[:, cc, h:h + 1], 0.0,
                                               ALU.subtract, ALU.min)
                    last.then_inc(seg_ok, 1)
                    dve.wait_ge(xs_ok, b * (3 * NT) + 3 * (cc + 1))
                    V.tensor_tensor(cbm[:], aux[2][:, 2 * P:4 * P].rearrange("p (g n) -> p g n", g=2),
                                    tri[:].unsqueeze(1).broadcast_to([P, 2, P]), ALU.mult).then_inc(cbm_ok, 1)
                    link(V.tensor_tensor(heads(xdt[:]), heads(xs[:]), dt_t[:, cc, :].unsqueeze(2)
                                         .broadcast_to([P, NH, HD]), ALU.mult))
                    dve.wait_ge(dex_ok, b * NT + (cc + 1))
                    V.tensor_tensor(heads(xdec[:]), heads(xdt[:]), dex[:, 0, :].unsqueeze(2)
                                    .broadcast_to([P, NH, HD]), ALU.mult).then_inc(xdec_ok, 1)
                    dve.wait_ge(yoff_done, b * NT + (cc + 1))
                    if cc == 0:
                        dve.wait_ge(eacs_ok, b + 1)
                    V.tensor_tensor(heads(y_sb[:, cc, :]), pair[1][:].rearrange("p g (h d) -> p (g h) d", d=HD),
                                    eacs_t[:, cc, :].unsqueeze(2).broadcast_to([P, NH, HD]), ALU.mult
                                    ).then_inc(yoff_used, 1)
                    dve.wait_ge(exp_ok, b * NT + (cc + 1))
                    dve.wait_ge(cbm_ok, b * NT + (cc + 1))
                    for g in range(2):
                        hs = slice(g * NH // 2, (g + 1) * NH // 2)
                        last = V.tensor_tensor(arow[:, hs, :], arow[:, hs, :], cbm[:, g, :].unsqueeze(1)
                                               .broadcast_to([P, NH // 2, P]), ALU.mult)
                    last.then_inc(att_ok, 1)
                    link(V.tensor_tensor(heads(xs[:]), heads(xs[:]), small[:, 1, :].unsqueeze(2)
                                         .broadcast_to([P, NH, HD]), ALU.mult))
                    dve.wait_ge(yoff_used, b * NT + (cc + 1))
                    link(V.tensor_tensor(y_sb[:, cc, :], y_sb[:, cc, :], xs[:], ALU.add))
                    dve.wait_ge(s_done, b * NT + (cc + 1))
                    link(V.tensor_tensor(heads(state[:]), heads(state[:]), dex[:, 1, :].unsqueeze(2)
                                         .broadcast_to([P, NH, HD]), ALU.mult))
                    V.tensor_tensor(state[:], state[:], pair[0][:].rearrange("p g n -> p (g n)"), ALU.add
                                    ).then_inc(state_ok, 1)
                    if cc == NT - 1:
                        full(G_UV + 3, 3)
                        for t in range(NT):
                            rms_stats(t, [v_sb[:, 0, t, :], v_sb[:, 1, t, :]])
                    dve.wait_ge(yd_done, b * NT + (cc + 1))
                    V.tensor_tensor(y_sb[:, cc, :], y_sb[:, cc, :], pair[1][:].rearrange("p g n -> p (g n)"),
                                    ALU.add).then_inc(yd_used, 1)

                rms_rstd(NT)
                for t in range(NT):
                    V.tensor_scalar(v_sb[:, :, t, :], v_sb[:, :, t, :], rstd[:, t:t + 1], None, ALU.mult
                                    ).then_inc(v_ok, 1)
                dve.wait_ge(vg_in, b * 16 + 16)
                for t in range(NT):
                    dve.wait_ge(sv_done, b * NT + (t + 1))
                    V.tensor_tensor(sv_tmp[:, t % 2, :], pair[t % 2][:].rearrange("p g n -> p (g n)"), vg_bc[:],
                                    ALU.mult).then_inc(sv_used, 1)
                    dve.wait_ge(sv_used, b * NT + (t + 1))
                    for h in range(GH):
                        uu = u_sb[:, h // 4, t, (h % 4) * P:(h % 4 + 1) * P]
                        last = V.scalar_tensor_tensor(out=uu, in0=sv_tmp[:, t % 2, h * P:(h + 1) * P],
                                                      scalar=col_b[:, R_BS + h:R_BS + h + 1], in1=uu,
                                                      op0=ALU.add, op1=ALU.mult)
                    link(last)
                    rms_stats(t, [u_sb[:, 0, t, :], u_sb[:, 1, t, :]])
                rms_rstd(NT)
                for t in range(NT):
                    V.tensor_scalar(u_sb[:, :, t, :], u_sb[:, :, t, :], rstd[:, t:t + 1], None, ALU.mult
                                    ).then_inc(gm_ok, 1)

                def gate_y(j):
                    for t in range(NT):
                        full(G_Z + j, t)
                        yy = y_sb[:, t, j * W:(j + 1) * W]
                        V.tensor_tensor(yy, yy, stage[:, t, HALO:], ALU.mult).then_inc(stage_used, 1)

                dve.wait_ge(yd_used, b * NT + NT)
                for k in range(KD):
                    if k == 4:
                        gate_y(0)
                    dve.wait_ge(gm_hi_ok, b * KD + (k + 1))
                    V.scalar_tensor_tensor(out=gmT_lo[:, k, :], in0=aux[k % 4], scalar=col_a[:, R_GO + k:R_GO + k + 1],
                                           in1=gmT_hi[:, k, :].bitcast(F32), op0=ALU.mult, op1=ALU.subtract
                                           ).then_inc(gm_lo_ok, 1)
                gate_y(1)
                dve.wait_ge(stage_used, b * STAGED + (4 * (S_Z + 2) + 4))
                for j in range(2):
                    for t in range(NT):
                        rms_stats(j * NT + t, [y_sb[:, t, j * W:(j + 1) * W]])
                rms_rstd(8)
                for t in range(NT):
                    for j in range(2):
                        yy = y_sb[:, t, j * W:(j + 1) * W]
                        last = V.tensor_scalar(yy, yy, rstd[:, j * NT + t:j * NT + t + 1], None, ALU.mult)
                    last.then_inc(y_ok, 1)
                for k in range(KD):
                    dve.wait_ge(y_hi_ok, b * KD + (k + 1))
                    V.scalar_tensor_tensor(out=yT_lo[:, k, :], in0=aux[k % 4], scalar=col_a[:, R_SN + k:R_SN + k + 1],
                                           in1=yT_hi[:, k, :].bitcast(F32), op0=ALU.mult, op1=ALU.subtract
                                           ).then_inc(y_lo_ok, 1)

                def add_half(t, c):
                    V.tensor_tensor(x2[:, t, c], x2[:, t, c], stage[:, t, HALO:], ALU.add).then_inc(stage_used, 1)

                def residual_stats(G, S, end):
                    for t in range(NT):
                        full(G, t)
                        link(V.tensor_tensor(stage[:, t, HALO:], stage[:, t, HALO:], g_bc[:, 0:W], ALU.mult))
                        add_half(t, slice(0, W))
                    dve.wait_ge(stage_used, b * STAGED + (4 * (S + 1) + 4))
                    for t in range(NT):
                        V.bn_stats(stats2[:, t, 0, :], x2[:, t, 0:W])
                    for t in range(NT):
                        if t < 3:
                            dve.wait_ge(bank_done, b * (3 * GROUPS) + (3 * (G + 1) + t + 1))
                        else:
                            dve.wait_ge(w_used, b * UNITS + (end + RING))
                        V.tensor_tensor(stage[:, t, HALO:], main[t][:], g_bc[:, W:D], ALU.mult).then_inc(evacuated, 1)
                        full(G + 1, t)
                        add_half(t, slice(W, D))
                        dve.wait_ge(stage_used, b * STAGED + (4 * (S + 1) + t + 5))
                        link(V.bn_stats(stats2[:, t, 1, :], x2[:, t, W:D]))
                        link(V.bn_aggr(mv[:, t, :], stats2[:, t, :, :]))

                dve.wait_ge(x2_in, b * 32 + 32)
                residual_stats(G_OUT, S_OUT, UP)
                rms_rstd(NT, rstd_ok)
                dve.wait_ge(rstd_ok, b + 1)
                for c in (slice(0, W), slice(W, D)):
                    for t in range(NT - 1):
                        last = V.tensor_scalar(xn2[:, t, c], x2[:, t, c], rstd[:, t:t + 1], None, ALU.mult)
                    last.then_inc(xn_ok, 1)
                h_lows(b * 2 + 1, range(KD), C_SC2, C_SH2)

                with dve.Fori(0, KF // 2) as j:
                    fresh()
                    for i in range(2):
                        m = j * 2 + i
                        dve.wait_ge(evacuated, b * (4 * GROUPS) + j * 4 + (4 * G_UP + i + 5))
                        conv(b * CONVS + j * 2 + (KX + i + 1), i, 3, halo_f[:, bass.ds(m, 1), :].squeeze(1),
                             lambda tap: col_b[:, bass.ds(m + (R_FW + tap * KF), 1)],
                             col_b[:, bass.ds(m + R_FB, 1)], i)
                        V.tensor_copy(halo_f[:, bass.ds(m, 1), :].squeeze(1), stage[:, i, W + 1:]).then_inc(stage_used, 1)
                    for i in range(2):
                        m = j * 2 + i
                        dve.wait_ge(evacuated, b * (4 * GROUPS) + j * 4 + (4 * G_UP + i + 7))
                        dve.wait_ge(silu_done, b * CONVS + j * 2 + (KX + i + 3))
                        val = stage[:, 2 + i, HALO:]
                        link(V.tensor_tensor(val, val, acc[:, i, :], ALU.mult))
                        link(V.tensor_copy(g_hi[:, bass.ds(m, 1), :].squeeze(1), val))
                        V.tensor_tensor(g_lo[:, bass.ds(m, 1), :].squeeze(1), val,
                                        g_hi[:, bass.ds(m, 1), :].squeeze(1).bitcast(F32), ALU.subtract
                                        ).then_inc(stage_used, 1)
                fresh()
                norm_x(b + 1)
                h_lows(b * 2 + 2, range(KD), C_SC1, C_SH1)
                dve.wait_ge(g2_in, b * 32 + 32)
                residual_stats(G_DOWN, S_DOWN, UNITS)
                rms_rstd(NT)
                for t in range(NT):
                    V.scalar_tensor_tensor(out=x2[:, t, :], in0=x2[:, t, :], scalar=rstd[:, t:t + 1], in1=fg_bc[:],
                                           op0=ALU.mult, op1=ALU.mult).then_inc(out_ok, 1)

        @block.tensor
        def _(pe):
            T = nc.tensor
            pe.wait_ge(const_ok, 4)
            pe.wait_ge(c_in, 16)
            T.transpose(aux[1][:, 0:KD], c_rows[:], ident[0:KD, 0:KD]).then_inc(c_tr, 1)
            pe.wait_ge(rows_in, 176)
            T.transpose(aux[0][:, 0:ROWS_A], rows_a[0:ROWS_A, :], ident[0:ROWS_A, 0:ROWS_A]).then_inc(col_tr, 1)
            T.transpose(aux[0][:, P:P + ROWS_B], rows_b[0:ROWS_B, :], ident[0:ROWS_B, 0:ROWS_B]).then_inc(col_tr, 1)
            pe.wait_ge(small_in, 80)
            for h in range(GH):
                last = T.transpose(aux[2 + h // 4][:, (h % 4) * P:(h % 4 + 1) * P], ws_raw[:, h, :], ident[:])
                if h % 4 == 3:
                    last.then_inc(ws_tr, 1)
            def h_transpose(q, ks, tiles):
                for k in ks:
                    if k >= 4:
                        pe.wait_ge(h_lo_ok, q * KD + (k - 3))
                    for t in range(NT):
                        last = T.transpose(aux[k % 4][:, t * P:(t + 1) * P], tiles[t][:, k * P:(k + 1) * P], ident[:])
                    last.then_inc(h_tr, 1)

            xn = [xn01[:, 0, :], xn01[:, 1, :], xn23[:, 0, :], xn23[:, 1, :]]
            ones = tri[:, P - 1:P]

            def mod_column(n):
                for m in range(2 * KD):
                    last = T.matmul(aux[0][:, m:m + 1], mod_sum[:, 2 * n + m // KD, (m % KD) * P:(m % KD + 1) * P], ones,
                                    start=True, stop=True)
                last.then_inc(mod_col, 1)

            pe.sem_inc(w_used, RING)
            pe.wait_ge(cact_ok, 1)
            pe.wait_ge(col_ok, 2)
            pe.wait_ge(ada_summed, KD)
            mod_column(0)
            pe.wait_ge(ready, 1)
            pe.wait_ge(ws_ok, 2)
            pe.wait_ge(xn_ok, NT)
            h_transpose(0, range(KD), xn)
            for k in range(KD):
                i = 2 * KD + k
                pe.wait_ge(ada_in[i % ADA_RING], 16 * (i // ADA_RING + 1))
                for m in range(2):
                    last = T.matmul(main[m][0:1, :], c_act[:, k:k + 1], ada_t[:, i % ADA_RING, m * W:(m + 1) * W],
                                    start=k == 0, stop=k == KD - 1)
                    if k == KD - 1:
                        last.then_inc(gate_mm, 1)
                if k == 3:
                    pe.wait_ge(h_lo_ok, KD)
                    pe.wait_ge(ada_summed, 2 * KD)
                    mod_column(1)
            pe.wait_ge(ada_summed, 3 * KD)
            for m in range(2):
                T.matmul(main[2 + m][0:1, :], ones, mod_sum[:, 0, m * W:(m + 1) * W], start=True, stop=True
                         ).then_inc(gate_mm, 1)

            def unit(n_at, n, G_at, first, last, mms):
                pe.wait_ge(w_lo_ok, n_at)
                for i in range(4):
                    if first:
                        pe.wait_ge(evacuated, G_at + (i + 1))
                    for p, (a, w) in enumerate(mms(i)):
                        ins = T.matmul(main[i][:], a, w, start=first and p == 0, stop=last and p == 2)
                    if last and i < 3:
                        ins.then_inc(bank_done, 1)
                ins.then_inc(w_used, 1)

            def tokens_out(hi, lo, k, s):
                return lambda i: ((hi[:, k, i * P:(i + 1) * P], w_hi[:, s, :]), (hi[:, k, i * P:(i + 1) * P], w_lo[:, s, :]),
                                  (lo[:, k, i * P:(i + 1) * P], w_hi[:, s, :]))

            def channels_out(k, s):
                return lambda i: ((w_hi[:, s, i * P:(i + 1) * P], h_hi[:, k, :]), (w_hi[:, s, i * P:(i + 1) * P], h_lo[:, k, :]),
                                  (w_lo[:, s, i * P:(i + 1) * P], h_hi[:, k, :]))

            with pe.Fori(0, NB) as b:
                def run(n, G, k, K, mms):
                    unit(b * UNITS + (n + 1 + RING), n, b * (4 * GROUPS) + 4 * G, k == 0, k == K - 1, mms)

                def bank_by_bank(n0, K, ops):
                    for i in range(4):
                        for k in range(K - RING, K):
                            if i == 0:
                                pe.wait_ge(w_lo_ok, b * UNITS + (n0 + k + 1 + RING))
                            for p, (a, w) in enumerate(ops(k)(i)):
                                ins = T.matmul(main[i][:], a, w, start=False, stop=k == K - 1 and p == 2)
                            if i == 3:
                                ins.then_inc(w_used, 1)
                            elif k == K - 1:
                                ins.then_inc(bank_done, 1)

                for j in range(3):
                    for k in range(KD):
                        run(j * KD + k, j, k, KD, channels_out(k, k % RING))
                        if j == 0 and k == 1:
                            for kk in range(KD):
                                for p, a in enumerate((h_hi, h_lo)):
                                    last = T.matmul(aux[3], wdt[:, 2 * kk * NH:2 * kk * NH + P], a[:, kk, :],
                                                    start=kk == 0 and p == 0, stop=kk == KD - 1 and p == 1)
                            last.then_inc(dt_mm, 1)
                        if j == 0 and k == 5:
                            pe.wait_ge(dtT_ok, b + 1)
                            pe.sem_inc(pe_past, 1)
                            for t in range(NT):
                                last = T.transpose(aux[3][:, 2 * t * NH:2 * (t + 1) * NH], dtT[:, t * P:(t + 1) * P],
                                                   ident[0:2 * NH, 0:2 * NH])
                            last.then_inc(dt_tr, 1)
                        if j == 1 and k == 1:
                            pe.wait_ge(da_ok, b + 1)
                            for t in range(NT):
                                last = T.transpose(aux[3][0:NH, t * P:(t + 1) * P], da_t[:, t, :], ident[:])
                            last.then_inc(da_tr, 1)
                        if j == 1 and k == 6:
                            pe.wait_ge(acs_ok, b + 1)
                            pe.sem_inc(pe_past, 1)
                            for t in range(NT):
                                last = T.transpose(aux[3][:, t * NH:(t + 1) * NH], acsT[:, t * P:(t + 1) * P],
                                                   ident[0:NH, 0:NH])
                            last.then_inc(acs_tr, 1)

                def chunk_scores(cc):
                    ts = slice(cc * P, (cc + 1) * P)
                    if cc == 0:
                        pe.wait_ge(silu_done, b * CONVS + (KX + 2))
                    else:
                        pe.wait_ge(state_ok, b * NT + cc)
                        pe.wait_ge(yd_used, b * NT + cc)
                    for k in range(KD):
                        T.transpose(aux[k // 4][:, (k % 4) * P:(k % 4 + 1) * P], xT[:, k, ts], ident[:])
                    for g in range(2):
                        T.transpose(aux[2][:, g * P:(g + 1) * P], bcT[:, g, ts], ident[:])
                    for g in range(2):
                        last = T.matmul(aux[2][:, (2 + g) * P:(3 + g) * P], bcT[:, g, ts], bcT[:, 2 + g, ts],
                                        start=True, stop=True)
                    last.then_inc(t_done, 1)

                def chunk_yoff(cc):
                    pe.wait_ge(xs_ok, b * (3 * NT) + 3 * (cc + 1))
                    pe.wait_ge(cbm_ok, b * NT + (cc + 1))
                    pe.wait_ge(acs_t_ok, b + 1)
                    if cc:
                        pe.wait_ge(state_ok, b * NT + cc)
                    for g in range(2):
                        last = T.matmul(aux[2 + g], bcT[:, 2 + g, cc * P:(cc + 1) * P], state[:, g * W:(g + 1) * W],
                                        start=True, stop=True)
                    last.then_inc(yoff_done, 1)

                def chunk_state(cc):
                    pe.wait_ge(xdec_ok, b * NT + (cc + 1))
                    for g in range(2):
                        last = T.matmul(aux[g], b_tok[:, g, :], xdec[:, g * W:(g + 1) * W], start=True, stop=True)
                    last.then_inc(s_done, 1)

                def chunk_ydiag(cc):
                    pe.wait_ge(att_ok, b * NT + (cc + 1))
                    pe.wait_ge(yoff_used, b * NT + (cc + 1))
                    for h in range(NH):
                        o = (h % (NH // 2)) * HD
                        last = T.matmul(aux[2 + h // (NH // 2)][:, o:o + HD], arow[:, h, :], xdt[:, h * HD:(h + 1) * HD],
                                        start=True, stop=True)
                    last.then_inc(yd_done, 1)

                for cc in range(NT):
                    for k in range(KD):
                        run(UV + cc * KD + k, G_UV + cc, k, KD, tokens_out(h_hi, h_lo, k, k % RING))
                        if k == 1 and cc:
                            chunk_ydiag(cc - 1)
                        if k == (4 if cc == 0 else 3):
                            chunk_scores(cc)
                        if k == 5:
                            chunk_yoff(cc)
                        if k == 7:
                            chunk_state(cc)

                def spatial(t):
                    pe.wait_ge(v_ok, b * NT + (t + 1))
                    if t < 2:
                        pe.wait_ge(state_ok, b * NT + NT)
                        pe.wait_ge(yd_used, b * NT + NT)
                    else:
                        pe.wait_ge(sv_used, b * NT + (t - 1))
                    for h in range(GH):
                        last = T.matmul(aux[2 * (t % 2) + h // 4][:, (h % 4) * P:(h % 4 + 1) * P], wsT[:, h, :],
                                        v_sb[:, h // 4, t, (h % 4) * P:(h % 4 + 1) * P], start=True, stop=True)
                    last.then_inc(sv_done, 1)

                def gm_transpose(ks):
                    for k in ks:
                        if k == 0:
                            pe.wait_ge(gm_ok, b * NT + NT)
                        if k >= 4:
                            pe.wait_ge(gm_lo_ok, b * KD + (k - 3))
                        for t in range(NT):
                            last = T.transpose(aux[k % 4][:, t * P:(t + 1) * P],
                                               u_sb[:, k // 4, t, (k % 4) * P:(k % 4 + 1) * P], ident[:])
                        last.then_inc(gm_tr, 1)

                def y_transpose(ks):
                    for k in ks:
                        if k == 0:
                            pe.wait_ge(y_ok, b * NT + NT)
                        if k >= 4:
                            pe.wait_ge(y_lo_ok, b * KD + (k - 3))
                        for t in range(NT):
                            last = T.transpose(aux[k % 4][:, t * P:(t + 1) * P], y_sb[:, t, k * P:(k + 1) * P], ident[:])
                        last.then_inc(y_tr, 1)

                for j in range(2):
                    for k in range(KD):
                        run(Z + j * KD + k, G_Z + j, k, KD, tokens_out(h_hi, h_lo, k, k % RING))
                        if j == 0 and k == 1:
                            chunk_ydiag(NT - 1)
                        if j == 0 and k == 5:
                            spatial(0)
                            spatial(1)
                        if j == 0 and k == 7:
                            spatial(2)
                        if j == 1 and k == 1:
                            spatial(3)
                        if j == 1 and k == 5:
                            gm_transpose(range(4))
                        if j == 1 and k == 6:
                            gm_transpose(range(4, KD))
                def out_ops(k):
                    ops = (gmT_hi, gmT_lo) if k < KD else (yT_hi, yT_lo)
                    return tokens_out(*ops, k % KD, k % RING)

                for j in range(2):
                    for k in range(2 * KD - (RING if j else 0)):
                        if j == 0 and k < KD:
                            pe.wait_ge(gm_lo_ok, b * KD + (k + 1))
                        if j == 0 and k >= KD:
                            pe.wait_ge(y_lo_ok, b * KD + (k - KD + 1))
                        run(OUT + j * 2 * KD + k, G_OUT + j, k, 2 * KD, out_ops(k))
                        if j == 0 and k == 6:
                            y_transpose(range(4))
                        if j == 0 and k == 7:
                            y_transpose(range(4, KD))
                bank_by_bank(OUT + 2 * KD, 2 * KD, out_ops)
                for i in range(WARM):
                    T.matmul(aux[3], h_hi[:, 0, 0:P], h_hi[:, 0, :], start=True, stop=True)
                pe.wait_ge(xn_ok, b * (NT + 2) + (NT + 1))
                pe.wait_ge(xn_act_ok, b * 2 + 1)
                xn2_tiles = [xn2[:, t, :] for t in range(NT)]
                h_transpose(b * 2 + 1, range(4), xn2_tiles)
                for k in range(KD):
                    if k == 0:
                        pe.wait_ge(w_lo_ok, b * UNITS + (UP + 1 + RING))
                        pe.wait_ge(h_hi_ok, b * (2 * KD) + (KD + 1))
                        parts = [channels_out(0, UP % RING)(i) for i in range(4)]
                        for i in range(4):
                            pe.wait_ge(evacuated, b * (4 * GROUPS) + (4 * G_UP + i + 1))
                            for p in (0, 2):
                                T.matmul(main[i][:], parts[i][p][0], parts[i][p][1], start=p == 0, stop=False)
                        pe.wait_ge(h_lo_ok, b * (2 * KD) + (KD + 1))
                        for i in range(4):
                            ins = T.matmul(main[i][:], parts[i][1][0], parts[i][1][1], start=False, stop=False)
                        ins.then_inc(w_used, 1)
                    else:
                        pe.wait_ge(h_lo_ok, b * (2 * KD) + (KD + k + 1))
                        run(UP + k, G_UP, k, KD, channels_out(k, k % RING))
                    if k < 2:
                        if k == 0:
                            pe.wait_ge(xn_ok, b * (NT + 2) + (NT + 2))
                            pe.wait_ge(xn_act_ok, b * 2 + 2)
                        h_transpose(b * 2 + 1, (4 + 2 * k, 5 + 2 * k), xn2_tiles)
                with pe.Fori(1, KF // 2) as j:
                    for k in range(KD):
                        unit(b * UNITS + j * KD + (UP + k + 1 + RING), UP + k, b * (4 * GROUPS) + j * 4 + 4 * G_UP,
                             k == 0, k == KD - 1, channels_out(k, k % RING))
                def down_ops(j):
                    return lambda k: tokens_out(g_hi, g_lo, k, (j * KF + k) % RING)

                for j in range(2):
                    for k in range(KF - (RING if j else 0)):
                        if j == 0:
                            if k == 0:
                                pe.wait_ge(stage_used, b * STAGED + (4 * S_DOWN))
                            if k >= KF - 2:
                                pe.wait_ge(stage_used, b * STAGED + (4 * S_DOWN + 4 - (KF - 1 - k)))
                        run(DOWN + j * KF + k, G_DOWN + j, k, KF, down_ops(j)(k))
                        if j == 0 and k == 15:
                            pe.wait_ge(xn_ok, b * (NT + 2) + (NT + 2 + NT))
                            h_transpose(b * 2 + 2, range(4), xn)
                        if j == 0 and k == 18:
                            h_transpose(b * 2 + 2, range(4, KD), xn)
                bank_by_bank(DOWN + KF, KF, down_ops(1))
                pe.wait_ge(h_lo_ok, b * (2 * KD) + 3 * KD)


_INS = ['x', 'c', 'ada_w', 'ada_b', 'norm1_g', 'norm2_g', 'w_in', 'ssd_conv_w', 'ssd_conv_b', 'ssd_dt_bias',
        'ssd_a_log', 'ssd_d', 'ssd_norm_g', 'gm_vnorm_g', 'gm_ws', 'gm_bs', 'gm_out_g', 'w_out', 'ff_up',
        'ff_conv_w', 'ff_conv_b', 'ff_down', 'final_g']


def kernel(**inputs):
    import numpy as _np
    import concourse.bacc as _bacc
    from concourse import mybir as _mybir
    from concourse.bass_utils import run_bass_kernel_spmd as _run

    nc = _bacc.Bacc("TRN2", target_bir_lowering=False, num_devices=1)
    arrays, args = {}, []
    for name in _INS:
        a = _np.ascontiguousarray(inputs[name])
        arrays[f"in_{name}_dram"] = a
        args.append(nc.dram_tensor(f"in_{name}_dram", a.shape, _mybir.dt.from_np(a.dtype), kind="ExternalInput").ap())
    out = nc.dram_tensor("out_dram", inputs["x"].shape, _mybir.dt.float32, kind="ExternalOutput").ap()
    hybrid_decoder_trunk(nc, *args, out)
    r = _run(nc, [arrays], core_ids=[0])
    return r.results[0]["out_dram"]
```
